# Optimizing a Trainium2 kernel written in Bass

```python
import math
import jax, jax.numpy as jnp
from jax import lax
import numpy as np
import jax
import jax.numpy as jnp

D_MODEL = 1024
BATCH = 1
SEQ = 512
DEPTH = 2

POOL_WIDTH = D_MODEL // 4
FOURIER_WIDTH = D_MODEL // 4
ATTN_WIDTH = D_MODEL // 2
POOL_WINDOWS = (2, 4, 8, 16)
N_POOL_GROUPS = len(POOL_WINDOWS)
POOL_GROUP_DIM = POOL_WIDTH // N_POOL_GROUPS
N_FOURIER_GROUPS = 4
FOURIER_GROUP_DIM = FOURIER_WIDTH // N_FOURIER_GROUPS
ATTN_HEADS = 4
ATTN_HEAD_DIM = ATTN_WIDTH // (2 * ATTN_HEADS)
ATTN_V_DIM = 2 * ATTN_HEAD_DIM
Q_BLOCK = 128
D_FF = 2816
IN_COLS = POOL_WIDTH + FOURIER_WIDTH + 3 * ATTN_WIDTH
NORM_EPS = 1e-6


def alibi_slopes(n_heads):
    return jnp.array([2.0 ** (-8.0 * (i + 1) / n_heads) for i in range(n_heads)], dtype=jnp.float32)

def lambda_init_fn(layer_idx):
    return 0.8 - 0.6 * math.exp(-0.3 * layer_idx)

def rmsnorm(x, g):
    xf = x.astype(jnp.float32)
    y = xf * lax.rsqrt(jnp.mean(xf * xf, axis=-1, keepdims=True) + NORM_EPS)
    return (y * g.astype(jnp.float32)).astype(x.dtype)

def swiglu(x, w_gate, w_up, w_down):
    return (jax.nn.silu(x @ w_gate) * (x @ w_up)) @ w_down

def pool_mixer(a, pool_w, pool_scale):
    B, S, _ = a.shape
    af = a.reshape(B, S, N_POOL_GROUPS, POOL_GROUP_DIM).astype(jnp.float32)
    prefix = jnp.concatenate(
        [jnp.zeros((B, 1, N_POOL_GROUPS, POOL_GROUP_DIM), jnp.float32), jnp.cumsum(af, axis=1)], axis=1)
    t = jnp.arange(S)
    outs = []
    for g, w in enumerate(POOL_WINDOWS):
        left = w // 2
        right = w - 1 - left
        hi = jnp.minimum(t + right + 1, S)
        lo = jnp.maximum(t - left, 0)
        pg = prefix[:, :, g]
        win_sum = jnp.take(pg, hi, axis=1) - jnp.take(pg, lo, axis=1)
        cnt = (hi - lo).astype(jnp.float32)[None, :, None]
        outs.append(win_sum / cnt - af[:, :, g])
    m = jnp.stack(outs, axis=2).astype(a.dtype)
    y = jnp.einsum('bsgc,gcd->bsgd', m, pool_w).reshape(B, S, POOL_WIDTH)
    return y * pool_scale

def fourier_mixer(f, fourier_w):
    B, S, _ = f.shape
    f4 = f.reshape(B, S, N_FOURIER_GROUPS, FOURIER_GROUP_DIM).astype(jnp.float32)
    y = jnp.real(jnp.fft.fft2(f4, axes=(1, 3), norm='ortho'))
    y = y.astype(f.dtype).reshape(B, S, FOURIER_WIDTH)
    return y @ fourier_w

def diff_attention(q, k, v, lam, lam_init, head_norm):
    B, S = q.shape[0], q.shape[1]
    n_blk = S // Q_BLOCK
    scale = ATTN_HEAD_DIM ** -0.5
    slopes = alibi_slopes(ATTN_HEADS)
    kpos = jnp.arange(S, dtype=jnp.float32)
    qb = q.reshape(B, n_blk, Q_BLOCK, ATTN_HEADS, 2, ATTN_HEAD_DIM).transpose(1, 0, 2, 3, 4, 5)

    def one_block(args):
        q_blk, i = args
        qpos = (i * Q_BLOCK + jnp.arange(Q_BLOCK)).astype(jnp.float32)
        bias = -slopes[:, None, None] * jnp.abs(qpos[:, None] - kpos[None, :])
        s = jnp.einsum('bqhjd,bkhjd->bhjqk', q_blk, k).astype(jnp.float32) * scale + bias[None, :, None]
        p = jax.nn.softmax(s, axis=-1)
        attn = p[:, :, 0] - lam.astype(jnp.float32) * p[:, :, 1]
        return jnp.einsum('bhqk,bkhe->bqhe', attn.astype(v.dtype), v)

    o = lax.map(one_block, (qb, jnp.arange(n_blk)))
    o = o.transpose(1, 0, 2, 3, 4).reshape(B, S, ATTN_HEADS, ATTN_V_DIM)
    o = rmsnorm(o, head_norm.reshape(ATTN_HEADS, ATTN_V_DIM)) * (1.0 - lam_init)
    return o.reshape(B, S, ATTN_WIDTH)

def first_inputs(seed: int = 0) -> dict:
    key = jax.random.key(seed)
    ks = jax.random.split(key, 24)
    f32 = jnp.float32

    def nrm(k, shape, fan_in):
        return jax.random.normal(k, shape, f32) * (fan_in ** -0.5)

    def gain(k, shape):
        return 1.0 + 0.05 * jax.random.normal(k, shape, f32)

    return {
        "x": jax.random.normal(ks[0], (BATCH, SEQ, D_MODEL), f32),
        "ffn1_norm": gain(ks[1], (DEPTH, D_MODEL)),
        "ffn1_w_gate": nrm(ks[2], (DEPTH, D_MODEL, D_FF), D_MODEL),
        "ffn1_w_up": nrm(ks[3], (DEPTH, D_MODEL, D_FF), D_MODEL),
        "ffn1_w_down": nrm(ks[4], (DEPTH, D_FF, D_MODEL), D_FF),
        "mix_norm": gain(ks[5], (DEPTH, D_MODEL)),
        "w_in": nrm(ks[6], (DEPTH, D_MODEL, IN_COLS), D_MODEL),
        "pool_w": nrm(ks[7], (DEPTH, N_POOL_GROUPS, POOL_GROUP_DIM, POOL_GROUP_DIM), POOL_GROUP_DIM),
        "pool_scale": gain(ks[8], (DEPTH, POOL_WIDTH)),
        "fourier_w": nrm(ks[9], (DEPTH, FOURIER_WIDTH, FOURIER_WIDTH), FOURIER_WIDTH),
        "lam_q1": 0.1 * jax.random.normal(ks[10], (DEPTH, ATTN_HEAD_DIM), f32),
        "lam_k1": 0.1 * jax.random.normal(ks[11], (DEPTH, ATTN_HEAD_DIM), f32),
        "lam_q2": 0.1 * jax.random.normal(ks[12], (DEPTH, ATTN_HEAD_DIM), f32),
        "lam_k2": 0.1 * jax.random.normal(ks[13], (DEPTH, ATTN_HEAD_DIM), f32),
        "attn_head_norm": gain(ks[14], (DEPTH, ATTN_WIDTH)),
        "w_out": nrm(ks[15], (DEPTH, D_MODEL, D_MODEL), D_MODEL),
        "ffn2_norm": gain(ks[16], (DEPTH, D_MODEL)),
        "ffn2_w_gate": nrm(ks[17], (DEPTH, D_MODEL, D_FF), D_MODEL),
        "ffn2_w_up": nrm(ks[18], (DEPTH, D_MODEL, D_FF), D_MODEL),
        "ffn2_w_down": nrm(ks[19], (DEPTH, D_FF, D_MODEL), D_FF),
        "final_norm": gain(ks[20], (D_MODEL,)),
    }

def first_block(x, ffn1_norm, ffn1_w_gate, ffn1_w_up, ffn1_w_down, mix_norm, w_in, pool_w, pool_scale,
              fourier_w, lam_q1, lam_k1, lam_q2, lam_k2, attn_head_norm, w_out,
              ffn2_norm, ffn2_w_gate, ffn2_w_up, ffn2_w_down, final_norm):
    B, S, _ = x.shape
    c0 = POOL_WIDTH
    c1 = c0 + FOURIER_WIDTH
    c2 = c1 + ATTN_WIDTH
    c3 = c2 + ATTN_WIDTH
    for l in range(DEPTH):
        h = rmsnorm(x, ffn1_norm[l])
        x = x + 0.5 * swiglu(h, ffn1_w_gate[l], ffn1_w_up[l], ffn1_w_down[l])

        h = rmsnorm(x, mix_norm[l])
        p = h @ w_in[l]
        a = p[..., :c0]
        f = p[..., c0:c1]
        q = p[..., c1:c2].reshape(B, S, ATTN_HEADS, 2, ATTN_HEAD_DIM)
        k = p[..., c2:c3].reshape(B, S, ATTN_HEADS, 2, ATTN_HEAD_DIM)
        v = p[..., c3:].reshape(B, S, ATTN_HEADS, ATTN_V_DIM)

        lam_init = lambda_init_fn(l)
        lam = (jnp.exp(jnp.sum(lam_q1[l].astype(jnp.float32) * lam_k1[l].astype(jnp.float32)))
               - jnp.exp(jnp.sum(lam_q2[l].astype(jnp.float32) * lam_k2[l].astype(jnp.float32)))
               + lam_init)

        y_pool = pool_mixer(a, pool_w[l], pool_scale[l])
        y_four = fourier_mixer(f, fourier_w[l])
        y_attn = diff_attention(q, k, v, lam, lam_init, attn_head_norm[l]).astype(x.dtype)
        y = jnp.concatenate([y_pool, y_four, y_attn], axis=-1) @ w_out[l]
        x = x + y

        h = rmsnorm(x, ffn2_norm[l])
        x = x + 0.5 * swiglu(h, ffn2_w_gate[l], ffn2_w_up[l], ffn2_w_down[l])
    return rmsnorm(x, final_norm)


N_MIXERS = 2
N_NSA_LAYERS = (DEPTH + 1) // 2
N_HGRN_LAYERS = DEPTH // 2

NSA_HEADS = 16
NSA_KV_GROUPS = 4
NSA_GROUP_SIZE = NSA_HEADS // NSA_KV_GROUPS
NSA_HEAD_DIM = D_MODEL // NSA_HEADS
NSA_Q_DIM = NSA_HEADS * NSA_HEAD_DIM
NSA_KV_DIM = NSA_KV_GROUPS * NSA_HEAD_DIM
NSA_IN_DIM = NSA_Q_DIM + 6 * NSA_KV_DIM + 3 * NSA_HEADS
CMP_BLOCK = 32
CMP_STRIDE = 16
SEL_BLOCK = 64
N_SELECT = 8
WINDOW = 512
Q_BLOCK_2 = 32
FORCED_SCORE = 1.0e4

REL_BUCKETS = 32
REL_MAX_DISTANCE = 1024

HGRN_EXPAND = 128
HGRN_HEADS = D_MODEL // HGRN_EXPAND
HGRN_KEY_DIM = HGRN_EXPAND
HGRN_VALUE_DIM = D_MODEL // HGRN_HEADS
HGRN_F_DIM = HGRN_HEADS * HGRN_KEY_DIM
HGRN_IN_DIM = 2 * HGRN_F_DIM + 2 * D_MODEL
HGRN_CHUNK = 32

MOE_GROUPS = 4
MOE_EXPERTS_PER_GROUP = 4
MOE_EXPERTS = MOE_GROUPS * MOE_EXPERTS_PER_GROUP
MOE_TOP_K = 2
MOE_FF = 512
MOE_ROW_BLOCK = 128


def rms_norm(x, gain):
    xf = x.astype(jnp.float32)
    y = xf * lax.rsqrt(jnp.mean(xf * xf, axis=-1, keepdims=True) + NORM_EPS)
    return (y * gain.astype(jnp.float32)).astype(x.dtype)

def masked_softmax(logits, mask):
    logits = jnp.where(mask, logits, -jnp.inf)
    m = jnp.max(logits, axis=-1, keepdims=True)
    m = jnp.where(jnp.isfinite(m), m, 0.0)
    e = jnp.exp(logits - m)
    return e / jnp.maximum(jnp.sum(e, axis=-1, keepdims=True), 1e-30)

def t5_bucket(dist):
    n = jnp.maximum(dist, 0)
    max_exact = REL_BUCKETS // 2
    nf = jnp.maximum(n, 1).astype(jnp.float32)
    large = max_exact + (jnp.log(nf / max_exact) / math.log(REL_MAX_DISTANCE / max_exact)
                         * (REL_BUCKETS - max_exact)).astype(jnp.int32)
    large = jnp.minimum(large, REL_BUCKETS - 1)
    return jnp.where(n < max_exact, n, large)

def compress_blocks(kv, pe, w1, w2):
    b, t, g, d = kv.shape
    n_cmp = (t - CMP_BLOCK) // CMP_STRIDE + 1
    idx = np.arange(n_cmp)[:, None] * CMP_STRIDE + np.arange(CMP_BLOCK)[None, :]
    blocks = kv[:, idx] + pe[None, None, :, None, :]
    flat = blocks.transpose(0, 1, 3, 2, 4).reshape(b, n_cmp, g, CMP_BLOCK * d)
    return jax.nn.silu(flat @ w1) @ w2

def cmp_to_sel_weights(n_cmp, n_sel):
    cs = np.arange(n_cmp) * CMP_STRIDE
    ss = np.arange(n_sel) * SEL_BLOCK
    shared = (np.minimum(cs[:, None] + CMP_BLOCK, ss[None, :] + SEL_BLOCK)
              - np.maximum(cs[:, None], ss[None, :]))
    return jnp.asarray(np.clip(shared, 0, None) / CMP_BLOCK, dtype=jnp.float32)

def nsa_mixer(h, rel_bias, w_in, q_gain, k_gain, cmp_pe, cmp_w1, cmp_w2, w_out):
    b, t, _ = h.shape
    G, R, Dh = NSA_KV_GROUPS, NSA_GROUP_SIZE, NSA_HEAD_DIM
    cuts = [NSA_Q_DIM + i * NSA_KV_DIM for i in range(7)]
    q, kc, vc, ks, vs, kw, vw, gl = jnp.split(h @ w_in, cuts, axis=-1)
    kvs = (b, t, G, Dh)
    q = rms_norm(q.reshape(b, t, G, R, Dh), q_gain)
    kc = rms_norm(compress_blocks(kc.reshape(kvs), cmp_pe[0], cmp_w1[0], cmp_w2[0]), k_gain[0])
    vc = compress_blocks(vc.reshape(kvs), cmp_pe[1], cmp_w1[1], cmp_w2[1])
    ks = rms_norm(ks.reshape(kvs), k_gain[1])
    vs = vs.reshape(kvs)
    kw = rms_norm(kw.reshape(kvs), k_gain[2])
    vw = vw.reshape(kvs)
    gates = jax.nn.sigmoid(gl.astype(jnp.float32)).reshape(b, t, G, R, 3)

    n_cmp = kc.shape[1]
    n_sel_blocks = t // SEL_BLOCK
    n_select = min(N_SELECT, n_sel_blocks)
    n_keys_sel = n_select * SEL_BLOCK
    cmp_end = jnp.arange(n_cmp) * CMP_STRIDE + (CMP_BLOCK - 1)
    cmp_to_sel = cmp_to_sel_weights(n_cmp, n_sel_blocks)
    ks_blk = ks.transpose(0, 2, 1, 3).reshape(b, G, n_sel_blocks, SEL_BLOCK, Dh)
    vs_blk = vs.transpose(0, 2, 1, 3).reshape(b, G, n_sel_blocks, SEL_BLOCK, Dh)
    kw_pad = jnp.pad(kw, ((0, 0), (WINDOW, 0), (0, 0), (0, 0)))
    vw_pad = jnp.pad(vw, ((0, 0), (WINDOW, 0), (0, 0), (0, 0)))
    bias_tbl = rel_bias.astype(jnp.float32).T.reshape(G, R, REL_BUCKETS)
    scale = NSA_HEAD_DIM ** -0.5
    blk_ids = jnp.arange(n_sel_blocks)
    b_ix = jnp.arange(b)[:, None, None, None]
    g_ix = jnp.arange(G)[None, :, None, None]
    g_ix5 = jnp.arange(G)[None, :, None, None, None]
    r_ix5 = jnp.arange(R)[None, None, :, None, None]

    def query_block(qb):
        t0 = qb * Q_BLOCK_2
        tq = t0 + jnp.arange(Q_BLOCK_2)
        q_b = lax.dynamic_slice_in_dim(q, t0, Q_BLOCK_2, axis=1)
        gate_b = lax.dynamic_slice_in_dim(gates, t0, Q_BLOCK_2, axis=1)

        dist_c = tq[:, None] - cmp_end[None, :]
        lg = (jnp.einsum('bqgrd,bngd->bgrqn', q_b, kc).astype(jnp.float32) * scale
              + bias_tbl[:, :, t5_bucket(dist_c)])
        p_c = masked_softmax(lg, dist_c >= 0)
        o_c = jnp.einsum('bgrqn,bngd->bqgrd', p_c.astype(vc.dtype), vc)

        imp = jnp.einsum('bgrqn,ns->bgqs', p_c, cmp_to_sel)
        cur = tq // SEL_BLOCK
        forced = ((blk_ids[None, :] == 0) | (blk_ids[None, :] == cur[:, None])
                  | (blk_ids[None, :] == cur[:, None] - 1))
        causal_blk = blk_ids[None, :] <= cur[:, None]
        score = jnp.where(forced, FORCED_SCORE, jnp.where(causal_blk, imp, -1.0))
        _, sel = lax.top_k(score, n_select)
        k_sel = ks_blk[b_ix, g_ix, sel].reshape(b, G, Q_BLOCK_2, n_keys_sel, Dh)
        v_sel = vs_blk[b_ix, g_ix, sel].reshape(b, G, Q_BLOCK_2, n_keys_sel, Dh)
        pos = (sel[..., None] * SEL_BLOCK + jnp.arange(SEL_BLOCK)).reshape(b, G, Q_BLOCK_2, n_keys_sel)
        dist_s = tq[None, None, :, None] - pos
        lg = (jnp.einsum('bqgrd,bgqkd->bgrqk', q_b, k_sel).astype(jnp.float32) * scale
              + bias_tbl[g_ix5, r_ix5, t5_bucket(dist_s)[:, :, None]])
        p_s = masked_softmax(lg, (dist_s >= 0)[:, :, None])
        o_s = jnp.einsum('bgrqk,bgqkd->bqgrd', p_s.astype(v_sel.dtype), v_sel)

        k_w = lax.dynamic_slice_in_dim(kw_pad, t0, Q_BLOCK_2 + WINDOW, axis=1)
        v_w = lax.dynamic_slice_in_dim(vw_pad, t0, Q_BLOCK_2 + WINDOW, axis=1)
        kpos = t0 - WINDOW + jnp.arange(Q_BLOCK_2 + WINDOW)
        dist_w = tq[:, None] - kpos[None, :]
        mask_w = (dist_w >= 0) & (dist_w < WINDOW) & (kpos[None, :] >= 0)
        lg = (jnp.einsum('bqgrd,bkgd->bgrqk', q_b, k_w).astype(jnp.float32) * scale
              + bias_tbl[:, :, t5_bucket(dist_w)])
        p_w = masked_softmax(lg, mask_w)
        o_w = jnp.einsum('bgrqk,bkgd->bqgrd', p_w.astype(v_w.dtype), v_w)

        o = gate_b[..., 0:1] * o_c + gate_b[..., 1:2] * o_s + gate_b[..., 2:3] * o_w
        return o.astype(h.dtype).reshape(b, Q_BLOCK_2, NSA_Q_DIM)

    o = lax.map(query_block, jnp.arange(t // Q_BLOCK_2))
    o = o.transpose(1, 0, 2, 3).reshape(b, t, NSA_Q_DIM)
    return o @ w_out

def hgrn2_mixer(h, lower_bound, w_in, out_gain, w_out):
    b, t, _ = h.shape
    NH, dk, dv, C = HGRN_HEADS, HGRN_KEY_DIM, HGRN_VALUE_DIM, HGRN_CHUNK
    q, f, i, g = jnp.split(h @ w_in, [HGRN_F_DIM, 2 * HGRN_F_DIM, 2 * HGRN_F_DIM + D_MODEL], axis=-1)
    q = jax.nn.silu(q.astype(jnp.float32)).reshape(b, t, NH, dk)
    lb = lower_bound.astype(jnp.float32).reshape(NH, dk)
    log_f = jnp.logaddexp(jnp.log(lb), jnp.log1p(-lb)
                          + jax.nn.log_sigmoid(f.astype(jnp.float32).reshape(b, t, NH, dk)))
    k = -jnp.expm1(log_f)
    v = i.astype(jnp.float32).reshape(b, t, NH, dv)
    n_chunks = t // C

    def to_chunks(a):
        return a.reshape(b, n_chunks, C, NH, a.shape[-1]).transpose(1, 0, 3, 2, 4)

    causal = jnp.tril(jnp.ones((C, C), dtype=bool))

    def chunk_step(S, xs):
        q_c, k_c, v_c, lf_c = xs
        cum = jnp.cumsum(lf_c, axis=2)
        rel = jnp.where(causal[:, :, None], cum[:, :, :, None, :] - cum[:, :, None, :, :], -jnp.inf)
        attn = jnp.einsum('bhtd,bhsd,bhtsd->bhts', q_c, k_c, jnp.exp(rel))
        o = attn @ v_c + jnp.einsum('bhtd,bhde->bhte', q_c * jnp.exp(cum), S)
        last = cum[:, :, -1:, :]
        S = (jnp.exp(last[:, :, 0, :, None]) * S
             + jnp.einsum('bhsd,bhse->bhde', k_c * jnp.exp(last - cum), v_c))
        return S, o

    S0 = jnp.zeros((b, NH, dk, dv), jnp.float32)
    _, o = lax.scan(chunk_step, S0, (to_chunks(q), to_chunks(k), to_chunks(v), to_chunks(log_f)))
    o = o.transpose(1, 0, 3, 2, 4).reshape(b, t, NH, dv)
    o = rms_norm(o, out_gain) * jax.nn.silu(g.astype(jnp.float32).reshape(b, t, NH, dv))
    return o.reshape(b, t, D_MODEL).astype(h.dtype) @ w_out

def grouped_expert_ffn(tok, expert, weight, w1, w3, w2):
    n, d = tok.shape
    a = n * MOE_TOP_K
    flat_e = expert.reshape(a)
    flat_t = jnp.repeat(jnp.arange(n, dtype=jnp.int32), MOE_TOP_K)
    flat_w = weight.reshape(a)
    order = jnp.argsort(flat_e)
    e_sorted, t_sorted, w_sorted = flat_e[order], flat_t[order], flat_w[order]
    counts = jnp.bincount(flat_e, length=MOE_EXPERTS)
    padded = (counts + MOE_ROW_BLOCK - 1) // MOE_ROW_BLOCK * MOE_ROW_BLOCK
    pad_end = jnp.cumsum(padded)
    pad_start = pad_end - padded
    start = jnp.cumsum(counts) - counts
    dest = pad_start[e_sorted] + (jnp.arange(a) - start[e_sorted])
    n_blk = -(-(a + MOE_EXPERTS * (MOE_ROW_BLOCK - 1)) // MOE_ROW_BLOCK)
    p = n_blk * MOE_ROW_BLOCK
    buf_t = jnp.full((p,), n, dtype=jnp.int32).at[dest].set(t_sorted)
    buf_w = jnp.zeros((p,), tok.dtype).at[dest].set(w_sorted)
    blk_e = jnp.minimum(jnp.searchsorted(pad_end, jnp.arange(n_blk) * MOE_ROW_BLOCK, side='right'),
                        MOE_EXPERTS - 1)
    tok_pad = jnp.concatenate([tok, jnp.zeros((1, d), tok.dtype)], axis=0)
    xb = tok_pad[buf_t].reshape(n_blk, MOE_ROW_BLOCK, d)

    def expert_block(args):
        xblk, e = args
        return (jax.nn.silu(xblk @ w1[e]) * (xblk @ w3[e])) @ w2[e]

    yb = lax.map(expert_block, (xb, blk_e)).reshape(p, d)
    out = jnp.zeros((n + 1, d), tok.dtype).at[buf_t].add(yb * buf_w[:, None])
    return out[:n]

def hier_moe(h, w_router_group, w_router_expert, w1, w3, w2):
    b, t, d = h.shape
    n = b * t
    tok = h.reshape(n, d)
    p_group = jax.nn.softmax((tok @ w_router_group).astype(jnp.float32), axis=-1)
    grp = jnp.argmax(p_group, axis=-1).astype(jnp.int32)
    p_grp_sel = jnp.take_along_axis(p_group, grp[:, None], axis=-1)
    e_logits = (tok @ w_router_expert).astype(jnp.float32).reshape(n, MOE_GROUPS, MOE_EXPERTS_PER_GROUP)
    e_logits = jnp.take_along_axis(e_logits, grp[:, None, None], axis=1)[:, 0]
    top_p, top_i = lax.top_k(jax.nn.softmax(e_logits, axis=-1), MOE_TOP_K)
    weight = p_grp_sel * top_p / jnp.sum(top_p, axis=-1, keepdims=True)
    expert = grp[:, None] * MOE_EXPERTS_PER_GROUP + top_i.astype(jnp.int32)
    y = grouped_expert_ffn(tok, expert, weight.astype(h.dtype), w1, w3, w2)
    return y.reshape(b, t, d)

def second_inputs(seed: int = 0) -> dict:
    key = jax.random.key(seed)
    ks = jax.random.split(key, 24)
    f32 = jnp.float32
    D = D_MODEL

    def nrm(k, shape, s):
        return jax.random.normal(k, shape, f32) * s

    return {
        'x': nrm(ks[0], (BATCH, SEQ, D), 1.0),
        'c': nrm(ks[1], (BATCH, D), 1.0),
        'ada_w': nrm(ks[2], (DEPTH, 2, D, 3 * D), 0.5 * D ** -0.5),
        'ada_b': nrm(ks[3], (DEPTH, 2, 3 * D), 0.01),
        'norm_g': 1.0 + nrm(ks[4], (DEPTH, 2, D), 0.01),
        'rel_bias': nrm(ks[5], (REL_BUCKETS, NSA_HEADS), 0.5),
        'nsa_w_in': nrm(ks[6], (N_NSA_LAYERS, D, NSA_IN_DIM), D ** -0.5),
        'nsa_q_gain': 1.0 + nrm(ks[7], (N_NSA_LAYERS, NSA_HEAD_DIM), 0.01),
        'nsa_k_gain': 1.0 + nrm(ks[8], (N_NSA_LAYERS, 3, NSA_HEAD_DIM), 0.01),
        'nsa_cmp_pe': nrm(ks[9], (N_NSA_LAYERS, 2, CMP_BLOCK, NSA_HEAD_DIM), 0.02),
        'nsa_cmp_w1': nrm(ks[10], (N_NSA_LAYERS, 2, CMP_BLOCK * NSA_HEAD_DIM, NSA_HEAD_DIM),
                          (CMP_BLOCK * NSA_HEAD_DIM) ** -0.5),
        'nsa_cmp_w2': nrm(ks[11], (N_NSA_LAYERS, 2, NSA_HEAD_DIM, NSA_HEAD_DIM), NSA_HEAD_DIM ** -0.5),
        'nsa_w_out': nrm(ks[12], (N_NSA_LAYERS, NSA_Q_DIM, D), NSA_Q_DIM ** -0.5),
        'hgrn_w_in': nrm(ks[13], (N_HGRN_LAYERS, D, HGRN_IN_DIM), D ** -0.5),
        'hgrn_lower_bounds': 1.0 + nrm(ks[14], (DEPTH, HGRN_F_DIM), 0.1),
        'hgrn_out_gain': 1.0 + nrm(ks[15], (N_HGRN_LAYERS, HGRN_VALUE_DIM), 0.01),
        'hgrn_w_out': nrm(ks[16], (N_HGRN_LAYERS, D, D), D ** -0.5),
        'moe_router_group': nrm(ks[17], (DEPTH, D, MOE_GROUPS), D ** -0.5),
        'moe_router_expert': nrm(ks[18], (DEPTH, D, MOE_EXPERTS), D ** -0.5),
        'moe_w1': nrm(ks[19], (DEPTH, MOE_EXPERTS, D, MOE_FF), D ** -0.5),
        'moe_w3': nrm(ks[20], (DEPTH, MOE_EXPERTS, D, MOE_FF), D ** -0.5),
        'moe_w2': nrm(ks[21], (DEPTH, MOE_EXPERTS, MOE_FF, D), MOE_FF ** -0.5),
    }

def second_block(x, c, ada_w, ada_b, norm_g, rel_bias, nsa_w_in, nsa_q_gain, nsa_k_gain,
              nsa_cmp_pe, nsa_cmp_w1, nsa_cmp_w2, nsa_w_out, hgrn_w_in, hgrn_lower_bounds,
              hgrn_out_gain, hgrn_w_out, moe_router_group, moe_router_expert,
              moe_w1, moe_w3, moe_w2):
    lb_soft = jax.nn.softmax(hgrn_lower_bounds.astype(jnp.float32), axis=0)
    lb_all = jnp.cumsum(lb_soft, axis=0) - lb_soft[0]
    cond = jax.nn.silu(c)
    for layer in range(DEPTH):
        mod = jnp.einsum('bd,sde->sbe', cond, ada_w[layer]) + ada_b[layer][:, None, :]
        j = layer // N_MIXERS

        shift, scale, gate = jnp.split(mod[0], 3, axis=-1)
        h = rms_norm(x, norm_g[layer, 0]) * (1.0 + scale[:, None, :]) + shift[:, None, :]
        if layer % N_MIXERS == 0:
            y = nsa_mixer(h, rel_bias, nsa_w_in[j], nsa_q_gain[j], nsa_k_gain[j],
                          nsa_cmp_pe[j], nsa_cmp_w1[j], nsa_cmp_w2[j], nsa_w_out[j])
        else:
            y = hgrn2_mixer(h, lb_all[layer], hgrn_w_in[j], hgrn_out_gain[j], hgrn_w_out[j])
        x = x + gate[:, None, :] * y

        shift, scale, gate = jnp.split(mod[1], 3, axis=-1)
        h = rms_norm(x, norm_g[layer, 1]) * (1.0 + scale[:, None, :]) + shift[:, None, :]
        y = hier_moe(h, moe_router_group[layer], moe_router_expert[layer],
                     moe_w1[layer], moe_w3[layer], moe_w2[layer])
        x = x + gate[:, None, :] * y
    return x


def setup_inputs(seed=0):
    out = dict(first_inputs(seed))
    for name, value in second_inputs(seed + 1).items():
        if name != "x":
            out[name + "_2"] = value
    return out


def reference(
    x, ffn1_norm, ffn1_w_gate, ffn1_w_up, ffn1_w_down, mix_norm, w_in, pool_w, pool_scale,
    fourier_w, lam_q1, lam_k1, lam_q2, lam_k2, attn_head_norm, w_out, ffn2_norm, ffn2_w_gate,
    ffn2_w_up, ffn2_w_down, final_norm, c_2, ada_w_2, ada_b_2, norm_g_2, rel_bias_2, nsa_w_in_2,
    nsa_q_gain_2, nsa_k_gain_2, nsa_cmp_pe_2, nsa_cmp_w1_2, nsa_cmp_w2_2, nsa_w_out_2,
    hgrn_w_in_2, hgrn_lower_bounds_2, hgrn_out_gain_2, hgrn_w_out_2, moe_router_group_2,
    moe_router_expert_2, moe_w1_2, moe_w3_2, moe_w2_2,
):
    x = first_block(
        x, ffn1_norm, ffn1_w_gate, ffn1_w_up, ffn1_w_down, mix_norm, w_in, pool_w, pool_scale,
        fourier_w, lam_q1, lam_k1, lam_q2, lam_k2, attn_head_norm, w_out, ffn2_norm,
        ffn2_w_gate, ffn2_w_up, ffn2_w_down, final_norm,
    )
    return second_block(
        x, c_2, ada_w_2, ada_b_2, norm_g_2, rel_bias_2, nsa_w_in_2, nsa_q_gain_2, nsa_k_gain_2,
        nsa_cmp_pe_2, nsa_cmp_w1_2, nsa_cmp_w2_2, nsa_w_out_2, hgrn_w_in_2, hgrn_lower_bounds_2,
        hgrn_out_gain_2, hgrn_w_out_2, moe_router_group_2, moe_router_expert_2, moe_w1_2,
        moe_w3_2, moe_w2_2,
    )


_drawn_inputs = setup_inputs


def setup_inputs(seed=0):
    import zlib

    import numpy as np

    out = dict(_drawn_inputs(seed))
    spreads = {}
    factors = {'ada_b_2': 3.345,
     'norm_g_2': 4.691,
     'nsa_q_gain_2': 8.0,
     'nsa_k_gain_2': 8.0,
     'nsa_cmp_pe_2': 8.0,
     'hgrn_lower_bounds_2': 8.0,
     'hgrn_out_gain_2': 8.0}
    for name, (base, spread) in spreads.items():
        noise = np.random.default_rng([zlib.crc32(name.encode()), seed]).standard_normal(out[name].shape)
        drawn = base * np.exp(spread * noise) if base else spread * noise
        out[name] = jnp.asarray(drawn.astype(out[name].dtype))
    for name, factor in factors.items():
        out[name] = (out[name] * factor).astype(out[name].dtype)
    return out
```

```python
import concourse.bass as bass
from concourse import mybir
from contextlib import ExitStack
import math

FP32 = mybir.dt.float32
I32 = mybir.dt.int32
ALU = mybir.AluOpType
ACT = mybir.ActivationFunctionType
AXX = mybir.AxisListType.X

SEQ, DM, DFF, EPS = 512, 1024, 2816, 1e-6
P = 128
TT = SEQ // P
KT = DM // P


COLS = [("ffn1_norm", 1024), ("mix_norm", 1024), ("ffn2_norm", 1024), ("pool_scale", 256),
        ("attn_head_norm", 512), ("c_2", 1024), ("ada_b_2", 3072), ("norm_g_2", 1024),
        ("nsa_q_gain_2", 64), ("nsa_k_gain_2", 64), ("hgrn_lower_bounds_2", 1024), ("hgrn_out_gain_2", 128)]
COUNT = {"ffn1_norm": 2, "mix_norm": 2, "ffn2_norm": 2, "pool_scale": 2, "attn_head_norm": 2, "c_2": 1,
         "ada_b_2": 4, "norm_g_2": 4, "nsa_q_gain_2": 1, "nsa_k_gain_2": 3, "hgrn_lower_bounds_2": 2, "hgrn_out_gain_2": 1}
AT, NCOLS = {}, 0
for _name, _width in COLS:
    AT[_name] = (NCOLS, max(_width // P, 1))
    NCOLS += COUNT[_name] * AT[_name][1]


class Chip:

    def __init__(self, nc, ctx, dram):
        self.nc, self.dram = nc, dram
        self.x = ctx.enter_context(nc.sbuf_tensor("x_tok", [P, TT, DM], FP32))
        self.ident = ctx.enter_context(nc.sbuf_tensor("ident", [P, P], FP32))
        self.ones = ctx.enter_context(nc.sbuf_tensor("ones", [P, P], FP32))
        self.cols = ctx.enter_context(nc.sbuf_tensor("cols", [P, NCOLS], FP32))

        self.cond = ctx.enter_context(nc.sbuf_tensor("cond", [P, KT], FP32))
        self.mod = ctx.enter_context(nc.sbuf_tensor("mod", [P, 4, 3, KT], FP32))
        self.mod_gain = ctx.enter_context(nc.sbuf_tensor("mod_gain", [P, 4, KT], FP32))
        self.stored = ctx.enter_context(nc.semaphore("stored"))

    def gain(self, name, i):
        at, n = AT[name]
        return self.cols[:, at + i * n:at + (i + 1) * n]


class Scope:

    def __init__(self, nc, stage):
        self.nc, self.stage, self.sems = nc, stage, []

    def __enter__(self):
        self.ctx = ExitStack()
        self.block_ctx = ExitStack()
        return self

    def sb(self, name, shape, dt=FP32):
        return self.ctx.enter_context(self.nc.sbuf_tensor(f"{self.stage}_{name}", shape, dt))

    def ps(self, name, shape):
        return self.ctx.enter_context(self.nc.psum_tensor(f"{self.stage}_{name}", shape, FP32))

    def sem(self, name):
        self.sems.append(self.nc.alloc_semaphore(f"{self.stage}_{name}"))
        return self.sems[-1]

    def block(self, name=""):
        self.block_ctx.close()
        return self.block_ctx.enter_context(self.nc.Block(self.stage + name))

    def __exit__(self, *what):
        self.block_ctx.__exit__(*what)
        self.ctx.__exit__(*what)
        if what[0] is None:
            self.nc.clear_and_free_semaphores(self.sems)
            self.nc.all_engine_barrier()


class Norm:

    def __init__(self, chip, s, banks, hT=None, xn=None):
        self.chip, self.nc, self.banks = chip, chip.nc, banks
        if hT is None:
            hT, xn = s.sb("hT", [P, KT * SEQ])[:, :], s.sb("xn", [P, TT * DM])[:, :]
        self.hT = hT.rearrange("p (k t) -> p k t", k=KT)
        self.xn = xn.rearrange("p (t d) -> p t d", t=TT)
        self.ssq = s.sb("ssq", [P, TT])
        self.var = s.sb("var", [P, TT])
        self.rvar = s.sb("rvar", [P, TT])
        self.rstd = s.sb("rstd", [P, TT])
        self.squared = s.sem("squared")
        self.var_ready = s.sem("var_ready")
        self.rstd_ready = s.sem("rstd_ready")
        self.xn_ready = s.sem("xn_ready")
        self.turned = s.sem("turned")
        self.hT_ready = s.sem("hT_ready")

    def scalar_stats(self, act):
        for t in range(TT):
            act.activation(self.xn[:, t, :], self.chip.x[:, t, :], ACT.Square,
                           accum_out=self.ssq[:, t:t + 1]).then_inc(self.squared, 1)
        act.wait_ge(self.var_ready, 2)
        act.activation(self.rstd[:, :], self.rvar[:, :], ACT.Sqrt).then_inc(self.rstd_ready, 1)

    def scalar_evacuate(self, act, gain, shift=None):
        for k in range(KT):
            act.wait_ge(self.turned, k + 1)
            if shift is None:
                act.activation(self.hT[:, k, :], self.banks[k % 4][:, :], ACT.Copy,
                               scale=gain[:, k:k + 1]).then_inc(self.hT_ready, 1)
            else:
                act.activation(self.hT[:, k, :], self.banks[k % 4][:, :], ACT.Identity,
                               scale=gain[:, k:k + 1], bias=shift[:, k:k + 1]).then_inc(self.hT_ready, 1)

    def vector(self, dve):
        dve.wait_ge(self.squared, TT)
        dve.tensor_scalar(self.var[:, :], self.ssq[:, :], 1.0 / DM, EPS, ALU.mult, ALU.add)\
            .then_inc(self.var_ready, 1)
        dve.wait_ge(self.var_ready, 1)
        dve.reciprocal(self.rvar[:, :], self.var[:, :]).then_inc(self.var_ready, 1)
        dve.wait_ge(self.rstd_ready, 1)
        for t in range(TT):
            dve.tensor_scalar(self.xn[:, t, :], self.chip.x[:, t, :], self.rstd[:, t:t + 1], None, ALU.mult)\
                .then_inc(self.xn_ready, 1)

    def tensor(self, pe):
        for k in range(KT):
            if k >= 4:
                pe.wait_ge(self.hT_ready, k - 3)
            for t in range(TT):
                if k == 0:
                    pe.wait_ge(self.xn_ready, t + 1)
                last = pe.transpose(self.banks[k % 4][:, t * P:(t + 1) * P],
                                    self.xn[:, t, k * P:(k + 1) * P], self.chip.ident[:, :])
            last.then_inc(self.turned, 1)


def start(chip, name="start"):
    nc = chip.nc
    with Scope(nc, name) as s:
        x_loaded, zeroed, made = s.sem("x_loaded"), s.sem("zeroed"), s.sem("made")
        block = s.block()

        @block.sync
        def _(sp):
            sp.dma_start(chip.x[:, :, :], chip.dram["x"]).then_inc(x_loaded, 16)
            sp.wait_ge(x_loaded, 16)
            sp.dma_start(chip.cols[:, :], chip.dram["cols"]).then_inc(x_loaded, 16)
            sp.wait_ge(x_loaded, 32)

        @block.scalar
        def _(act):
            act.wait_ge(x_loaded, 32)
            act.activation(chip.cond[:, :], chip.gain("c_2", 0), ACT.Silu).then_inc(made, 1)

        @block.gpsimd
        def _(pool):
            pool.memset(chip.ones[:, :], 1.0)
            pool.memset(chip.ident[:, :], 0.0).then_inc(zeroed, 1)
            pool.wait_ge(zeroed, 1)
            pool.affine_select(out=chip.ident[:, :], in_=chip.ident[:, :], compare_op=ALU.not_equal, fill=1.0,
                               base=0, pattern=[[-1, P]], channel_multiplier=1).then_inc(made, 1)


FC = 256
NCHUNK = DFF // FC


def ffn(chip, name, which, gain):
    nc = chip.nc
    ada_dram = chip.dram["ada_w"]
    gate_up_dram, down_dram = chip.dram["ffn_gate_up"], chip.dram["ffn_down"]
    first = which * NCHUNK
    with Scope(nc, name) as s:
        gate_up_ps = [s.ps(f"gate_up{i}", [P, SEQ]) for i in range(4)]
        down_ps = [s.ps(f"down{i}", [P, SEQ]) for i in range(4)]
        norm = Norm(chip, s, down_ps)
        w_gu = [s.sb(f"w_gate_up{i}", [P, 2, KT, FC]) for i in range(2)]
        w_d = [s.sb(f"w_down{i}", [P, 2, DM]) for i in range(2)]
        silu_gate = s.sb("silu_gate", [P, 2, SEQ])
        hidden = [s.sb(f"hidden{i}", [P, 2, SEQ]) for i in range(2)]
        gate_up_loaded = [s.sem(f"gate_up_loaded{i}") for i in range(2)]
        down_loaded = [s.sem(f"down_loaded{i}") for i in range(2)]
        gate_up_done = s.sem("gate_up_done")
        silu_done = s.sem("silu_done")
        hidden_ready = s.sem("hidden_ready")
        down_done = s.sem("down_done")
        x_added = s.sem("x_added")
        ada_w = [s.sb(f"ada_w{i}", [P, 3 * DM]) for i in range(2)]
        ada_acc = s.sb("ada_acc", [P, 3 * DM])
        ada_loaded = [s.sem(f"ada_loaded{i}") for i in range(2)]
        ada_added, ada_summed, mod_ready = s.sem("ada_added"), s.sem("ada_summed"), s.sem("mod_ready")
        block = s.block()

        @block.sync
        def _(sp):
            def load(c, slot, again):
                if again:
                    sp.wait_ge(gate_up_done, 2 * (c - 1))
                sp.dma_start(w_gu[slot][:, :, :, :], gate_up_dram[first + c]).then_inc(gate_up_loaded[slot], 16)
                if again:
                    sp.wait_ge(down_done, 8 * (c - 1))
                sp.dma_start(w_d[slot][:, :, :], down_dram[first + c]).then_inc(down_loaded[slot], 16)

            def load_ada(k, slot, again):
                if again:
                    sp.wait_ge(ada_added, k - 1)
                sp.dma_start(ada_w[slot][:, :], ada_dram[which * KT + k]).then_inc(ada_loaded[slot], 16)

            load(0, 0, False)
            load(1, 1, False)
            load_ada(0, 0, False)
            load_ada(1, 1, False)
            with sp.Fori(1, KT // 2) as i:
                load(2 * i, 0, True)
                load_ada(2 * i, 0, True)
                load(2 * i + 1, 1, True)
                load_ada(2 * i + 1, 1, True)
            with sp.Fori(KT // 2, NCHUNK // 2) as i:
                load(2 * i, 0, True)
                load(2 * i + 1, 1, True)
            load(NCHUNK - 1, 0, True)

        @block.tensor
        def _(pe):
            norm.tensor(pe)
            pe.wait_ge(norm.hT_ready, KT)

            def gate_up(c, slot, n, again):
                pe.wait_ge(gate_up_loaded[slot], 16 * (n + 1))
                for f in range(2):
                    if again:
                        pe.wait_ge(hidden_ready, 2 * (c - 1) + f + 1)
                    for m in range(2):
                        for k in range(KT):
                            last = pe.matmul(gate_up_ps[2 * f + m][:, :], w_gu[slot][:, m, k, f * P:(f + 1) * P],
                                             norm.hT[:, k, :], start=(k == 0), stop=(k == KT - 1))
                    last.then_inc(gate_up_done, 1)

            def down(c, slot, n, again):
                pe.wait_ge(down_loaded[slot], 16 * (n + 1))
                pe.wait_ge(hidden_ready, 2 * (c + 1))
                for o in range(8):
                    if again or o >= 4:
                        pe.wait_ge(x_added, 8 * c + o - 3)
                    t, half = o // 2, o % 2
                    for f in range(2):
                        last = pe.matmul(down_ps[o % 4][:, :], hidden[slot][:, f, t * P:(t + 1) * P],
                                         w_d[slot][:, f, half * 512:(half + 1) * 512],
                                         start=(f == 0), stop=(f == 1))
                    last.then_inc(down_done, 1)

            gate_up(0, 0, 0, False)
            gate_up(1, 1, 0, True)
            down(0, 0, 0, False)
            gate_up(2, 0, 1, True)
            down(1, 1, 0, True)
            with pe.Fori(1, NCHUNK // 2) as i:
                gate_up(2 * i + 1, 1, i, True)
                down(2 * i, 0, i, True)
                gate_up(2 * i + 2, 0, i + 1, True)
                down(2 * i + 1, 1, i, True)
            pe.wait_ge(ada_added, KT)
            pe.wait_ge(hidden_ready, 2 * NCHUNK)
            for j in range(3 * KT):
                last = pe.matmul(gate_up_ps[0][:, j:j + 1], ada_acc[:, j * P:(j + 1) * P], chip.ones[:, 0:1],
                                 start=True, stop=True)
            last.then_inc(ada_summed, 1)
            down(NCHUNK - 1, 0, NCHUNK // 2, True)

        @block.scalar
        def _(act):
            norm.scalar_stats(act)
            norm.scalar_evacuate(act, gain)
            with act.Fori(0, NCHUNK) as c:
                for f in range(2):
                    act.wait_ge(gate_up_done, 2 * c + f + 1)
                    act.activation(silu_gate[:, f, :], gate_up_ps[2 * f][:, :], ACT.Silu).then_inc(silu_done, 1)

        @block.vector
        def _(dve):
            norm.vector(dve)

            def multiply(c, slot):
                for f in range(2):
                    dve.wait_ge(silu_done, 2 * c + f + 1)
                    dve.tensor_tensor(hidden[slot][:, f, :], silu_gate[:, f, :], gate_up_ps[2 * f + 1][:, :], ALU.mult)\
                        .then_inc(hidden_ready, 1)

            def add(c, again):
                for o in range(8):
                    t, half = o // 2, o % 2
                    xs = chip.x[:, t, half * 512:(half + 1) * 512]
                    dve.wait_ge(down_done, 8 * c + o + 1)
                    if again:
                        dve.wait_ge(x_added, 8 * c + o - 7)
                    dve.scalar_tensor_tensor(out=xs, in0=down_ps[o % 4][:, :], scalar=0.5, in1=xs,
                                             op0=ALU.mult, op1=ALU.add).then_inc(x_added, 1)

            def add_ada(k, slot, n, again):
                dve.wait_ge(ada_loaded[slot], 16 * (n + 1))
                if again:
                    dve.wait_ge(ada_added, k)
                    dve.scalar_tensor_tensor(out=ada_acc[:, :], in0=ada_w[slot][:, :],
                                             scalar=chip.cond[:, bass.ds(k, 1)], in1=ada_acc[:, :],
                                             op0=ALU.mult, op1=ALU.add).then_inc(ada_added, 1)
                else:
                    dve.tensor_scalar(ada_acc[:, :], ada_w[slot][:, :], chip.cond[:, 0:1], None, ALU.mult)\
                        .then_inc(ada_added, 1)

            multiply(0, 0)
            add_ada(0, 0, 0, False)
            multiply(1, 1)
            add(0, False)
            add_ada(1, 1, 0, True)
            with dve.Fori(1, KT // 2) as i:
                multiply(2 * i, 0)
                add(2 * i - 1, True)
                add_ada(2 * i, 0, i, True)
                multiply(2 * i + 1, 1)
                add(2 * i, True)
                add_ada(2 * i + 1, 1, i, True)
            with dve.Fori(KT // 2, NCHUNK // 2) as i:
                multiply(2 * i, 0)
                add(2 * i - 1, True)
                multiply(2 * i + 1, 1)
                add(2 * i, True)
            multiply(NCHUNK - 1, 0)
            add(NCHUNK - 2, True)
            dve.wait_ge(ada_summed, 1)
            mod = chip.mod[:, which, :, :]
            bias = chip.gain("ada_b_2", which).rearrange("p (a k) -> p a k", a=3)
            dve.tensor_tensor(mod, gate_up_ps[0][:, 0:3 * KT].rearrange("p (a k) -> p a k", a=3), bias, ALU.add)\
                .then_inc(mod_ready, 1)
            dve.wait_ge(mod_ready, 1)
            dve.scalar_tensor_tensor(out=chip.mod_gain[:, which, :], in0=mod[:, 1, :], scalar=1.0,
                                     in1=chip.gain("norm_g_2", which), op0=ALU.add, op1=ALU.mult)\
                .then_inc(mod_ready, 1)
            add(NCHUNK - 1, True)
            dve.wait_ge(mod_ready, 2)


class Banks:

    def __init__(self, s, n=8):
        self.n = n
        self.ps = [s.ps(f"bank{i}", [P, 512]) for i in range(n)]
        self.computed = s.sem("computed")
        self.evacuated = [s.sem("evacuated_by_scalar"), s.sem("evacuated_by_vector")]

    def open(self, pe, o):
        if o >= self.n:
            pe.wait_ge(self.evacuated[o % 2], (o - self.n) // 2 + 1)
        return self.ps[o % self.n]

    def take(self, eng, o):
        eng.wait_ge(self.computed, o + 1)
        return self.ps[o % self.n]

    def wait_for(self, eng, o):
        eng.wait_ge(self.evacuated[o % 2], o // 2 + 1)


def piece(dst, cols=(0, 512), scale=None, rows=(0, P), func=None, bias=None):
    return dst, rows, cols, scale, func, bias


def evacuate(banks, eng, parity, outputs, first=0, last=None):
    for o in sorted(outputs):
        if o % 2 != parity or o < first or (last is not None and o >= last):
            continue
        bank = banks.take(eng, o)
        for dst, rows, cols, scale, func, bias in outputs[o]:
            src = bank[rows[0]:rows[1], cols[0]:cols[1]]
            if bias is not None:
                ins = eng.activation(dst, src, func, bias=bias)
            elif parity == 0:
                ins = eng.activation(dst, src, func or ACT.Copy, scale=1.0 if scale is None else scale)
            elif scale is None:
                ins = eng.tensor_copy(dst, src)
            else:
                ins = eng.tensor_scalar(dst, src, scale, None, ALU.mult)
        ins.then_inc(banks.evacuated[parity], 1)


class Ring:

    def __init__(self, s, slots, loads, computed):
        self.slots = [s.sb(f"ring{i}", [P, 4096]) for i in range(slots)]
        self.loaded = [s.sem(f"ring_loaded{i}") for i in range(slots)]
        self.loads, self.computed = loads, computed

    def fill(self, sp, first=0, last=None):
        n = len(self.slots)
        for i in range(first, len(self.loads) if last is None else last):
            src, width, _ = self.loads[i]
            if i >= n:
                sp.wait_ge(self.computed, self.loads[i - n][2])
            sp.dma_start(self.slots[i % n][:, 0:width], src).then_inc(self.loaded[i % n], 16)

    def get(self, pe, i):
        n = len(self.slots)
        pe.wait_ge(self.loaded[i % n], 16 * (i // n + 1))
        return self.slots[i % n]

    def weights(self, pe, i):
        return self.get(pe, i)[:, :].rearrange("p (k n) -> p k n", k=KT)


class Own:

    def __init__(self, eng, done):
        self.eng, self.done, self.n = eng, done, 0

    def __call__(self, ins):
        self.n += 1
        ins.then_inc(self.done, 1)
        self.eng.wait_ge(self.done, self.n)


def token_major(pe, banks, o, w, hT):
    for t in range(TT):
        bank = banks.open(pe, o + t)
        for k in range(KT):
            last = pe.matmul(bank[:, :], hT[:, k, t * P:(t + 1) * P], w[:, k, :], start=(k == 0), stop=(k == KT - 1))
        last.then_inc(banks.computed, 1)


def feature_major(pe, banks, o, w, hT, tiles=4):
    for m in range(tiles):
        bank = banks.open(pe, o + m)
        for k in range(KT):
            last = pe.matmul(bank[:, :], w[:, k, m * P:(m + 1) * P], hT[:, k, :], start=(k == 0), stop=(k == KT - 1))
        last.then_inc(banks.computed, 1)


HEADS = 4
STRIP = 896


def mixer(chip, name, layer, lam_init):
    nc, dram = chip.nc, chip.dram
    scale = 64 ** -0.5
    units = [(h, i) for h in range(HEADS) for i in range(TT)]
    U = len(units)
    with Scope(nc, name) as s:
        banks = Banks(s)
        norm = Norm(chip, s, banks.ps[0:4])
        ws = [dram["mix_w"][layer, i] for i in range(6)]
        cs = [dram["mix_const"][i] for i in range(3)]
        ring = Ring(s, 3, [(w, 4096, n) for w, n in zip(ws[0:4] + cs + ws[4:6], [4, 8, 12, 16, 17, 18, 24, 36, 40])],
                    banks.computed)
        yT = norm.xn[:, :, :].rearrange("p t d -> p (t d)").rearrange("p (k t) -> p k t", k=KT)
        spare = norm.hT[:, :, :].rearrange("p k t -> p (k t)")
        pooled = spare[:, 0:1024].rearrange("p (a t) -> p a t", a=2)
        chan = spare[:, 1024:2048].rearrange("p (a n) -> p a n", a=2)
        timed = spare[:, 2048:4096].rearrange("p (a t) -> p a t", a=4)
        af = s.sb("af", [P, TT, 512])
        qT = s.sb("qT", [P, HEADS, SEQ])
        kT = s.sb("kT", [P, HEADS, SEQ])
        v = s.sb("v", [P, TT, 512])
        small = s.sb("small", [P, 1024])
        pool_blk = small[:, 0:256].rearrange("p (a n) -> p a n", a=2)
        four_w = small[:, 256:768].rearrange("p (a n) -> p a n", a=2)
        lam_in = small[:, 768:1024].rearrange("p (a n) -> p a n", a=4)
        chan_dft = s.sb("chan_dft", [P, 2, P])
        alibi = s.sb("alibi", [P, HEADS, STRIP])
        sc = [s.sb(f"scores{i}", [P, 2, SEQ]) for i in range(2)]
        ex = [s.sb(f"exps{i}", [P, 2, SEQ]) for i in range(2)]
        mix = [s.sb(f"mixed{i}", [P, SEQ]) for i in range(2)]
        mixT = [s.sb(f"mixedT{i}", [P, TT, P]) for i in range(2)]
        o_tok = s.sb("o_tok", [P, TT, HEADS, P])
        lam = s.sb("lam", [P, 8])
        lam_prod = s.sb("lam_prod", [P, 2, 64])
        head_gain = s.sb("head_gain", [P, HEADS])
        neg_max = s.sb("neg_max", [P, U, 2])
        sums = s.sb("sums", [P, U, 2])
        rsum = s.sb("rsum", [P, U, 2])
        ratio = s.sb("ratio", [P, U])
        hss = s.sb("hss", [P, 4, U])
        small_loaded, alibi_loaded = s.sem("small_loaded"), s.sem("alibi_loaded")
        lam_dots, lam_exps = s.sem("lam_dots"), s.sem("lam_exps")
        own_v = s.sem("own_v")
        scores_done, scores_read, max_ready = s.sem("scores_done"), s.sem("scores_read"), s.sem("max_ready")
        exps_done, mixed, mix_turned = s.sem("exps_done"), s.sem("mixed"), s.sem("mix_turned")
        mixT_ready, values_done, o_ready = s.sem("mixT_ready"), s.sem("values_done"), s.sem("o_ready")
        head_var, head_rstd, o_normed = s.sem("head_var"), s.sem("head_rstd"), s.sem("o_normed")
        x_added = s.sem("x_added")
        block = s.block()

        outputs = {}
        for t in range(TT):
            outputs[t] = [piece(af[:, t, :])]
            outputs[4 + t] = [piece(qT[:, t, :])]
            outputs[8 + t] = [piece(kT[:, t, :])]
            outputs[12 + t] = [piece(v[:, t, :])]
        for a in range(2):
            outputs[16 + a] = [piece(pooled[:, a, :])]
            outputs[18 + a] = [piece(chan[:, a, :])]
            outputs[20 + a] = [piece(timed[:, a, :])]
            outputs[22 + a] = [piece(timed[:, 2 + a, :])]
            outputs[24 + a] = [piece(yT[:, a, :], scale=chip.gain("pool_scale", layer)[:, a:a + 1])]
            outputs[26 + a] = [piece(yT[:, 2 + a, :])]
        HEAD_T = 28
        OUT = 32
        late = {HEAD_T + h: [piece(yT[:, 4 + h, :], scale=head_gain[:, h:h + 1])] for h in range(HEADS)}

        @block.sync
        def _(sp):
            ring.fill(sp, 0, 1)
            sp.dma_start(small[:, :], dram["mix_small"][layer]).then_inc(small_loaded, 16)
            sp.dma_start(chan_dft[:, :, :], dram["chan_dft"]).then_inc(small_loaded, 16)
            ring.fill(sp, 1, 3)
            sp.dma_start(alibi[:, :, :], dram["alibi"]).then_inc(alibi_loaded, 16)
            ring.fill(sp, 3)

        @block.tensor
        def _(pe):
            norm.tensor(pe)
            pe.wait_ge(norm.hT_ready, KT)
            token_major(pe, banks, 0, ring.weights(pe, 0), norm.hT)
            feature_major(pe, banks, 4, ring.weights(pe, 1), norm.hT)
            feature_major(pe, banks, 8, ring.weights(pe, 2), norm.hT)
            token_major(pe, banks, 12, ring.weights(pe, 3), norm.hT)
            banks.wait_for(pe, 2)
            banks.wait_for(pe, 3)
            for a in range(2):
                near = ring.get(pe, 4 + a)[:, :].rearrange("p (g s t) -> p g s t", g=2, s=TT)
                bank = banks.open(pe, 16 + a)
                for g in range(2):
                    for t in range(TT):
                        last = pe.matmul(bank[64 * g:64 * g + 64, :], af[:, t, P * a + 64 * g:P * a + 64 * g + 64],
                                         near[:, g, t, :], start=(t == 0), stop=(t == TT - 1))
                last.then_inc(banks.computed, 1)
            pe.wait_ge(small_loaded, 32)
            for part in range(2):
                bank = banks.open(pe, 18 + part)
                for a in range(2):
                    last = pe.matmul(bank[:, 256 * a:256 * a + 256], chan_dft[:, part, :], four_w[:, a, :],
                                     start=True, stop=True)
                last.then_inc(banks.computed, 1)
            dft = ring.get(pe, 6)[:, :].rearrange("p (c s t) -> p c s t", c=2, s=TT)
            for part in range(2):
                for a in range(2):
                    bank = banks.open(pe, 20 + 2 * part + a)
                    for t in range(TT):
                        last = pe.matmul(bank[:, :], af[:, t, 256 + P * a:256 + P * a + P], dft[:, part, t, :],
                                         start=(t == 0), stop=(t == TT - 1))
                    last.then_inc(banks.computed, 1)
            banks.wait_for(pe, 16)
            banks.wait_for(pe, 17)
            for a in range(2):
                bank = banks.open(pe, 24 + a)
                pe.matmul(bank[:, :], pool_blk[:, a, :], pooled[:, a, :], start=True, stop=True)\
                    .then_inc(banks.computed, 1)
            banks.wait_for(pe, 22)
            banks.wait_for(pe, 23)
            for m in range(2):
                bank = banks.open(pe, 26 + m)
                for part in range(2):
                    for a in range(2):
                        last = pe.matmul(bank[:, :], chan[:, part, 256 * a + P * m:256 * a + P * m + P],
                                         timed[:, 2 * part + a, :], start=(part == 0 and a == 0),
                                         stop=(part == 1 and a == 1))
                last.then_inc(banks.computed, 1)
            banks.wait_for(pe, 26)
            banks.wait_for(pe, 27)
            for step in range(U + 2):
                if step < U:
                    h, i = units[step]
                    if step >= 2:
                        pe.wait_ge(scores_read, step - 1)
                    for j in range(2):
                        last = pe.matmul(banks.ps[2 * (step % 2) + j][:, :],
                                         qT[64 * j:64 * j + 64, h, i * P:(i + 1) * P], kT[64 * j:64 * j + 64, h, :],
                                         start=True, stop=True)
                    last.then_inc(scores_done, 1)
                if 1 <= step <= U:
                    u = step - 1
                    pe.wait_ge(mixed, u + 1)
                    if u >= 2:
                        pe.wait_ge(mixT_ready, u - 1)
                    for b in range(TT):
                        last = pe.transpose(banks.ps[4 + u % 2][:, b * P:(b + 1) * P], mix[u % 2][:, b * P:(b + 1) * P],
                                            chip.ident[:, :])
                    last.then_inc(mix_turned, 1)
                if step >= 2:
                    u = step - 2
                    h, i = units[u]
                    pe.wait_ge(mixT_ready, u + 1)
                    if u >= 2:
                        pe.wait_ge(o_ready, u - 1)
                    for b in range(TT):
                        last = pe.matmul(banks.ps[6 + u % 2][:, 0:P], mixT[u % 2][:, b, :], v[:, b, h * P:(h + 1) * P],
                                         start=(b == 0), stop=(b == TT - 1))
                    last.then_inc(values_done, 1)
            for h in range(HEADS):
                bank = banks.open(pe, HEAD_T + h)
                for t in range(TT):
                    if h == 0:
                        pe.wait_ge(o_normed, 1)
                    last = pe.transpose(bank[:, t * P:(t + 1) * P], o_tok[:, t, h, :], chip.ident[:, :])
                last.then_inc(banks.computed, 1)
            banks.wait_for(pe, HEAD_T + 2)
            banks.wait_for(pe, HEAD_T + 3)
            token_major(pe, banks, OUT, ring.weights(pe, 7), yT)
            token_major(pe, banks, OUT + 4, ring.weights(pe, 8), yT)

        @block.scalar
        def _(act):
            norm.scalar_stats(act)
            norm.scalar_evacuate(act, chip.gain("mix_norm", layer))
            evacuate(banks, act, 0, outputs)
            act.wait_ge(lam_dots, 1)
            act.activation(lam[:, 2:4], lam[:, 0:2], ACT.Exp).then_inc(lam_exps, 1)
            for step in range(U + 2):
                if step < U:
                    u = step
                    act.wait_ge(max_ready, u + 1)
                    if u >= 2:
                        act.wait_ge(mixed, u - 1)
                    for j in range(2):
                        act.activation(ex[u % 2][:, j, :], sc[u % 2][:, j, :], ACT.Exp, bias=neg_max[:, u, j:j + 1],
                                       accum_out=sums[:, u, j:j + 1]).then_inc(exps_done, 1)
                if 1 <= step <= U:
                    u = step - 1
                    act.wait_ge(mix_turned, u + 1)
                    if u >= 2:
                        act.wait_ge(values_done, u - 1)
                    act.activation(mixT[u % 2][:, :, :].rearrange("p b q -> p (b q)"), banks.ps[4 + u % 2][:, :],
                                   ACT.Copy).then_inc(mixT_ready, 1)
                if step >= 2:
                    u = step - 2
                    h, i = units[u]
                    act.wait_ge(values_done, u + 1)
                    act.activation(o_tok[:, i, h, :], banks.ps[6 + u % 2][:, 0:P], ACT.Copy,
                                   scale=rsum[:, u, 0:1]).then_inc(o_ready, 1)
            act.wait_ge(head_var, 1)
            act.activation(hss[:, 3, :], hss[:, 2, :], ACT.Sqrt).then_inc(head_rstd, 1)
            evacuate(banks, act, 0, late)

        @block.vector
        def _(dve):
            own = Own(dve, own_v)
            norm.vector(dve)
            evacuate(banks, dve, 1, outputs)
            dve.wait_ge(small_loaded, 32)
            own(dve.tensor_tensor(lam_prod[:, :, :], lam_in[:, 0:4:2, :], lam_in[:, 1:4:2, :], ALU.mult))
            dve.reduce_sum(lam[:, 0:2], lam_prod[:, :, :], AXX).then_inc(lam_dots, 1)
            dve.wait_ge(lam_exps, 1)
            own(dve.tensor_tensor(lam[:, 4:5], lam[:, 3:4], lam[:, 2:3], ALU.subtract))
            own(dve.tensor_scalar(lam[:, 5:6], lam[:, 4:5], -lam_init, None, ALU.add))
            own(dve.tensor_scalar(head_gain[:, :], chip.gain("attn_head_norm", layer), 1.0 - lam_init, None, ALU.mult))
            dve.wait_ge(alibi_loaded, 16)
            for step in range(U + 1):
                if step < U:
                    u = step
                    h, i = units[u]
                    dve.wait_ge(scores_done, u + 1)
                    if u >= 2:
                        dve.wait_ge(exps_done, 2 * (u - 1))
                    c = 384 - P * i
                    for j in range(2):
                        last = dve.scalar_tensor_tensor(out=sc[u % 2][:, j, :], in0=banks.ps[2 * (u % 2) + j][:, :],
                                                        scalar=scale, in1=alibi[:, h, c:c + SEQ],
                                                        op0=ALU.mult, op1=ALU.add)
                        if j == 0:
                            own(last)
                    last.then_inc(scores_read, 1)
                    dve.wait_ge(scores_read, u + 1)
                    dve.tensor_reduce(neg_max[:, u, :], sc[u % 2][:, :, :], axis=AXX, op=ALU.max, negate=True)\
                        .then_inc(max_ready, 1)
                if step >= 1:
                    u = step - 1
                    dve.wait_ge(exps_done, 2 * (u + 1))
                    own(dve.reciprocal(rsum[:, u, :], sums[:, u, :]))
                    own(dve.scalar_tensor_tensor(out=ratio[:, u:u + 1], in0=sums[:, u, 0:1], scalar=rsum[:, u, 1:2],
                                                 in1=lam[:, 5:6], op0=ALU.mult, op1=ALU.mult))
                    if u >= 2:
                        dve.wait_ge(mix_turned, u - 1)
                    dve.scalar_tensor_tensor(out=mix[u % 2][:, :], in0=ex[u % 2][:, 1, :], scalar=ratio[:, u:u + 1],
                                             in1=ex[u % 2][:, 0, :], op0=ALU.mult, op1=ALU.add).then_inc(mixed, 1)
            dve.wait_ge(o_ready, U)
            flat = o_tok[:, :, :, :].rearrange("p t h e -> p (t h) e")
            squares = spare[:, 0:2048].rearrange("p (u e) -> p u e", u=U)
            own(dve.tensor_tensor(squares, flat, flat, ALU.mult))
            own(dve.reduce_sum(hss[:, 0, :], squares, AXX))
            own(dve.tensor_scalar(hss[:, 1, :], hss[:, 0, :], 1.0 / P, EPS, ALU.mult, ALU.add))
            dve.reciprocal(hss[:, 2, :], hss[:, 1, :]).then_inc(head_var, 1)
            dve.wait_ge(head_rstd, 1)
            dve.tensor_tensor(flat, flat, hss[:, 3, :].unsqueeze(2).broadcast_to([P, U, P]), ALU.mult)\
                .then_inc(o_normed, 1)
            evacuate(banks, dve, 1, late)
            for o in range(8):
                t, half = o % 4, o // 4
                xs = chip.x[:, t, half * 512:(half + 1) * 512]
                dve.tensor_tensor(xs, banks.take(dve, OUT + o)[:, :], xs, ALU.add).then_inc(x_added, 1)
            dve.wait_ge(x_added, 8)


NH, NG, HD = 16, 4, 64
NCMP = 31
BELOW = 512
MASKED = -1e30


def modulated_residual(dve, chip, banks, first, gate_row, scratch, own, x_added):
    for o in range(8):
        t, half = o % 4, o // 4
        cols = slice(half * 512, (half + 1) * 512)
        own(dve.tensor_tensor(scratch, banks.take(dve, first + o)[:, :], gate_row[:, cols], ALU.mult))
        dve.tensor_tensor(chip.x[:, t, cols], scratch, chip.x[:, t, cols], ALU.add).then_inc(x_added, 1)
        dve.wait_ge(x_added, o + 1)


def nsa(chip):
    nc, dram = chip.nc, chip.dram
    scale = HD ** -0.5
    units = [(h, i) for h in range(NH) for i in range(TT)]
    U = len(units)
    NB = [min(8 * i + 7, NCMP) for i in range(TT)]
    with Scope(nc, "nsa") as s:
        banks = Banks(s)
        ROWS, Q, K, V, C, GATES, QT, KTR = 0, 2, 10, 14, 18, 22, 23, 31
        PEB, HID, GROW, CMP, CMPT, OT, OUT = 35, 36, 37, 40, 42, 43, 51
        region = s.sb("region", [P, NH * BELOW])
        norm = Norm(chip, s, banks.ps[4:8], region[:, 0:4096], region[:, 4096:8192])
        strip = region[:, :].rearrange("p (h c) -> p h c", h=NH)
        loads = [(dram["nsa_w"][i], 4096, n) for i, n in enumerate([6, 10, 14, 18, 22])]
        loads += [(dram["nsa_cmp_w1"], 4096, HID + 3), (dram["nsa_w"][5], 4096, OUT + 4), (dram["nsa_w"][6], 4096, OUT + 8)]
        ring = Ring(s, 2, loads, banks.computed)
        q_tok = s.sb("q_tok", [P, TT, NH, HD])
        o_tok = q_tok
        k_tok = s.sb("k_tok", [P, TT, 2 * NG, HD])
        cT = s.sb("cT", [P, 2, NG, SEQ])
        oT = cT[:, :, :, :].rearrange("p a g t -> p (a g) t")
        qT = s.sb("qT", [P, KT, SEQ])
        kT = s.sb("kT", [P, 4, SEQ])
        v = s.sb("v", [P, TT, 2, NG, HD])
        gates = s.sb("gates", [P, TT, 3 * NH])
        w_gates = s.sb("w_gates", [P, KT, 3 * NH])
        small = s.sb("small", [64, 192])
        peT = small[:, 0:64].rearrange("p (a j) -> p a j", a=2)
        w2 = small[:, 64:192].rearrange("p (a n) -> p a n", a=2)
        table = s.sb("table", [64, NH])
        buckets = s.sb("buckets", [64, 640])
        rows = s.sb("rows", [NH, 640])
        peb = s.sb("peb", [64, 2])
        hid = s.sb("hid", [64, 2, NG * NCMP])
        kc_tok = s.sb("kc_tok", [NCMP, NG, HD])
        vc = s.sb("vc", [NCMP, NG * HD])
        kcT = s.sb("kcT", [P, 2, NCMP])
        gate_row = s.sb("gate_row", [P, DM])
        cmp_bias = k_tok[:, :, :, :].rearrange("p t g d -> p (t g d)")[:, 0:NH * TT * NCMP]\
            .rearrange("p (h i n) -> p h i n", h=NH, i=TT)
        sc = [s.sb(f"scores{i}", [P, 2, SEQ]) for i in range(2)]
        ex = [s.sb(f"exps{i}", [P, 2, SEQ]) for i in range(2)]
        pT = [s.sb(f"probsT{i}", [P, 2, SEQ]) for i in range(2)]
        diag = sc[1][:, :, :].rearrange("p a c -> p (a c)").rearrange("p (k n) -> p k n", k=KT)
        squares = sc[0][:, :, :].rearrange("p a c -> p (a c)").rearrange("p (h d) -> p h d", d=HD)
        qs = s.sb("q_stat", [P, 4, TT * NH])
        ks = s.sb("k_stat", [P, 4, TT * 2 * NG])
        cs = s.sb("cmp_stat", [NCMP, 4, NG])
        neg_max = s.sb("neg_max", [P, U, 2])
        sums = s.sb("sums", [P, U, 2])
        rsum = s.sb("rsum", [P, U, 2])
        fac = s.sb("fac", [P, U, 2])
        c_neg_max, c_raw_max, c_sums, c_safe, c_rsum, c_fac = [
            s.sb(f"cmp_{what}", [P, NH, TT]) for what in ("neg_max", "raw_max", "sums", "safe", "rsum", "fac")]
        small_loaded, rows_stored, strip_loaded = s.sem("small_loaded"), s.sem("rows_stored"), s.sem("strip_loaded")
        own_v, stat_var, stat_rstd = s.sem("own_v"), s.sem("stat_var"), s.sem("stat_rstd")
        q_normed, k_normed, kc_normed = s.sem("q_normed"), s.sem("k_normed"), s.sem("kc_normed")
        diag_ready, bias_filled = s.sem("diag_ready"), s.sem("bias_filled")
        c_scores, c_read, c_max, c_exps = s.sem("c_scores"), s.sem("c_read"), s.sem("c_max"), s.sem("c_exps")
        c_turned, c_probsT, c_values, c_out = s.sem("c_turned"), s.sem("c_probsT"), s.sem("c_values"), s.sem("c_out")
        scores_done, scores_read, max_ready = s.sem("scores_done"), s.sem("scores_read"), s.sem("max_ready")
        exps_done, turned, probsT, values_done = s.sem("exps_done"), s.sem("probs_turned"), s.sem("probsT"), s.sem("values_done")
        o_added, x_added = s.sem("o_added"), s.sem("x_added")
        block = s.block()

        outputs = {ROWS: [piece(rows[:, 0:512], rows=(0, NH))],
                   ROWS + 1: [piece(rows[:, 512:640], cols=(0, 128), rows=(0, NH))],
                   GATES: [piece(gates[:, :, :].rearrange("p t c -> p (t c)"), cols=(0, 192), func=ACT.Sigmoid)],
                   PEB: [piece(peb[:, :], cols=(0, 2), rows=(0, 64))],
                   CMP: [piece(kc_tok[:, :, :].rearrange("n g d -> n (g d)"), cols=(0, 256), rows=(0, NCMP))],
                   CMP + 1: [piece(vc[:, :], cols=(0, 256), rows=(0, NCMP))],
                   CMPT: [piece(kcT[:, a, :], cols=(32 * a, 32 * a + NCMP), scale=chip.gain("nsa_k_gain_2", 0))
                          for a in range(2)]}
        for t in range(TT):
            for a in range(2):
                outputs[Q + 4 * a + t] = [piece(q_tok[:, t, 8 * a:8 * a + 8, :].rearrange("p h d -> p (h d)"))]
            outputs[K + t] = [piece(k_tok[:, t, :, :].rearrange("p g d -> p (g d)"))]
            outputs[V + t] = [piece(v[:, t, :, :, :].rearrange("p a g d -> p (a g d)"))]
            outputs[C + t] = [piece(cT[0:64, t // 2, 2 * (t % 2) + a, :], rows=(64 * a, 64 * a + 64)) for a in range(2)]
            outputs[KTR + t] = [piece(kT[:, t, :], scale=chip.gain("nsa_k_gain_2", 1 + t // 2))]
        for m in range(KT):
            outputs[QT + m] = [piece(qT[:, m, :], scale=chip.gain("nsa_q_gain_2", 0))]
            outputs[OT + m] = [piece(oT[:, m, :])]
        for a in range(2):
            outputs[HID + 2 * a] = [piece(hid[:, a, :], cols=(0, NG * NCMP), rows=(0, 64), func=ACT.Silu,
                                          bias=peb[:, a:a + 1])]
            outputs[GROW + 2 * a] = [piece(gate_row[:, 512 * a:512 * a + 512])]

        def query(h, i):
            half, m = (h // 4) % 2, (h // 8) * 4 + h % 4
            return qT[64 * half:64 * half + 64, m, i * P:(i + 1) * P]

        @block.sync
        def _(sp):
            sp.dma_start(table[:, :], dram["nsa_table"]).then_inc(small_loaded, 16)
            sp.dma_start(buckets[:, :], dram["nsa_buckets"]).then_inc(small_loaded, 16)
            ring.fill(sp, 0, 2)
            sp.dma_start(small[:, :], dram["nsa_small"]).then_inc(small_loaded, 16)
            sp.dma_start(w_gates[:, :, :], dram["nsa_w_gates"]).then_inc(small_loaded, 16)
            banks.wait_for(sp, ROWS)
            banks.wait_for(sp, ROWS + 1)
            sp.dma_start(dram["bias_rows"], rows[:, :]).then_inc(rows_stored, 16)
            sp.wait_ge(rows_stored, 16)
            one = bass.AP(dram["bias_rows"].tensor, 0, [[0, P], [1, NH * 640]])
            sp.dma_start(dram["bias_copies"], one).then_inc(rows_stored, 16)
            ring.fill(sp, 2, 6)
            sp.wait_ge(banks.computed, GATES + 1)
            sp.wait_ge(rows_stored, 32)
            askew = bass.AP(dram["bias_copies"].tensor, 127, [[NH * 640 - 1, P], [640, NH], [1, BELOW]])
            sp.dma_start(strip, askew).then_inc(strip_loaded, 16)
            ring.fill(sp, 6)

        @block.gpsimd
        def _(pool):
            pool.wait_ge(banks.computed, KTR + 4)
            pool.memset(cmp_bias, MASKED).then_inc(bias_filled, 1)

        @block.tensor
        def _(pe):
            pe.wait_ge(small_loaded, 64)
            for o, (a, b) in enumerate(((0, 512), (512, 640))):
                pe.matmul(banks.open(pe, ROWS + o)[0:NH, 0:b - a], table[:, :], buckets[:, a:b],
                          start=True, stop=True).then_inc(banks.computed, 1)
            norm.tensor(pe)
            pe.wait_ge(norm.hT_ready, KT)
            token_major(pe, banks, Q, ring.weights(pe, 0), norm.hT)
            token_major(pe, banks, Q + 4, ring.weights(pe, 1), norm.hT)
            token_major(pe, banks, K, ring.weights(pe, 2), norm.hT)
            token_major(pe, banks, V, ring.weights(pe, 3), norm.hT)
            feature_major(pe, banks, C, ring.weights(pe, 4), norm.hT)
            bank = banks.open(pe, GATES)
            for t in range(TT):
                for k in range(KT):
                    last = pe.matmul(bank[:, 48 * t:48 * t + 48], norm.hT[:, k, t * P:(t + 1) * P], w_gates[:, k, :],
                                     start=(k == 0), stop=(k == KT - 1))
            last.then_inc(banks.computed, 1)
            pe.wait_ge(q_normed, TT)
            for m in range(KT):
                bank = banks.open(pe, QT + m)
                for t in range(TT):
                    last = pe.transpose(bank[:, t * P:(t + 1) * P],
                                        q_tok[:, t, 2 * m:2 * m + 2, :].rearrange("p h d -> p (h d)"), chip.ident[:, :])
                last.then_inc(banks.computed, 1)
            pe.wait_ge(k_normed, 1)
            for m in range(4):
                bank = banks.open(pe, KTR + m)
                for t in range(TT):
                    last = pe.transpose(bank[:, t * P:(t + 1) * P],
                                        k_tok[:, t, 2 * m:2 * m + 2, :].rearrange("p g d -> p (g d)"), chip.ident[:, :])
                last.then_inc(banks.computed, 1)
            w1 = ring.get(pe, 5)[:, :].rearrange("p (a j e) -> p a j e", a=2, j=32)
            bank = banks.open(pe, PEB)
            for a in range(2):
                for j in range(32):
                    last = pe.matmul(bank[0:64, a:a + 1], w1[0:64, a, j, :], peT[:, a, j:j + 1],
                                     start=(j == 0), stop=(j == 31))
            last.then_inc(banks.computed, 1)
            banks.wait_for(pe, C + 2)
            banks.wait_for(pe, C + 3)
            for a in range(2):
                bank = banks.open(pe, HID + 2 * a)
                for j in range(32):
                    last = pe.matmul(bank[0:64, 0:NG * NCMP].rearrange("p (g n) -> p g n", g=NG), w1[0:64, a, j, :],
                                     cT[0:64, a, :, j:j + 16 * (NCMP - 1) + 1:16], start=(j == 0), stop=(j == 31))
                last.then_inc(banks.computed, 1)
                pe.wait_ge(diag_ready, 1)
                bank = banks.open(pe, GROW + 2 * a)
                for k in range(4):
                    last = pe.matmul(bank[:, k * P:(k + 1) * P], chip.ones[:, :], diag[:, 4 * a + k, :],
                                     start=True, stop=True)
                last.then_inc(banks.computed, 1)
            banks.wait_for(pe, HID + 2)
            for a in range(2):
                bank = banks.open(pe, CMP + a)
                for g in range(NG):
                    last = pe.matmul(bank[0:NCMP, g * HD:(g + 1) * HD], hid[:, a, g * NCMP:(g + 1) * NCMP], w2[:, a, :],
                                     start=True, stop=True)
                last.then_inc(banks.computed, 1)
            pe.wait_ge(kc_normed, 1)
            bank = banks.open(pe, CMPT)
            for a in range(2):
                last = pe.transpose(bank[:, 32 * a:32 * a + NCMP],
                                    kc_tok[:, 2 * a:2 * a + 2, :].rearrange("n g d -> n (g d)"),
                                    chip.ident[0:NCMP, 0:NCMP])
            last.then_inc(banks.computed, 1)
            banks.wait_for(pe, CMPT)
            banks.wait_for(pe, CMPT - 1)
            for step in range(NH + 2):
                if step < NH:
                    h = step
                    half = (h // 4) % 2
                    if h >= 2:
                        pe.wait_ge(c_read, h - 1)
                    for i in range(TT):
                        last = pe.matmul(banks.ps[h % 2][:, i * NCMP:(i + 1) * NCMP], query(h, i),
                                         kcT[64 * half:64 * half + 64, h // 8, :], start=True, stop=True)
                    last.then_inc(c_scores, 1)
                if 1 <= step <= NH:
                    h = step - 1
                    pe.wait_ge(c_exps, TT * (h + 1))
                    if h >= 2:
                        pe.wait_ge(c_probsT, h - 1)
                    for i in range(TT):
                        last = pe.transpose(banks.ps[2 + h % 2][0:NCMP, i * P:(i + 1) * P],
                                            ex[h % 2][:, 0, i * NCMP:(i + 1) * NCMP], chip.ident[:, :])
                    last.then_inc(c_turned, 1)
                if step >= 2:
                    h = step - 2
                    pe.wait_ge(c_probsT, h + 1)
                    if h >= 2:
                        pe.wait_ge(c_out, h - 1)
                    for i in range(TT):
                        last = pe.matmul(banks.ps[4 + h % 2][:, i * HD:(i + 1) * HD], pT[h % 2][0:NCMP, 0, i * P:(i + 1) * P],
                                         vc[:, (h // 4) * HD:(h // 4 + 1) * HD], start=True, stop=True)
                    last.then_inc(c_values, 1)
            pe.wait_ge(c_out, NH)
            for step in range(U + 2):
                if step < U:
                    u = step
                    h, i = units[u]
                    half = (h // 4) % 2
                    W = (i + 1) * P
                    if u >= 2:
                        pe.wait_ge(scores_read, u - 1)
                    for b in range(2):
                        last = pe.matmul(banks.ps[2 * (u % 2) + b][:, 0:W], query(h, i),
                                         kT[64 * half:64 * half + 64, 2 * b + h // 8, 0:W], start=True, stop=True)
                    last.then_inc(scores_done, 1)
                if 1 <= step <= U:
                    u = step - 1
                    h, i = units[u]
                    pe.wait_ge(exps_done, 2 * (u + 1))
                    if u >= 1:
                        pe.wait_ge(probsT, 2 * u)
                    for b in range(2):
                        for c in range(i + 1):
                            last = pe.transpose(banks.ps[4 + b][:, c * P:(c + 1) * P], ex[u % 2][:, b, c * P:(c + 1) * P],
                                                chip.ident[:, :])
                    last.then_inc(turned, 1)
                if step >= 2:
                    u = step - 2
                    h, i = units[u]
                    pe.wait_ge(probsT, 2 * (u + 1))
                    if u >= 2:
                        pe.wait_ge(o_added, 2 * (u - 1))
                    for b in range(2):
                        for c in range(i + 1):
                            last = pe.matmul(banks.ps[6 + u % 2][:, b * HD:(b + 1) * HD], pT[u % 2][:, b, c * P:(c + 1) * P],
                                             v[:, c, b, h // 4, :], start=(c == 0), stop=(c == i))
                    last.then_inc(values_done, 1)
            pe.wait_ge(o_added, 2 * U)
            for m in range(KT):
                bank = banks.open(pe, OT + m)
                for t in range(TT):
                    last = pe.transpose(bank[:, t * P:(t + 1) * P],
                                        o_tok[:, t, 2 * m:2 * m + 2, :].rearrange("p h d -> p (h d)"), chip.ident[:, :])
                last.then_inc(banks.computed, 1)
            banks.wait_for(pe, OT + KT - 2)
            banks.wait_for(pe, OT + KT - 1)
            token_major(pe, banks, OUT, ring.weights(pe, 6), oT)
            token_major(pe, banks, OUT + 4, ring.weights(pe, 7), oT)

        @block.scalar
        def _(act):
            evacuate(banks, act, 0, outputs, 0, Q)
            norm.scalar_stats(act)
            norm.scalar_evacuate(act, chip.mod_gain[:, 0, :], chip.mod[:, 0, 0, :])
            evacuate(banks, act, 0, outputs, Q, V)
            for n, st in enumerate((qs, ks)):
                act.wait_ge(stat_var, n + 1)
                act.activation(st[:, 3, :], st[:, 2, :], ACT.Sqrt).then_inc(stat_rstd, 1)
            evacuate(banks, act, 0, outputs, V, PEB)
            banks.wait_for(act, PEB)
            evacuate(banks, act, 0, outputs, PEB, CMP + 1)
            act.wait_ge(stat_var, 3)
            act.activation(cs[:, 3, :], cs[:, 2, :], ACT.Sqrt).then_inc(stat_rstd, 1)
            evacuate(banks, act, 0, outputs, CMP + 1, OT)
            for step in range(NH + 1):
                if step < NH:
                    h = step
                    act.wait_ge(c_max, h + 1)
                    if h >= 2:
                        act.wait_ge(c_turned, h - 1)
                    for i in range(TT):
                        act.activation(ex[h % 2][:, 0, i * NCMP:(i + 1) * NCMP], sc[h % 2][:, 0, i * NCMP:(i + 1) * NCMP],
                                       ACT.Exp, bias=c_neg_max[:, h, i:i + 1], accum_out=c_sums[:, h, i:i + 1])\
                            .then_inc(c_exps, 1)
                if step >= 1:
                    h = step - 1
                    act.wait_ge(c_turned, h + 1)
                    if h >= 2:
                        act.wait_ge(c_values, h - 1)
                    act.activation(pT[h % 2][0:NCMP, 0, :], banks.ps[2 + h % 2][0:NCMP, :], ACT.Copy)\
                        .then_inc(c_probsT, 1)
            act.wait_ge(c_out, NH)
            for step in range(U + 1):
                if step < U:
                    u = step
                    h, i = units[u]
                    W = (i + 1) * P
                    act.wait_ge(max_ready, u + 1)
                    if u >= 2:
                        act.wait_ge(turned, u - 1)
                    for b in range(2):
                        act.activation(ex[u % 2][:, b, 0:W], sc[u % 2][:, b, 0:W], ACT.Exp, bias=neg_max[:, u, b:b + 1],
                                       accum_out=sums[:, u, b:b + 1]).then_inc(exps_done, 1)
                if step >= 1:
                    u = step - 1
                    h, i = units[u]
                    W = (i + 1) * P
                    act.wait_ge(turned, u + 1)
                    if u >= 2:
                        act.wait_ge(values_done, u - 1)
                    for b in range(2):
                        act.activation(pT[u % 2][:, b, 0:W], banks.ps[4 + b][:, 0:W], ACT.Copy).then_inc(probsT, 1)
            evacuate(banks, act, 0, outputs, OT)

        @block.vector
        def _(dve):
            own = Own(dve, own_v)
            evacuate(banks, dve, 1, outputs, 0, Q)
            norm.vector(dve)
            evacuate(banks, dve, 1, outputs, Q, V)

            def head_stats(t, n, st, src, at):
                width = src.shape[1]
                sq = squares[0:n, 0:width, :]
                own(dve.tensor_tensor(sq, src, src, ALU.mult))
                own(dve.reduce_sum(st[:, 0, at:at + width], sq, AXX))

            def head_var(st):
                own(dve.tensor_scalar(st[:, 1, :], st[:, 0, :], 1.0 / HD, EPS, ALU.mult, ALU.add))
                dve.reciprocal(st[:, 2, :], st[:, 1, :]).then_inc(stat_var, 1)

            for o in (V - 2, V - 1):
                banks.wait_for(dve, o)
            for t in range(TT):
                head_stats(t, P, qs, q_tok[:, t, :, :], NH * t)
            head_var(qs)
            for t in range(TT):
                head_stats(t, P, ks, k_tok[:, t, :, :], 2 * NG * t)
            dve.wait_ge(stat_rstd, 1)
            for t in range(TT):
                dve.tensor_tensor(q_tok[:, t, :, :], q_tok[:, t, :, :],
                                  qs[:, 3, NH * t:NH * t + NH].unsqueeze(2).broadcast_to([P, NH, HD]), ALU.mult)\
                    .then_inc(q_normed, 1)
            head_var(ks)
            dve.wait_ge(stat_rstd, 2)
            k_all = k_tok[:, :, :, :].rearrange("p t g d -> p (t g) d")
            dve.tensor_tensor(k_all, k_all, ks[:, 3, :].unsqueeze(2).broadcast_to([P, TT * 2 * NG, HD]), ALU.mult)\
                .then_inc(k_normed, 1)
            dve.tensor_tensor(diag, chip.ident[:, :].unsqueeze(1).broadcast_to([P, KT, P]),
                              chip.mod[:, 0, 2, :].unsqueeze(2).broadcast_to([P, KT, P]), ALU.mult).then_inc(diag_ready, 1)
            evacuate(banks, dve, 1, outputs, V, CMP)
            banks.wait_for(dve, CMP)
            head_stats(0, NCMP, cs, kc_tok[:, :, :], 0)
            head_var(cs)
            dve.wait_ge(stat_rstd, 3)
            dve.tensor_tensor(kc_tok[:, :, :], kc_tok[:, :, :], cs[:, 3, :].unsqueeze(2).broadcast_to([NCMP, NG, HD]),
                              ALU.mult).then_inc(kc_normed, 1)
            evacuate(banks, dve, 1, outputs, CMP, OT)
            dve.wait_ge(strip_loaded, 16)
            dve.wait_ge(bias_filled, 1)
            for i in range(TT):
                c = 384 - P * i + 31
                own(dve.tensor_copy(cmp_bias[:, :, i, 0:NB[i]], strip[:, :, c:c + 16 * (NB[i] - 1) + 1:16]))
            for step in range(NH + 2):
                if step < NH:
                    h = step
                    dve.wait_ge(c_scores, h + 1)
                    if h >= 2:
                        dve.wait_ge(c_exps, TT * (h - 1))
                    W = TT * NCMP
                    dve.scalar_tensor_tensor(out=sc[h % 2][:, 0, 0:W], in0=banks.ps[h % 2][:, 0:W], scalar=scale,
                                             in1=cmp_bias[:, h, :, :].rearrange("p i n -> p (i n)"),
                                             op0=ALU.mult, op1=ALU.add).then_inc(c_read, 1)
                    dve.wait_ge(c_read, h + 1)
                    own(dve.tensor_reduce(c_raw_max[:, h, :], sc[h % 2][:, 0, 0:W].rearrange("p (i n) -> p i n", i=TT),
                                          axis=AXX, op=ALU.max, negate=True))
                    dve.tensor_scalar(c_neg_max[:, h, :], c_raw_max[:, h, :], -MASKED * 1e-6, None, ALU.min)\
                        .then_inc(c_max, 1)
                if 1 <= step <= NH:
                    h = step - 1
                    dve.wait_ge(c_exps, TT * (h + 1))
                    own(dve.tensor_scalar(c_safe[:, h, :], c_sums[:, h, :], 1e-30, None, ALU.max))
                    own(dve.reciprocal(c_rsum[:, h, :], c_safe[:, h, :]))
                    own(dve.tensor_tensor(c_fac[:, h, :], c_rsum[:, h, :], gates[:, :, 3 * h], ALU.mult))
                if step >= 2:
                    h = step - 2
                    dve.wait_ge(c_values, h + 1)
                    dve.tensor_tensor(o_tok[:, :, h, :], banks.ps[4 + h % 2][:, 0:TT * HD].rearrange("p (i d) -> p i d", i=TT),
                                      c_fac[:, h, :].unsqueeze(2).broadcast_to([P, TT, HD]), ALU.mult).then_inc(c_out, 1)
            dve.wait_ge(c_out, NH)
            for step in range(U + 2):
                if step < U:
                    u = step
                    h, i = units[u]
                    W, c = (i + 1) * P, 384 - P * i
                    dve.wait_ge(scores_done, u + 1)
                    if u >= 2:
                        dve.wait_ge(exps_done, 2 * (u - 1))
                    for b in range(2):
                        last = dve.scalar_tensor_tensor(out=sc[u % 2][:, b, 0:W], in0=banks.ps[2 * (u % 2) + b][:, 0:W],
                                                        scalar=scale, in1=strip[:, h, c:c + W], op0=ALU.mult, op1=ALU.add)
                        if b == 0:
                            own(last)
                    last.then_inc(scores_read, 1)
                    dve.wait_ge(scores_read, u + 1)
                    dve.tensor_reduce(neg_max[:, u, :], sc[u % 2][:, :, 0:W], axis=AXX, op=ALU.max, negate=True)\
                        .then_inc(max_ready, 1)
                if 1 <= step <= U:
                    u = step - 1
                    h, i = units[u]
                    dve.wait_ge(exps_done, 2 * (u + 1))
                    own(dve.reciprocal(rsum[:, u, :], sums[:, u, :]))
                    own(dve.tensor_tensor(fac[:, u, :], rsum[:, u, :], gates[:, i, 3 * h + 1:3 * h + 3], ALU.mult))
                if step >= 2:
                    u = step - 2
                    h, i = units[u]
                    dve.wait_ge(values_done, u + 1)
                    for b in range(2):
                        dve.scalar_tensor_tensor(out=o_tok[:, i, h, :], in0=banks.ps[6 + u % 2][:, b * HD:(b + 1) * HD],
                                                 scalar=fac[:, u, b:b + 1], in1=o_tok[:, i, h, :],
                                                 op0=ALU.mult, op1=ALU.add).then_inc(o_added, 1)
                        dve.wait_ge(o_added, 2 * u + b + 1)
            evacuate(banks, dve, 1, outputs, OT)
            modulated_residual(dve, chip, banks, OUT, gate_row, sc[0][:, 0, :], own, x_added)


HG = 8
LEVELS = [None] + [1 << l for l in range(7)]


def hgrn(chip):
    nc, dram = chip.nc, chip.dram
    units = [(h, None) for h in range(HG)] + [(h, b) for h in range(HG) for b in LEVELS[1:]]
    U = len(units)
    with Scope(nc, "hgrn") as s:
        banks = Banks(s, 6)
        level_ps = [s.ps(f"level{i}", [P, SEQ]) for i in range(2)]
        FQ, VG, KK, GROW, OC, OT, OUT = 0, 16, 32, 40, 42, 50, 58
        a = s.sb("region_a", [P, 4096])
        b = s.sb("region_b", [P, 4096])
        norm = Norm(chip, s, banks.ps[0:4], a[:, :], b[:, :])
        qT = s.sb("qT", [P, HG, SEQ])
        kT = s.sb("kT", [P, HG, SEQ])
        cum = s.sb("cum", [P, HG, SEQ])
        v = s.sb("v", [P, TT, DM])
        g = s.sb("g", [P, TT, DM])
        scratch = a[:, :].rearrange("p (h t) -> p h t", h=HG)
        att = b[:, :].rearrange("p (h c t) -> p h c t", h=HG, c=TT)
        kk = a[:, :].rearrange("p (c d) -> p c d", c=TT)
        o_tok = cum[:, :, :].rearrange("p h t -> p (h t)").rearrange("p (c d) -> p c d", c=TT)
        o_heads = cum[:, :, :].rearrange("p h t -> p (h t)").rearrange("p (u e) -> p u e", e=P)
        squares = kT[:, :, :].rearrange("p h t -> p (h t)").rearrange("p (u e) -> p u e", e=P)
        cum_ch = cum[:, :, :].rearrange("p h t -> p (h t)").rearrange("p (u t) -> p u t", t=P)
        scratch_ch = a[:, :].rearrange("p (u t) -> p u t", t=P)
        counts = [4, 8, 12, 16, 20, 24, 28, 32, OUT + 4, OUT + 8]
        ring = Ring(s, 2, [(dram["hgrn_w"][i], 4096, n) for i, n in enumerate(counts)], banks.computed)
        masks = s.sb("masks", [P, len(LEVELS), P], I32)
        keep = s.sb("keep", [P, SEQ])
        M = [s.sb(f"decayed{i}", [P, SEQ]) for i in range(4)]
        state = [s.sb(f"state{i}", [P, HG, P]) for i in range(2)]
        decay = s.sb("decay", [P, HG, TT])
        lb = s.sb("lb", [P, 8, 2 * HG])
        ost = s.sb("o_stat", [P, 4, TT * HG])
        gate_row = s.sb("gate_row", [P, DM])
        diag = s.sb("diag", [P, KT, P])
        small_loaded, own_v = s.sem("small_loaded"), s.sem("own_v")
        lb_diff, lb_exp = s.sem("lb_diff"), s.sem("lb_exp")
        f_scaled, f_log, q_silu, g_silu, cum_ready = s.sem("f_scaled"), s.sem("f_log"), s.sem("q_silu"), s.sem("g_silu"), s.sem("cum_ready")
        gaps_ready, decays_ready, m_ready = s.sem("gaps_ready"), s.sem("decays_ready"), s.sem("m_ready")
        level_done, level_taken, att_zeroed = s.sem("level_done"), s.sem("level_taken"), s.sem("att_zeroed")
        cum_exp, last_gaps, last_exp, q_decayed, k_decayed = s.sem("cum_exp"), s.sem("last_gaps"), s.sem("last_exp"), s.sem("q_decayed"), s.sem("k_decayed")
        decay_ready, state_done, state_ready = s.sem("decay_ready"), s.sem("state_done"), s.sem("state_ready")
        o_var, o_rstd, o_normed, diag_ready, x_added = s.sem("o_var"), s.sem("o_rstd"), s.sem("o_normed"), s.sem("diag_ready"), s.sem("x_added")
        block = s.block()

        outputs = {}
        for m in range(HG):
            outputs[FQ + 2 * m] = [piece(cum[:, m, :], func=ACT.Sigmoid), piece(kT[:, m, :], func=ACT.Sigmoid, scale=-1.0)]
            outputs[FQ + 2 * m + 1] = [piece(qT[:, m, :])]
            outputs[KK + m] = [piece(kk[:, m // 2, 512 * (m % 2):512 * (m % 2) + 512])]
            outputs[OC + m] = [piece(o_tok[:, m // 2, 512 * (m % 2):512 * (m % 2) + 512])]
            outputs[OT + m] = [piece(qT[:, m, :], scale=chip.gain("hgrn_out_gain_2", 0))]
        for o in range(16):
            dst, half, t = (v, g)[o // 8], (o // 4) % 2, o % 4
            outputs[VG + o] = [piece(dst[:, t, 512 * half:512 * half + 512])]
        for half in range(2):
            outputs[GROW + half] = [piece(gate_row[:, 512 * half:512 * half + 512])]

        def halves(x, size):
            blocks = x.rearrange("p (n s) -> p n s", s=2 * size)
            return blocks[:, :, 0:size], blocks[:, :, size:2 * size]

        @block.sync
        def _(sp):
            ring.fill(sp, 0, 2)
            sp.dma_start(masks[:, :, :], dram["hgrn_masks"]).then_inc(small_loaded, 16)
            sp.dma_start(keep[:, :], dram["hgrn_keep"]).then_inc(small_loaded, 16)
            ring.fill(sp, 2)

        @block.gpsimd
        def _(pool):
            pool.wait_ge(norm.turned, KT)
            pool.memset(b[:, :], 0.0).then_inc(att_zeroed, 1)

        @block.tensor
        def _(pe):
            norm.tensor(pe)
            pe.wait_ge(norm.hT_ready, KT)
            for j in range(4):
                w = ring.weights(pe, j)
                for m in range(4):
                    bank = banks.open(pe, FQ + 4 * j + m)
                    for k in range(KT):
                        last = pe.matmul(bank[:, :], w[:, k, m * P:(m + 1) * P], norm.hT[:, k, :],
                                         start=(k == 0), stop=(k == KT - 1))
                    last.then_inc(banks.computed, 1)
            for step in range(16):
                if step % 4 == 0:
                    w = ring.weights(pe, 4 + step // 4)
                bank = banks.open(pe, VG + step)
                t = step % 4
                for k in range(KT):
                    last = pe.matmul(bank[:, :], norm.hT[:, k, t * P:(t + 1) * P], w[:, k, :],
                                     start=(k == 0), stop=(k == KT - 1))
                last.then_inc(banks.computed, 1)
                for u in range(4 * step, 4 * step + 4):
                    h, size = units[u]
                    if size is None:
                        pe.wait_ge(cum_ready, h + 1)
                        pe.wait_ge(q_silu, h + 1)
                        left, right = kT[:, h, :], qT[:, h, :]
                    else:
                        pe.wait_ge(m_ready, u - HG + 1)
                        left = right = M[u % 4][:, :]
                    if u >= 2:
                        pe.wait_ge(level_taken, u - 1)
                    for c in range(TT):
                        last = pe.matmul(level_ps[u % 2][:, c * P:(c + 1) * P], left[:, c * P:(c + 1) * P],
                                         right[:, c * P:(c + 1) * P], start=True, stop=True)
                    last.then_inc(level_done, 1)
            pe.wait_ge(k_decayed, 1)
            for m in range(HG):
                bank = banks.open(pe, KK + m)
                for i in range(4):
                    h = 4 * (m % 2) + i
                    last = pe.transpose(bank[:, i * P:(i + 1) * P], kT[:, h, (m // 2) * P:(m // 2 + 1) * P], chip.ident[:, :])
                last.then_inc(banks.computed, 1)
            pe.wait_ge(diag_ready, 1)
            for half in range(2):
                bank = banks.open(pe, GROW + half)
                for k in range(4):
                    last = pe.matmul(bank[:, k * P:(k + 1) * P], chip.ones[:, :], diag[:, 4 * half + k, :],
                                     start=True, stop=True)
                last.then_inc(banks.computed, 1)
            banks.wait_for(pe, KK + HG - 2)
            banks.wait_for(pe, KK + HG - 1)
            pe.wait_ge(level_taken, U)
            pe.wait_ge(q_decayed, 1)
            for c in range(TT):
                for half in range(2):
                    if c < TT - 1:
                        if c >= 1:
                            pe.wait_ge(state_ready, HG * (c - 1) + 4 * half + 4)
                        for i in range(4):
                            h = 4 * half + i
                            last = pe.matmul(level_ps[half][:, i * P:(i + 1) * P], kk[:, c, h * P:(h + 1) * P],
                                             v[:, c, h * P:(h + 1) * P], start=True, stop=True)
                        last.then_inc(state_done, 1)
                for half in range(2):
                    bank = banks.open(pe, OC + 2 * c + half)
                    for i in range(4):
                        h = 4 * half + i
                        last = pe.matmul(bank[:, i * P:(i + 1) * P], att[:, h, c, :], v[:, c, h * P:(h + 1) * P],
                                         start=True, stop=(c == 0))
                        if c >= 1:
                            pe.wait_ge(state_ready, HG * (c - 1) + h + 1)
                            last = pe.matmul(bank[:, i * P:(i + 1) * P], qT[:, h, c * P:(c + 1) * P],
                                             state[c % 2][:, h, :], start=False, stop=True)
                    last.then_inc(banks.computed, 1)
            pe.wait_ge(o_normed, 1)
            for m in range(KT):
                bank = banks.open(pe, OT + m)
                for t in range(TT):
                    last = pe.transpose(bank[:, t * P:(t + 1) * P], o_tok[:, t, m * P:(m + 1) * P], chip.ident[:, :])
                last.then_inc(banks.computed, 1)
            banks.wait_for(pe, OT + KT - 2)
            banks.wait_for(pe, OT + KT - 1)
            for half in range(2):
                w = ring.weights(pe, 8 + half)
                for t in range(TT):
                    o = 4 * half + t
                    if o >= 6:
                        pe.wait_ge(x_added, o - 5)
                        bank = banks.ps[(OUT + o) % 6]
                    else:
                        bank = banks.open(pe, OUT + o)
                    for k in range(KT):
                        last = pe.matmul(bank[:, :], qT[:, k, t * P:(t + 1) * P], w[:, k, :],
                                         start=(k == 0), stop=(k == KT - 1))
                    last.then_inc(banks.computed, 1)

        @block.scalar
        def _(act):
            norm.scalar_stats(act)
            act.wait_ge(lb_diff, 1)
            act.activation(lb[:, 2, :], lb[:, 1, :], ACT.Exp).then_inc(lb_exp, 1)
            norm.scalar_evacuate(act, chip.mod_gain[:, 2, :], chip.mod[:, 2, 0, :])
            evacuate(banks, act, 0, outputs, FQ, VG)
            for h in range(HG):
                act.wait_ge(f_scaled, h + 1)
                act.activation(cum[:, h, :], cum[:, h, :], ACT.Ln).then_inc(f_log, 1)
            banks.wait_for(act, VG - 1)
            for h in range(HG):
                act.activation(qT[:, h, :], qT[:, h, :], ACT.Silu).then_inc(q_silu, 1)
            for u in range(U):
                h, size = units[u]
                if size is not None:
                    act.wait_ge(gaps_ready, u - HG + 1)
                    act.activation(M[u % 4][:, :], M[u % 4][:, :], ACT.Exp).then_inc(decays_ready, 1)
                if u % 4 == 3:
                    evacuate(banks, act, 0, outputs, VG + u // 4, VG + u // 4 + 1)
            banks.wait_for(act, VG + 15)
            act.wait_ge(level_done, U)
            act.activation(scratch, cum[:, :, :], ACT.Exp).then_inc(cum_exp, 1)
            act.activation(decay[:, :, :].rearrange("p h c -> p (h c)"), cum_ch[:, :, P - 1], ACT.Exp).then_inc(decay_ready, 1)
            act.wait_ge(last_gaps, 1)
            act.activation(scratch, scratch, ACT.Exp).then_inc(last_exp, 1)
            for t in range(TT):
                act.activation(g[:, t, :], g[:, t, :], ACT.Silu).then_inc(g_silu, 1)
            evacuate(banks, act, 0, outputs, KK, OT)
            act.wait_ge(o_var, 1)
            act.activation(ost[:, 3, :], ost[:, 2, :], ACT.Sqrt).then_inc(o_rstd, 1)
            evacuate(banks, act, 0, outputs, OT)

        @block.vector
        def _(dve):
            own = Own(dve, own_v)
            low = [chip.gain("hgrn_lower_bounds_2", l) for l in range(2)]
            own(dve.tensor_tensor(lb[:, 0, 0:HG], low[0], low[1], ALU.max))
            own(dve.tensor_tensor(lb[:, 1, 0:HG], low[0], lb[:, 0, 0:HG], ALU.subtract))
            dve.tensor_tensor(lb[:, 1, HG:2 * HG], low[1], lb[:, 0, 0:HG], ALU.subtract).then_inc(lb_diff, 1)
            norm.vector(dve)
            dve.wait_ge(lb_exp, 1)
            own(dve.tensor_tensor(lb[:, 3, 0:HG], lb[:, 2, 0:HG], lb[:, 2, HG:2 * HG], ALU.add))
            own(dve.reciprocal(lb[:, 3, HG:2 * HG], lb[:, 3, 0:HG]))
            for l in range(2):
                own(dve.tensor_tensor(lb[:, 4, HG * l:HG * l + HG], lb[:, 2, HG * l:HG * l + HG], lb[:, 3, HG:2 * HG], ALU.mult))
            own(dve.tensor_tensor(lb[:, 5, 0:HG], lb[:, 4, 0:HG], lb[:, 4, HG:2 * HG], ALU.add))
            own(dve.tensor_tensor(lb[:, 6, 0:HG], lb[:, 5, 0:HG], lb[:, 4, 0:HG], ALU.subtract))
            own(dve.tensor_scalar(lb[:, 7, 0:HG], lb[:, 6, 0:HG], -1.0, 1.0, ALU.mult, ALU.add))
            low, rest = lb[:, 6, 0:HG], lb[:, 7, 0:HG]
            dve.tensor_tensor(diag[:, :, :], chip.ident[:, :].unsqueeze(1).broadcast_to([P, KT, P]),
                              chip.mod[:, 2, 2, :].unsqueeze(2).broadcast_to([P, KT, P]), ALU.mult).then_inc(diag_ready, 1)
            for h in range(HG):
                evacuate(banks, dve, 1, outputs, FQ + 2 * h, FQ + 2 * h + 2)
                banks.wait_for(dve, FQ + 2 * h)
                own(dve.tensor_scalar(kT[:, h, :], kT[:, h, :], rest[:, h:h + 1], None, ALU.mult))
                own(dve.tensor_scalar(cum[:, h, :], cum[:, h, :], rest[:, h:h + 1], low[:, h:h + 1], ALU.mult, ALU.add))
                dve.tensor_scalar(cum[:, h, :], cum[:, h, :], 1e-19, None, ALU.max).then_inc(f_scaled, 1)
            dve.wait_ge(small_loaded, 32)
            for h in range(HG):
                dve.wait_ge(f_log, h + 1)
                dve.tensor_tensor_scan(cum[:, h, :], keep[:, :], cum[:, h, :], 0.0, ALU.mult, ALU.add).then_inc(cum_ready, 1)
            dve.wait_ge(cum_ready, HG)
            dve.wait_ge(q_silu, HG)
            dve.wait_ge(att_zeroed, 1)
            for u in range(U + 2):
                if u < U and units[u][1] is not None:
                    h, size = units[u]
                    if u - 4 >= HG:
                        dve.wait_ge(level_done, u - 3)
                    c1, c2 = halves(cum[:, h, :], size)
                    m1, m2 = halves(M[u % 4][:, :], size)
                    mid = c1[:, :, size - 1:size].broadcast_to([P, SEQ // (2 * size), size])
                    own(dve.tensor_tensor(m1, mid, c1, ALU.subtract))
                    dve.tensor_tensor(m2, c2, mid, ALU.subtract).then_inc(gaps_ready, 1)
                if 1 <= u <= U and units[u - 1][1] is not None:
                    w = u - 1
                    h, size = units[w]
                    dve.wait_ge(decays_ready, w - HG + 1)
                    m1, m2 = halves(M[w % 4][:, :], size)
                    k1, _ = halves(kT[:, h, :], size)
                    _, q2 = halves(qT[:, h, :], size)
                    own(dve.tensor_tensor(m1, m1, k1, ALU.mult))
                    dve.tensor_tensor(m2, m2, q2, ALU.mult).then_inc(m_ready, 1)
                if u >= 2:
                    w = u - 2
                    h, size = units[w]
                    dve.wait_ge(level_done, w + 1)
                    if w >= 1:
                        dve.wait_ge(level_taken, w)
                    dve.copy_predicated(att[:, h, :, :], masks[:, LEVELS.index(size), :].unsqueeze(1).broadcast_to([P, TT, P]),
                                        level_ps[w % 2][:, :].rearrange("p (c t) -> p c t", c=TT)).then_inc(level_taken, 1)
                if u % 4 == 3 and u < U:
                    evacuate(banks, dve, 1, outputs, VG + u // 4, VG + u // 4 + 1)
            dve.wait_ge(cum_exp, 1)
            dve.tensor_tensor(qT[:, :, :], qT[:, :, :], scratch, ALU.mult).then_inc(q_decayed, 1)
            dve.wait_ge(q_decayed, 1)
            dve.tensor_tensor(scratch_ch, cum_ch[:, :, P - 1:P].broadcast_to([P, HG * TT, P]), cum_ch, ALU.subtract)\
                .then_inc(last_gaps, 1)
            dve.wait_ge(last_exp, 1)
            dve.tensor_tensor(kT[:, :, :], kT[:, :, :], scratch, ALU.mult).then_inc(k_decayed, 1)
            evacuate(banks, dve, 1, outputs, KK, OC)
            dve.wait_ge(decay_ready, 1)
            for c in range(TT):
                if c < TT - 1:
                    for h in range(HG):
                        if h % 4 == 0:
                            dve.wait_ge(state_done, 2 * c + h // 4 + 1)
                        new = state[(c + 1) % 2][:, h, :]
                        inc = level_ps[h // 4][:, (h % 4) * P:(h % 4 + 1) * P]
                        if c == 0:
                            dve.tensor_copy(new, inc).then_inc(state_ready, 1)
                        else:
                            dve.wait_ge(state_ready, HG * (c - 1) + h + 1)
                            if h == 0:
                                dve.wait_ge(banks.computed, OC + 2 * c)
                            dve.scalar_tensor_tensor(out=new, in0=state[c % 2][:, h, :], scalar=decay[:, h, c:c + 1],
                                                     in1=inc, op0=ALU.mult, op1=ALU.add).then_inc(state_ready, 1)
                evacuate(banks, dve, 1, outputs, OC + 2 * c, OC + 2 * c + 2)
            banks.wait_for(dve, OT - 2)
            banks.wait_for(dve, OT - 1)
            own(dve.tensor_tensor(squares, o_heads, o_heads, ALU.mult))
            own(dve.reduce_sum(ost[:, 0, :], squares, AXX))
            own(dve.tensor_scalar(ost[:, 1, :], ost[:, 0, :], 1.0 / P, EPS, ALU.mult, ALU.add))
            dve.reciprocal(ost[:, 2, :], ost[:, 1, :]).then_inc(o_var, 1)
            dve.wait_ge(o_rstd, 1)
            own(dve.tensor_tensor(o_heads, o_heads, ost[:, 3, :].unsqueeze(2).broadcast_to([P, TT * HG, P]), ALU.mult))
            dve.wait_ge(g_silu, TT)
            dve.tensor_tensor(o_tok, o_tok, g[:, :, :], ALU.mult).then_inc(o_normed, 1)
            evacuate(banks, dve, 1, outputs, OT)
            modulated_residual(dve, chip, banks, OUT, gate_row, M[0][:, :], own, x_added)


NE, NEG = 16, 4
NOV = 7
FF = 512
U32 = mybir.dt.uint32


def moe(chip, name, layer):
    nc, dram = chip.nc, chip.dram
    part = 2 * layer + 1
    mod, mod_gain = chip.mod[:, part, :, :], chip.mod_gain[:, part, :]
    with Scope(nc, name) as s:
        ps = [s.ps(f"bank{i}", [P, 512]) for i in range(8)]
        gather_ps, up_ps, turn_ps = ps[0:2], ps[2:4], ps[4:8]
        norm = Norm(chip, s, ps[0:4])
        w_router = s.sb("w_router", [P, KT, NEG + NE])
        const = s.sb("const", [P, 512])
        earlier, slot_no = const[:, 0:P], const[:, P:2 * P]
        first_slot, expert_no, block_no = const[:, 256:272], const[:, 272:288], const[:, 288:288 + NOV]
        w13 = [s.sb(f"w13_{i}", [P, 2, KT, FF]) for i in range(2)]
        w2 = [s.sb(f"w2_{i}", [P, TT, DM]) for i in range(2)]
        gate_row = s.sb("gate_row", [P, DM])
        diag = norm.hT[:, 0:2, :].rearrange("p a t -> p (a t)").rearrange("p (k n) -> p k n", k=KT)
        logits = s.sb("logits", [P, TT, NEG + NE])
        group8 = s.sb("group8", [P, TT, 8])
        top = s.sb("top", [P, 2, TT, 8])
        top_at = s.sb("top_at", [P, 2, TT, 8], U32)
        top_f = s.sb("top_f", [P, 2, TT, 2])
        group_exp = s.sb("group_exp", [P, TT, NEG])
        pick = s.sb("pick", [P, TT, NEG])
        score = s.sb("score", [P, TT, NE])
        hot = s.sb("hot", [P, 2, TT, NE])
        member = s.sb("member", [P, TT, NE])
        tiny = s.sb("tiny", [P, 8, TT])
        weight = s.sb("weight", [P, 2, TT])
        place = s.sb("place", [P, TT, NE])
        over = s.sb("over", [P, 8, NE])
        slot_of = s.sb("slot_of", [P, 2, TT])
        route = s.sb("route", [P, 2, TT, NE])
        over_cmp = s.sb("over_cmp", [P, NOV, NE])
        over_expert = s.sb("over_expert", [P, NOV])
        over_expert_i = s.sb("over_expert_i", [P, NOV], I32)
        over_count_i = s.sb("over_count_i", [P, 1], I32)
        equal = s.sb("equal", [P, 2 * TT, P])
        sel = [s.sb(f"sel{i}", [P, TT, P]) for i in range(2)]
        sel_w = [s.sb(f"sel_w{i}", [P, TT, P]) for i in range(2)]
        sel_wT = [s.sb(f"sel_wT{i}", [P, SEQ]) for i in range(2)]
        xeT = [s.sb(f"xeT{i}", [P, KT, P]) for i in range(2)]
        silu_gate = s.sb("silu_gate", [P, FF])
        hid = s.sb("hid", [P, FF])
        hidT = s.sb("hidT", [P, 4, P])
        y = [s.sb(f"y{i}", [P, DM]) for i in range(2)]

        w_loaded = [s.sem(f"w13_loaded{i}") for i in range(2)]
        w2_loaded = [s.sem(f"w2_loaded{i}") for i in range(2)]
        small_loaded, own_v = s.sem("small_loaded"), s.sem("own_v")
        logits_done, exp_in, exp_out = s.sem("logits_done"), s.sem("exp_in"), s.sem("exp_out")
        member_ready, places_done, diag_ready, rows_done = s.sem("member_ready"), s.sem("places_done"), s.sem("diag_ready"), s.sem("rows_done")
        row_ready = s.sem("row_ready")
        sel_ready, gathered, xe_ready = s.sem("sel_ready"), s.sem("gathered"), s.sem("xe_ready")
        up_done, silu_done, hid_ready, hid_turned, hidT_ready = s.sem("up_done"), s.sem("silu_done"), s.sem("hid_ready"), s.sem("hid_turned"), s.sem("hidT_ready")
        down_done, y_ready, sel_turned, selT_ready = s.sem("down_done"), s.sem("y_ready"), s.sem("sel_turned"), s.sem("selT_ready")
        scattered, x_added = s.sem("scattered"), s.sem("x_added")
        slots_read, slots_moved, weighted = s.sem("slots_read"), s.sem("slots_moved"), s.sem("weighted")
        block = s.block()

        def gather(pe, slot, first_wait, second_wait):
            for i, wait in enumerate((first_wait, second_wait)):
                if wait is not None:
                    pe.wait_ge(xe_ready, wait)
                for k in range(4 * i, 4 * i + 4):
                    for t in range(TT):
                        last = pe.matmul(gather_ps[i][:, (k % 4) * P:(k % 4 + 1) * P], norm.xn[:, t, k * P:(k + 1) * P],
                                         sel[slot][:, t, :], start=(t == 0), stop=(t == TT - 1))
                last.then_inc(gathered, 1)

        def gate_up(pe, slot):
            for m in range(2):
                for k in range(KT):
                    last = pe.matmul(up_ps[m][:, :], xeT[slot][:, k, :], w13[slot][:, m, k, :], start=(k == 0), stop=(k == KT - 1))
                last.then_inc(up_done, 1)

        def turn(pe, bank, src, done):
            for t in range(TT):
                last = pe.transpose(bank[:, t * P:(t + 1) * P], src[:, t * P:(t + 1) * P], chip.ident[:, :])
            last.then_inc(done, 1)

        def down(pe, half, slot):
            bank, w = turn_ps[1 + half], w2[slot]
            for f in range(4):
                last = pe.matmul(bank[:, :], hidT[:, f, :], w[:, f, half * 512:(half + 1) * 512], start=(f == 0), stop=(f == 3))
            last.then_inc(down_done, 1)

        def scatter(pe, o, bank, slot):
            t, half = o // 2, o % 2
            pe.matmul(bank[:, :], sel_wT[slot][:, t * P:(t + 1) * P], y[slot][:, half * 512:(half + 1) * 512],
                      start=True, stop=True).then_inc(scattered, 1)

        def take_gathered(act, slot, b):
            for k in range(KT):
                if k % 4 == 0:
                    act.wait_ge(gathered, 2 * b + k // 4 + 1)
                ins = act.activation(xeT[slot][:, k, :], gather_ps[k // 4][:, (k % 4) * P:(k % 4 + 1) * P], ACT.Identity,
                                     scale=mod_gain[:, k:k + 1], bias=mod[:, 0, k:k + 1])
                if k % 4 == 3:
                    ins.then_inc(xe_ready, 1)

        def add_to_x(dve, o, bank):
            t, half = o // 2, o % 2
            xs = chip.x[:, t, half * 512:(half + 1) * 512]
            dve.tensor_tensor(xs, bank[:, :], xs, ALU.add).then_inc(x_added, 1)

        @block.sync
        def _(sp):
            sp.dma_start(w_router[:, :, :], dram["moe_router"][layer]).then_inc(small_loaded, 16)
            sp.dma_start(const[:, :], dram["moe_const"]).then_inc(small_loaded, 16)

            def load(b, slot, again):
                if again:
                    sp.wait_ge(up_done, 2 * (b - 1))
                sp.dma_start(w13[slot][:, :, :, :], dram["moe_w13"][NE * layer + b]).then_inc(w_loaded[slot], 16)
                if again:
                    sp.wait_ge(down_done, 2 * (b - 1))
                sp.dma_start(w2[slot][:, :, :], dram["moe_w2"][NE * layer + b]).then_inc(w2_loaded[slot], 16)

            load(0, 0, False)
            load(1, 1, False)
            with sp.Fori(1, NE // 2) as i:
                load(2 * i, 0, True)
                load(2 * i + 1, 1, True)

        @block.tensor
        def _(pe):
            norm.tensor(pe)
            pe.wait_ge(norm.hT_ready, KT)
            pe.wait_ge(small_loaded, 32)
            for t in range(TT):
                for k in range(KT):
                    last = pe.matmul(ps[4][:, 20 * t:20 * t + 20], norm.hT[:, k, t * P:(t + 1) * P], w_router[:, k, :],
                                     start=(k == 0), stop=(k == KT - 1))
            last.then_inc(logits_done, 1)
            pe.wait_ge(diag_ready, 1)
            for k in range(KT):
                last = pe.matmul(ps[6 + k // 4][:, (k % 4) * P:(k % 4 + 1) * P], chip.ones[:, :], diag[:, k, :],
                                 start=True, stop=True)
            last.then_inc(rows_done, 1)
            pe.wait_ge(member_ready, 1)
            for t in range(TT):
                for u in range(t + 1):
                    pe.matmul(ps[5][:, NE * t:NE * t + NE], earlier if u == t else chip.ones[:, :], member[:, u, :],
                              start=(u == 0), stop=(u == t))
            for u in range(TT):
                last = pe.matmul(ps[5][:, NE * TT:NE * TT + NE], chip.ones[:, :], member[:, u, :], start=(u == 0), stop=(u == 3))
            last.then_inc(places_done, 1)
            pe.wait_ge(row_ready, 2)

            def iteration(b, slot, n, peeled=None):
                pe.wait_ge(w_loaded[slot], 16 * (n + 1))
                pe.wait_ge(xe_ready, 2 * (b + 1))
                if peeled != 0:
                    pe.wait_ge(hid_ready, b)
                gate_up(pe, slot)
                if peeled != NE - 1:
                    pe.wait_ge(sel_ready, 2 * (b + 2))
                    gather(pe, 1 - slot, 2 * b + 1, 2 * b + 2)
                pe.wait_ge(hid_ready, b + 1)
                if peeled not in (0, 1):
                    pe.wait_ge(x_added, 8 * (b - 1))
                turn(pe, turn_ps[0], hid, hid_turned)
                if peeled != 0:
                    scatter_block(b, 1 - slot)
                pe.wait_ge(hidT_ready, b + 1)
                pe.wait_ge(w2_loaded[slot], 16 * (n + 1))
                for half in range(2):
                    if peeled != 0:
                        pe.wait_ge(x_added, 8 * (b - 1) + 5 + half)
                    down(pe, half, slot)
                pe.wait_ge(sel_ready, 2 * (b + 1))
                if peeled != 0:
                    pe.wait_ge(x_added, 8 * (b - 1) + 7)
                turn(pe, turn_ps[3], sel_w[slot][:, :, :].rearrange("p t s -> p (t s)"), sel_turned)

            def scatter_block(b, slot, turned=True):
                pe.wait_ge(y_ready, 2 * b)
                pe.wait_ge(selT_ready, b)
                for o in range(8):
                    if o == 3 and turned:
                        pe.wait_ge(hidT_ready, b + 1)
                    if o >= 4:
                        pe.wait_ge(x_added, 8 * (b - 1) + o - 3)
                    scatter(pe, o, turn_ps[(o + 1) % 4], slot)

            pe.wait_ge(sel_ready, 2)
            gather(pe, 0, None, None)
            iteration(0, 0, 0, peeled=0)
            iteration(1, 1, 0, peeled=1)
            with pe.Fori(1, NE // 2 - 1) as i:
                iteration(2 * i, 0, i)
                iteration(2 * i + 1, 1, i)
            iteration(NE - 2, 0, NE // 2 - 1)
            iteration(NE - 1, 1, NE // 2 - 1, peeled=NE - 1)
            scatter_block(NE, 1, turned=False)

        @block.scalar
        def _(act):
            norm.scalar_stats(act)
            norm.scalar_evacuate(act, mod_gain, mod[:, 0, :])
            act.wait_ge(exp_in, 1)
            act.activation(group_exp[:, :, :], group_exp[:, :, :], ACT.Exp).then_inc(exp_out, 1)
            act.wait_ge(exp_in, 2)
            act.activation(tiny[:, 1, :], tiny[:, 0, :], ACT.Exp).then_inc(exp_out, 1)
            act.wait_ge(rows_done, 1)
            for half in range(2):
                act.activation(gate_row[:, half * 512:(half + 1) * 512], ps[6 + half][:, :], ACT.Copy).then_inc(row_ready, 1)

            def iteration(b, slot, peeled=None):
                act.wait_ge(up_done, 2 * b + 1)
                if peeled != 0:
                    act.wait_ge(hid_ready, b)
                act.activation(silu_gate[:, :], up_ps[0][:, :], ACT.Silu).then_inc(silu_done, 1)
                if peeled != NE - 1:
                    take_gathered(act, 1 - slot, b + 1)
                act.wait_ge(hid_turned, b + 1)
                if peeled != 0:
                    act.wait_ge(down_done, 2 * b)
                act.activation(hidT[:, :, :].rearrange("p f s -> p (f s)"), turn_ps[0][:, :], ACT.Copy).then_inc(hidT_ready, 1)
                act.wait_ge(sel_turned, b + 1)
                if peeled not in (0, 1):
                    act.wait_ge(scattered, 8 * (b - 1))
                act.activation(sel_wT[slot][:, :], turn_ps[3][:, :], ACT.Copy).then_inc(selT_ready, 1)

            take_gathered(act, 0, 0)
            iteration(0, 0, peeled=0)
            iteration(1, 1, peeled=1)
            with act.Fori(1, NE // 2 - 1) as i:
                iteration(2 * i, 0)
                iteration(2 * i + 1, 1)
            iteration(NE - 2, 0)
            iteration(NE - 1, 1, peeled=NE - 1)

        @block.vector
        def _(dve):
            own = Own(dve, own_v)
            norm.vector(dve)
            own(dve.memset(group8[:, :, :], MASKED))
            dve.wait_ge(logits_done, 1)
            own(dve.tensor_copy(logits[:, :, :].rearrange("p t c -> p (t c)"), ps[4][:, 0:TT * (NEG + NE)]))
            dve.tensor_tensor(diag, chip.ident[:, :].unsqueeze(1).broadcast_to([P, KT, P]),
                              mod[:, 2, :].unsqueeze(2).broadcast_to([P, KT, P]), ALU.mult).then_inc(diag_ready, 1)
            dve.wait_ge(small_loaded, 32)
            own(dve.tensor_copy(group8[:, :, 0:NEG], logits[:, :, 0:NEG]))
            for t in range(TT):
                own(dve.max(top[:, 0, t, :], group8[:, t, :]))
                own(dve.max_index(top_at[:, 0, t, :], top[:, 0, t, :], group8[:, t, :]))
            own(dve.tensor_copy(top_f[:, 0, :, :], top_at[:, 0, :, 0:2]))
            dve.tensor_tensor(group_exp[:, :, :], logits[:, :, 0:NEG], top[:, 0, :, 0:1].broadcast_to([P, TT, NEG]),
                              ALU.subtract).then_inc(exp_in, 1)
            own(dve.tensor_tensor(pick[:, :, :], expert_no[:, 0:NEG].unsqueeze(1).broadcast_to([P, TT, NEG]),
                                  top_f[:, 0, :, 0:1].broadcast_to([P, TT, NEG]), ALU.is_equal))
            own(dve.tensor_scalar(pick[:, :, :], pick[:, :, :], -MASKED, MASKED, ALU.mult, ALU.add))
            for t in range(TT):
                own(dve.tensor_tensor(score[:, t, :].rearrange("p (g e) -> p g e", g=NEG),
                                      logits[:, t, NEG:NEG + NE].rearrange("p (g e) -> p g e", g=NEG),
                                      pick[:, t, :].unsqueeze(2).broadcast_to([P, NEG, 4]), ALU.add))
                own(dve.max(top[:, 1, t, :], score[:, t, :]))
                own(dve.max_index(top_at[:, 1, t, :], top[:, 1, t, :], score[:, t, :]))
            dve.tensor_tensor(tiny[:, 0, :], top[:, 1, :, 1], top[:, 1, :, 0], ALU.subtract).then_inc(exp_in, 1)
            own(dve.tensor_copy(top_f[:, 1, :, :], top_at[:, 1, :, 0:2]))
            for a in range(2):
                own(dve.tensor_tensor(hot[:, a, :, :], expert_no.unsqueeze(1).broadcast_to([P, TT, NE]),
                                      top_f[:, 1, :, a:a + 1].broadcast_to([P, TT, NE]), ALU.is_equal))
            dve.tensor_tensor(member[:, :, :], hot[:, 0, :, :], hot[:, 1, :, :], ALU.add).then_inc(member_ready, 1)
            dve.wait_ge(exp_out, 2)
            own(dve.reduce_sum(tiny[:, 2, :], group_exp[:, :, :], AXX))
            own(dve.tensor_scalar(tiny[:, 3, :], tiny[:, 1, :], 1.0, None, ALU.add))
            own(dve.tensor_tensor(tiny[:, 4, :], tiny[:, 3, :], tiny[:, 2, :], ALU.mult))
            own(dve.reciprocal(weight[:, 0, :], tiny[:, 4, :]))
            own(dve.tensor_tensor(weight[:, 1, :], weight[:, 0, :], tiny[:, 1, :], ALU.mult))
            dve.wait_ge(places_done, 1)
            count = over[:, 0, :]
            own(dve.tensor_copy(place[:, :, :].rearrange("p t e -> p (t e)"), ps[5][:, 0:TT * NE]))
            own(dve.tensor_copy(count, ps[5][:, TT * NE:(TT + 1) * NE]))
            own(dve.tensor_scalar(over[:, 1, :], count, float(P), None, ALU.is_gt))
            for i in range(2, 4):
                own(dve.scalar_tensor_tensor(out=over[:, i, :], in0=count, scalar=float(i * P), in1=over[:, i - 1, :],
                                             op0=ALU.is_gt, op1=ALU.add))
            ends = over[:, 4, :]
            own(dve.tensor_tensor_scan(ends, chip.ones[:, 0:NE], over[:, 3, :], 0.0, ALU.mult, ALU.add))
            own(dve.tensor_tensor(over[:, 5, :], ends, over[:, 3, :], ALU.subtract))
            own(dve.tensor_scalar(over[:, 6, :], over[:, 5, :], float(P), float((NE - 1) * P), ALU.mult, ALU.add))
            own(dve.tensor_tensor(over[:, 7, :], over[:, 6, :], first_slot, ALU.subtract))
            slots = route[:, 0, :, :]
            own(dve.tensor_scalar(slots, place[:, :, :], float(P), None, ALU.is_ge))
            own(dve.tensor_tensor(slots, slots, over[:, 7, :].unsqueeze(1).broadcast_to([P, TT, NE]), ALU.mult))
            own(dve.tensor_tensor(slots, slots, first_slot.unsqueeze(1).broadcast_to([P, TT, NE]), ALU.add))
            own(dve.tensor_tensor(place[:, :, :], place[:, :, :], slots, ALU.add))
            for a in range(2):
                own(dve.tensor_tensor(route[:, a, :, :], hot[:, a, :, :], place[:, :, :], ALU.mult))
                own(dve.reduce_sum(slot_of[:, a, :], route[:, a, :, :], AXX))
            own(dve.tensor_tensor(over_cmp[:, :, :], ends.unsqueeze(1).broadcast_to([P, NOV, NE]),
                                  block_no.unsqueeze(2).broadcast_to([P, NOV, NE]), ALU.is_le))
            own(dve.reduce_sum(over_expert[:, :], over_cmp[:, :, :], AXX))
            own(dve.tensor_scalar(over_expert[:, :], over_expert[:, :], float(NE - 1), float(NE * layer), ALU.min, ALU.add))
            own(dve.tensor_copy(over_expert_i[:, :], over_expert[:, :]))
            own(dve.tensor_copy(over_count_i[:, :], ends[:, NE - 1:NE]))

            def next_block(slot, n):
                dve.tensor_tensor(equal[:, :, :], slot_no.unsqueeze(1).broadcast_to([P, 2 * TT, P]),
                                  slot_of[:, :, :].rearrange("p a t -> p (a t)").unsqueeze(2).broadcast_to([P, 2 * TT, P]),
                                  ALU.is_equal).then_inc(slots_read, 1)
                dve.wait_ge(slots_read, n + 1)
                dve.tensor_scalar(slot_of[:, :, :], slot_of[:, :, :], -float(P), None, ALU.add).then_inc(slots_moved, 1)
                dve.tensor_tensor(sel[slot][:, :, :], equal[:, 0:TT, :], equal[:, TT:2 * TT, :], ALU.add).then_inc(sel_ready, 1)
                dve.wait_ge(sel_ready, 2 * n + 1)
                dve.wait_ge(slots_moved, n + 1)
                dve.tensor_tensor(equal[:, :, :], equal[:, :, :],
                                  weight[:, :, :].rearrange("p a t -> p (a t)").unsqueeze(2).broadcast_to([P, 2 * TT, P]),
                                  ALU.mult).then_inc(weighted, 1)
                dve.wait_ge(weighted, n + 1)
                dve.tensor_tensor(sel_w[slot][:, :, :], equal[:, 0:TT, :], equal[:, TT:2 * TT, :], ALU.add).then_inc(sel_ready, 1)
                dve.wait_ge(sel_ready, 2 * n + 2)

            def add_block(b, peeled=None):
                for o in range(8):
                    dve.wait_ge(scattered, 8 * (b - 1) + o + 1)
                    if peeled != 1:
                        dve.wait_ge(x_added, 8 * (b - 2) + o + 1)
                    add_to_x(dve, o, turn_ps[(o + 1) % 4])

            def iteration(b, slot, peeled=None):
                dve.wait_ge(silu_done, b + 1)
                dve.wait_ge(up_done, 2 * b + 2)
                if peeled != 0:
                    dve.wait_ge(hid_turned, b)
                dve.tensor_tensor(hid[:, :], silu_gate[:, :], up_ps[1][:, :], ALU.mult).then_inc(hid_ready, 1)
                if peeled != 0:
                    add_block(b, peeled)
                for half in range(2):
                    dve.wait_ge(down_done, 2 * b + half + 1)
                    cols = slice(half * 512, (half + 1) * 512)
                    dve.tensor_tensor(y[slot][:, cols], turn_ps[1 + half][:, :], gate_row[:, cols], ALU.mult).then_inc(y_ready, 1)
                if peeled not in (NE - 2, NE - 1):
                    dve.wait_ge(sel_turned, b + 1)
                    next_block(slot, b + 2)

            next_block(0, 0)
            next_block(1, 1)
            dve.wait_ge(row_ready, 2)
            iteration(0, 0, peeled=0)
            iteration(1, 1, peeled=1)
            with dve.Fori(1, NE // 2 - 1) as i:
                iteration(2 * i, 0)
                iteration(2 * i + 1, 1)
            iteration(NE - 2, 0, peeled=NE - 2)
            iteration(NE - 1, 1, peeled=NE - 1)
            add_block(NE)

        up_done, down_done, hid_turned, gathered, xe_ready, sel_turned, scattered, x_added = [
            s.sem("over_" + what) for what in ("up_done", "down_done", "hid_turned", "gathered", "xe_ready", "sel_turned",
                                               "scattered", "x_added")]
        silu_done, hid_ready, hidT_ready, y_ready, selT_ready, sel_steps, w_arrived, block_gone = [
            s.sem("over_" + what) for what in ("silu_done", "hid_ready", "hidT_ready", "y_ready", "selT_ready", "sel_steps",
                                               "w_arrived", "block_gone")]
        block = s.block("overflow")

        def if_overflow(eng):
            count = eng.value_load(over_count_i[0:1, 0:1], min_val=0, max_val=NOV)
            return eng.If(count > 0)

        @block.sync
        def _(sp):
            with if_overflow(sp):
                with sp.Fori(0, NOV) as j:
                    sp.wait_ge(block_gone, j + 1)
                    e = sp.value_load(over_expert_i[0:1, bass.ds(j, 1)], min_val=0, max_val=2 * NE - 1)
                    sp.dma_start(w13[0][:, :, :, :], dram["moe_w13"][bass.ds(e, 1)][0]).then_inc(w_arrived, 16)
                    sp.dma_start(w2[0][:, :, :], dram["moe_w2"][bass.ds(e, 1)][0]).then_inc(w_arrived, 16)

        @block.tensor
        def _(pe):
            with if_overflow(pe):
                with pe.Fori(0, NOV) as j:
                    pe.wait_ge(sel_steps, 4 * j + 4)
                    gather(pe, 0, None, None)
                    pe.wait_ge(w_arrived, 32 * (j + 1))
                    pe.wait_ge(xe_ready, 2 * (j + 1))
                    gate_up(pe, 0)
                    turn(pe, turn_ps[3], sel_w[0][:, :, :].rearrange("p t s -> p (t s)"), sel_turned)
                    pe.wait_ge(hid_ready, j + 1)
                    turn(pe, turn_ps[0], hid, hid_turned)
                    pe.wait_ge(hidT_ready, j + 1)
                    down(pe, 0, 0)
                    down(pe, 1, 0)
                    pe.wait_ge(y_ready, 2 * (j + 1))
                    pe.wait_ge(selT_ready, j + 1)
                    for o in range(8):
                        if o >= 4:
                            pe.wait_ge(x_added, 8 * j + o - 3)
                        scatter(pe, o, turn_ps[(o + 1) % 4], 0)

        @block.scalar
        def _(act):
            with if_overflow(act):
                with act.Fori(0, NOV) as j:
                    take_gathered(act, 0, j)
                    act.wait_ge(up_done, 2 * j + 1)
                    act.activation(silu_gate[:, :], up_ps[0][:, :], ACT.Silu).then_inc(silu_done, 1)
                    act.wait_ge(sel_turned, j + 1)
                    act.activation(sel_wT[0][:, :], turn_ps[3][:, :], ACT.Copy).then_inc(selT_ready, 1)
                    act.wait_ge(hid_turned, j + 1)
                    act.activation(hidT[:, :, :].rearrange("p f s -> p (f s)"), turn_ps[0][:, :], ACT.Copy).then_inc(hidT_ready, 1)

        @block.vector
        def _(dve):
            with if_overflow(dve):
                dve.sem_inc(block_gone, 1)
                with dve.Fori(0, NOV) as j:
                    dve.tensor_tensor(equal[:, :, :], slot_no.unsqueeze(1).broadcast_to([P, 2 * TT, P]),
                                      slot_of[:, :, :].rearrange("p a t -> p (a t)").unsqueeze(2).broadcast_to([P, 2 * TT, P]),
                                      ALU.is_equal).then_inc(sel_steps, 1)
                    dve.wait_ge(sel_steps, 4 * j + 1)
                    dve.tensor_tensor(sel[0][:, :, :], equal[:, 0:TT, :], equal[:, TT:2 * TT, :], ALU.add).then_inc(sel_steps, 1)
                    dve.wait_ge(sel_steps, 4 * j + 2)
                    dve.tensor_tensor(equal[:, :, :], equal[:, :, :],
                                      weight[:, :, :].rearrange("p a t -> p (a t)").unsqueeze(2).broadcast_to([P, 2 * TT, P]),
                                      ALU.mult).then_inc(sel_steps, 1)
                    dve.wait_ge(sel_steps, 4 * j + 3)
                    dve.tensor_tensor(sel_w[0][:, :, :], equal[:, 0:TT, :], equal[:, TT:2 * TT, :], ALU.add).then_inc(sel_steps, 1)
                    dve.wait_ge(silu_done, j + 1)
                    dve.wait_ge(up_done, 2 * j + 2)
                    dve.tensor_tensor(hid[:, :], silu_gate[:, :], up_ps[1][:, :], ALU.mult).then_inc(hid_ready, 1)
                    for half in range(2):
                        dve.wait_ge(down_done, 2 * j + half + 1)
                        cols = slice(half * 512, (half + 1) * 512)
                        dve.tensor_tensor(y[0][:, cols], turn_ps[1 + half][:, :], gate_row[:, cols], ALU.mult).then_inc(y_ready, 1)
                    for o in range(8):
                        dve.wait_ge(scattered, 8 * j + o + 1)
                        add_to_x(dve, o, turn_ps[(o + 1) % 4])
                    dve.wait_ge(x_added, 8 * j + 8)
                    dve.tensor_scalar(slot_of[:, :, :], slot_of[:, :, :], -float(P), None, ALU.add).then_inc(block_gone, 1)
                    dve.wait_ge(block_gone, j + 2)


def final_norm(chip):
    with Scope(chip.nc, "final_norm") as s:
        row = s.sb("row", [P, DM])
        scratch = s.sb("scratch", [P, TT, DM])
        stat = s.sb("stat", [P, 4, TT])
        row_loaded, squared, var_ready, rstd_ready = s.sem("row_loaded"), s.sem("squared"), s.sem("var_ready"), s.sem("rstd_ready")
        block = s.block()

        @block.sync
        def _(sp):
            sp.dma_start(row[:, :], chip.dram["final_row"]).then_inc(row_loaded, 16)

        @block.scalar
        def _(act):
            for t in range(TT):
                act.activation(scratch[:, t, :], chip.x[:, t, :], ACT.Square, accum_out=stat[:, 0, t:t + 1])\
                    .then_inc(squared, 1)
            act.wait_ge(var_ready, 2)
            act.activation(stat[:, 3, :], stat[:, 2, :], ACT.Sqrt).then_inc(rstd_ready, 1)

        @block.vector
        def _(dve):
            dve.wait_ge(squared, TT)
            dve.tensor_scalar(stat[:, 1, :], stat[:, 0, :], 1.0 / DM, EPS, ALU.mult, ALU.add).then_inc(var_ready, 1)
            dve.wait_ge(var_ready, 1)
            dve.reciprocal(stat[:, 2, :], stat[:, 1, :]).then_inc(var_ready, 1)
            dve.wait_ge(row_loaded, 16)
            dve.wait_ge(rstd_ready, 1)
            for t in range(TT):
                dve.scalar_tensor_tensor(out=chip.x[:, t, :], in0=chip.x[:, t, :], scalar=stat[:, 3, t:t + 1],
                                         in1=row[:, :], op0=ALU.mult, op1=ALU.mult)


def store(chip, out):
    with Scope(chip.nc, "store") as s:
        stored = chip.stored
        block = s.block()

        @block.sync
        def _(sp):
            sp.dma_start(out[0].rearrange("(t p) d -> p t d", p=P), chip.x[:, :, :]).then_inc(stored, 16)
            sp.wait_ge(stored, 16)


def program(nc, dram, out):
    with ExitStack() as ctx:
        chip = Chip(nc, ctx, dram)
        start(chip)
        for l in range(2):
            ffn(chip, f"ffn1_{l}", l, chip.gain("ffn1_norm", l))
            mixer(chip, f"mixer_{l}", l, 0.8 - 0.6 * math.exp(-0.3 * l))
            ffn(chip, f"ffn2_{l}", 2 + l, chip.gain("ffn2_norm", l))
        final_norm(chip)
        nsa(chip)
        moe(chip, "moe_0", 0)
        hgrn(chip)
        moe(chip, "moe_1", 1)
        store(chip, out)



def constants():
    import numpy as np
    t = np.arange(SEQ)
    near = np.zeros((4, SEQ, SEQ))
    for g, w in enumerate((2, 4, 8, 16)):
        lo, hi = np.maximum(t - w // 2, 0), np.minimum(t + w - w // 2, SEQ)
        inside = (t[:, None] >= lo[None, :]) & (t[:, None] < hi[None, :])
        near[g] = inside / (hi - lo)[None, :] - np.eye(SEQ)
    near = near.reshape(2, 2, TT, P, SEQ).transpose(0, 3, 1, 2, 4).reshape(2, P, 4096)
    turn = 2 * np.pi * (np.outer(t, t) % SEQ) / SEQ
    dft = np.stack([np.cos(turn), np.sin(turn)]) / math.sqrt(SEQ)
    dft = dft.reshape(2, TT, P, SEQ).transpose(2, 0, 1, 3).reshape(1, P, 4096)
    c = np.arange(64)
    turn = 2 * np.pi * (np.outer(c, c) % 64) / 64
    chan = np.zeros((P, 2, P))
    for i in range(2):
        chan[64 * i:64 * i + 64, 0, 64 * i:64 * i + 64] = np.cos(turn) / 8
        chan[64 * i:64 * i + 64, 1, 64 * i:64 * i + 64] = -np.sin(turn) / 8
    gap = np.abs(np.arange(P)[:, None] + 384 - np.arange(STRIP)[None, :])
    slopes = 2.0 ** (-8.0 * (np.arange(HEADS) + 1) / HEADS)
    alibi = -slopes[None, :, None] * gap[:, None, :]
    at = np.arange(P)
    masks = np.zeros((P, len(LEVELS), P), np.int32)
    masks[:, 0] = np.eye(P)
    for l, b in enumerate(LEVELS[1:]):
        same = at[:, None] // (2 * b) == at[None, :] // (2 * b)
        masks[:, l + 1] = same & (at[:, None] // b % 2 == 0) & (at[None, :] // b % 2 == 1)
    keep = np.broadcast_to((np.arange(SEQ) % P != 0).astype(np.float32), (P, SEQ))
    moe = np.zeros((P, 512))
    moe[:, 0:P] = at[:, None] < at[None, :]
    moe[:, P:2 * P] = at
    moe[:, 256:272], moe[:, 272:288], moe[:, 288:288 + NOV] = P * np.arange(NE), np.arange(NE), np.arange(NOV)
    f = np.float32
    return {"moe_const": moe.astype(f), "hgrn_masks": masks, "hgrn_keep": keep, "nsa_buckets": distance_buckets(), "mix_const": np.concatenate([near, dft]).astype(f), "chan_dft": chan.astype(f), "alibi": alibi.astype(f)}


def distance_buckets():
    import numpy as np
    dist = 511 - np.arange(640)
    nf = np.maximum(dist, 1).astype(np.float32)
    large = 16 + (np.log(nf / np.float32(16)) / np.float32(math.log(64)) * np.float32(16)).astype(np.int32)
    bucket = np.where(dist < 16, dist, np.minimum(large, 31))
    bucket = np.where(dist < 0, 32, bucket)
    return (bucket[None, :] == np.arange(64)[:, None]).astype(np.float32)


def nsa_layouts(inp):
    import numpy as np
    w = inp["nsa_w_in_2"][0]
    heads = [8 * (m // 4) + 4 * half + m % 4 for m in range(KT) for half in range(2)]
    q = w[:, 0:1024].reshape(DM, NH, HD)[:, heads].reshape(DM, 1024)
    kc, vc, ks, vs, kw, vw = (w[:, 1024 + 256 * i:1280 + 256 * i] for i in range(6))
    groups = column_groups(np.concatenate([q, ks, kw, vs, vw, kc, vc], 1))
    gates = w[:, 2560:].reshape(KT, P, 3 * NH).transpose(1, 0, 2)
    small = np.concatenate([inp["nsa_cmp_pe_2"][0].transpose(2, 0, 1).reshape(64, 64),
                            inp["nsa_cmp_w2_2"][0].transpose(1, 0, 2).reshape(64, 128)], 1)
    return np.concatenate([groups, column_groups(inp["nsa_w_out_2"][0])]), gates, small


def column_groups(w):
    return w.reshape(KT, P, -1, 512).transpose(2, 1, 0, 3).reshape(-1, P, 4096)


def chunked(w_gate, w_up, w_down):
    import numpy as np
    n, d, f = w_gate.shape
    c = f // FC
    gu = np.stack([w_gate, w_up], 1).reshape(n, 2, KT, P, c, FC).transpose(0, 4, 3, 1, 2, 5)
    down = w_down.reshape(n, c, 2, P, DM).transpose(0, 1, 3, 2, 4)
    return gu.reshape(n * c, P, 2, KT, FC), down.reshape(n * c, P, 2, DM)


def layouts(inp):
    import numpy as np
    d = {}
    d["x"] = inp["x"][0].reshape(TT, P, DM).transpose(1, 0, 2)
    cols = []
    for name, width in COLS:
        a = np.broadcast_to(inp[name], inp[name].shape).reshape(-1, width)
        if width >= P:
            a = a.reshape(-1, P)
        elif width == 64:
            a = np.concatenate([a, a], 1)
        cols.append(a.T)
    d["cols"] = np.concatenate(cols, 1)
    gs = [chunked(inp[f"ffn{i}_w_gate"], inp[f"ffn{i}_w_up"], inp[f"ffn{i}_w_down"]) for i in (1, 2)]
    d["ffn_gate_up"] = np.concatenate([g for g, _ in gs])
    d["ffn_down"] = np.concatenate([w for _, w in gs])
    d["mix_w"] = np.stack([np.concatenate([column_groups(inp["w_in"][l]), column_groups(inp["w_out"][l])]) for l in range(2)])
    small = np.zeros((2, P, 1024), np.float32)
    for g in range(4):
        half = 64 * (g % 2)
        small[:, half:half + 64, P * (g // 2) + half:P * (g // 2) + half + 64] = inp["pool_w"][:, g]
    small[:, :, 256:768] = inp["fourier_w"].reshape(2, 2, P, 256).transpose(0, 2, 1, 3).reshape(2, P, 512)
    for i, lam_name in enumerate(("lam_q1", "lam_k1", "lam_q2", "lam_k2")):
        small[:, :, 768 + 64 * i:832 + 64 * i] = inp[lam_name][:, None, :]
    d["mix_small"] = small
    d["ada_w"] = inp["ada_w_2"].reshape(4 * KT, P, 3 * DM)
    d["final_row"] = np.broadcast_to(inp["final_norm"], (P, DM))
    d["nsa_w"], d["nsa_w_gates"], d["nsa_small"] = nsa_layouts(inp)
    d["nsa_cmp_w1"] = np.zeros((P, 4096), np.float32)
    d["nsa_cmp_w1"][0:64] = inp["nsa_cmp_w1_2"][0].reshape(2, 32, 64, 64).transpose(2, 0, 1, 3).reshape(64, 4096)
    d["nsa_table"] = np.zeros((64, NH), np.float32)
    d["nsa_table"][0:32] = inp["rel_bias_2"]
    d["nsa_table"][32] = MASKED
    w = inp["hgrn_w_in_2"][0]
    fq = np.concatenate([w[:, c:c + P] for m in range(HG) for c in (1024 + P * m, P * m)], 1)
    d["hgrn_w"] = np.concatenate([column_groups(np.concatenate([fq, w[:, 2048:]], 1)),
                                  column_groups(inp["hgrn_w_out_2"][0])])
    router = np.concatenate([inp["moe_router_group_2"], inp["moe_router_expert_2"]], 2)
    d["moe_router"] = router.reshape(2, KT, P, NEG + NE).transpose(0, 2, 1, 3)
    w13 = np.stack([inp["moe_w1_2"], inp["moe_w3_2"]], 2).reshape(2 * NE, 2, KT, P, FF)
    d["moe_w13"] = w13.transpose(0, 3, 1, 2, 4)
    d["moe_w2"] = inp["moe_w2_2"].reshape(2 * NE, TT, P, DM).transpose(0, 2, 1, 3)
    d.update(constants())
    return d


def kernel(**inputs):
    import numpy as np
    import concourse.bacc as bacc
    from concourse.bass_utils import run_bass_kernel_spmd

    nc = bacc.Bacc("TRN2", target_bir_lowering=False, num_devices=1)
    arrays, dram = {}, {}
    for name, a in layouts({k: np.asarray(v) for k, v in inputs.items()}).items():
        a = np.ascontiguousarray(a)
        arrays[f"in_{name}"] = a
        dram[name] = nc.dram_tensor(f"in_{name}", a.shape, mybir.dt.from_np(a.dtype), kind="ExternalInput").ap()
    dram["bias_rows"] = nc.dram_tensor("bias_rows", (NH, 640), FP32, kind="Internal").ap()
    dram["bias_copies"] = nc.dram_tensor("bias_copies", (P, NH * 640), FP32, kind="Internal").ap()
    out = nc.dram_tensor("out_x", (1, SEQ, DM), FP32, kind="ExternalOutput").ap()
    program(nc, dram, out)
    r = run_bass_kernel_spmd(nc, [arrays], core_ids=[0])
    return r.results[0]["out_x"]
```

```python
import concourse.bass as bass
from concourse import mybir
from contextlib import ExitStack
import math

FP32 = mybir.dt.float32
I32 = mybir.dt.int32
F32R = mybir.dt.float32r
ALU = mybir.AluOpType
ACT = mybir.ActivationFunctionType
AXX = mybir.AxisListType.X

SEQ, DM, DFF, EPS = 512, 1024, 2816, 1e-6
P = 128
TT = SEQ // P
KT = DM // P


COLS = [("ffn1_norm", 1024), ("mix_norm", 1024), ("ffn2_norm", 1024), ("pool_scale", 256),
        ("attn_head_norm", 512), ("c_2", 1024), ("ada_b_2", 3072), ("norm_g_2", 1024),
        ("nsa_q_gain_2", 64), ("nsa_k_gain_2", 64), ("hgrn_lower_bounds_2", 1024), ("hgrn_out_gain_2", 128)]
COUNT = {"ffn1_norm": 2, "mix_norm": 2, "ffn2_norm": 2, "pool_scale": 2, "attn_head_norm": 2, "c_2": 1,
         "ada_b_2": 4, "norm_g_2": 4, "nsa_q_gain_2": 1, "nsa_k_gain_2": 3, "hgrn_lower_bounds_2": 2, "hgrn_out_gain_2": 1}
AT, NCOLS = {}, 0
for _name, _width in COLS:
    AT[_name] = (NCOLS, max(_width // P, 1))
    NCOLS += COUNT[_name] * AT[_name][1]


class Chip:

    def __init__(self, nc, ctx, dram):
        self.nc, self.dram = nc, dram
        self.x = ctx.enter_context(nc.sbuf_tensor("x_tok", [P, TT, DM], FP32))
        self.ident = ctx.enter_context(nc.sbuf_tensor("ident", [P, P], FP32))
        self.ones = ctx.enter_context(nc.sbuf_tensor("ones", [P, P], FP32))
        self.cols = ctx.enter_context(nc.sbuf_tensor("cols", [P, NCOLS], FP32))

        self.cond = ctx.enter_context(nc.sbuf_tensor("cond", [P, KT], FP32))
        self.mod = ctx.enter_context(nc.sbuf_tensor("mod", [P, 4, 3, KT], FP32))
        self.mod_gain = ctx.enter_context(nc.sbuf_tensor("mod_gain", [P, 4, KT], FP32))
        self.stored = ctx.enter_context(nc.semaphore("stored"))

    def gain(self, name, i):
        at, n = AT[name]
        return self.cols[:, at + i * n:at + (i + 1) * n]


class Scope:

    def __init__(self, nc, stage):
        self.nc, self.stage, self.sems = nc, stage, []

    def __enter__(self):
        self.ctx = ExitStack()
        self.block_ctx = ExitStack()
        return self

    def sb(self, name, shape, dt=FP32):
        return self.ctx.enter_context(self.nc.sbuf_tensor(f"{self.stage}_{name}", shape, dt))

    def ps(self, name, shape):
        return self.ctx.enter_context(self.nc.psum_tensor(f"{self.stage}_{name}", shape, FP32))

    def short_lived(self, name, shape, dt=FP32):
        with self.nc.sbuf_tensor(f"{self.stage}_{name}", shape, dt) as buffer:
            return buffer

    def sem(self, name):
        self.sems.append(self.nc.alloc_semaphore(f"{self.stage}_{name}"))
        return self.sems[-1]

    def block(self, name=""):
        self.block_ctx.close()
        return self.block_ctx.enter_context(self.nc.Block(self.stage + name))

    def __exit__(self, *what):
        self.block_ctx.__exit__(*what)
        self.ctx.__exit__(*what)
        if what[0] is None:
            self.nc.clear_and_free_semaphores(self.sems)
            self.nc.all_engine_barrier()


class Norm:

    def __init__(self, chip, s, banks, hT=None, xn=None):
        self.chip, self.nc, self.banks = chip, chip.nc, banks
        own = hT is None
        if own:
            hT, xn = s.sb("hT", [P, KT * SEQ])[:, :], s.sb("xn", [P, TT * DM])[:, :]
        self.hT = hT.rearrange("p (k t) -> p k t", k=KT)
        self.xn = xn.rearrange("p (t d) -> p t d", t=TT)
        if own:
            self.allocate(s)

    def allocate(self, s):
        self.ssq = s.sb("ssq", [P, TT])
        self.var = s.sb("var", [P, TT])
        self.rvar = s.sb("rvar", [P, TT])
        self.rstd = s.sb("rstd", [P, TT])
        self.squared = [s.sem("squared_by_scalar"), s.sem("squared_by_vector")]
        self.var_ready = s.sem("var_ready")
        self.rstd_ready = s.sem("rstd_ready")
        self.xn_ready = [s.sem("xn_ready_by_scalar"), s.sem("xn_ready_by_vector")]
        self.turned = s.sem("turned")
        self.hT_ready = [s.sem("hT_ready_by_scalar"), s.sem("hT_ready_by_vector")]

    def scalar_stats(self, act):
        act.activation(self.rstd[:, :], self.chip.ones[:, 0:TT], ACT.Sqrt)
        act.activation(self.xn[:, 0, :], self.chip.x[:, 0, :], ACT.Square, accum_out=self.ssq[:, 0:1])\
            .then_inc(self.squared[0], 1)
        act.wait_ge(self.var_ready, 2)
        act.activation(self.rstd[:, :], self.rvar[:, :], ACT.Sqrt).then_inc(self.rstd_ready, 1)
        act.wait_ge(self.rstd_ready, 1)
        act.activation(self.xn[:, TT - 1, :], self.chip.x[:, TT - 1, :], ACT.Copy, scale=self.rstd[:, TT - 1:TT])\
            .then_inc(self.xn_ready[0], 1)

    def scalar_evacuate(self, act, gain, shift=None):
        for k in range(0, KT, 2):
            act.wait_ge(self.turned, k + 1)
            if shift is None:
                act.activation(self.hT[:, k, :], self.banks[k % 4][:, :], ACT.Copy,
                               scale=gain[:, k:k + 1]).then_inc(self.hT_ready[0], 1)
            else:
                act.activation(self.hT[:, k, :], self.banks[k % 4][:, :], ACT.Identity,
                               scale=gain[:, k:k + 1], bias=shift[:, k:k + 1]).then_inc(self.hT_ready[0], 1)

    def vector(self, dve):
        for t in range(1, TT):
            dve.scalar_tensor_tensor(out=self.xn[:, t, :], in0=self.chip.x[:, t, :], scalar=1.0, in1=self.chip.x[:, t, :],
                                     op0=ALU.mult, op1=ALU.mult, accum_out=self.ssq[:, t:t + 1]).then_inc(self.squared[1], 1)
        dve.wait_ge(self.squared[0], 1)
        dve.wait_ge(self.squared[1], TT - 1)
        dve.tensor_scalar(self.var[:, :], self.ssq[:, :], 1.0 / DM, EPS, ALU.mult, ALU.add)\
            .then_inc(self.var_ready, 1)
        dve.wait_ge(self.var_ready, 1)
        dve.reciprocal(self.rvar[:, :], self.var[:, :]).then_inc(self.var_ready, 1)
        dve.wait_ge(self.rstd_ready, 1)
        for t in range(TT - 1):
            dve.tensor_scalar(self.xn[:, t, :], self.chip.x[:, t, :], self.rstd[:, t:t + 1], None, ALU.mult)\
                .then_inc(self.xn_ready[1], 1)

    def vector_evacuate(self, dve, gain, shift=None):
        for k in range(1, KT, 2):
            dve.wait_ge(self.turned, k + 1)
            if shift is None:
                dve.tensor_scalar(self.hT[:, k, :], self.banks[k % 4][:, :], gain[:, k:k + 1], None, ALU.mult)\
                    .then_inc(self.hT_ready[1], 1)
            else:
                dve.tensor_scalar(self.hT[:, k, :], self.banks[k % 4][:, :], gain[:, k:k + 1], shift[:, k:k + 1],
                                  ALU.mult, ALU.add).then_inc(self.hT_ready[1], 1)

    def bank_free(self, pe, k):
        pe.wait_ge(self.hT_ready[k % 2], k // 2 + 1)

    def complete(self, pe):
        pe.wait_ge(self.hT_ready[0], KT // 2)
        pe.wait_ge(self.hT_ready[1], KT // 2)

    def tensor(self, pe):
        for k in range(KT):
            if k >= 4:
                self.bank_free(pe, k - 4)
            for t in range(TT):
                if k == 0:
                    if t == TT - 1:
                        pe.wait_ge(self.xn_ready[0], 1)
                    else:
                        pe.wait_ge(self.xn_ready[1], t + 1)
                last = pe.transpose(self.banks[k % 4][:, t * P:(t + 1) * P],
                                    self.xn[:, t, k * P:(k + 1) * P], self.chip.ident[:, :])
            last.then_inc(self.turned, 1)



def split_matmul(pe, out, lhsT, rhs, first, last):
    pe.matmul(out, lhsT[0], rhs[0], start=first, stop=False)
    pe.matmul(out, lhsT[0], rhs[1], start=False, stop=False)
    return pe.matmul(out, lhsT[1], rhs[0], start=False, stop=last)


class SplitNorm(Norm):

    def __init__(self, chip, s, banks):
        self.chip, self.nc, self.banks = chip, chip.nc, banks
        self.xn = s.short_lived("xn", [P, TT, DM])

    def allocate(self, s):
        super().allocate(s)
        self.high = s.sb("h_high", [P, KT, SEQ], F32R)
        self.low = s.sb("h_low", [P, KT, SEQ], F32R)
        self.high_ready, self.low_ready = s.sem("h_high_ready"), s.sem("h_low_ready")

    def bank_free(self, pe, k):
        pe.wait_ge(self.low_ready, k + 1)

    def complete(self, pe):
        pe.wait_ge(self.low_ready, KT)

    def scalar_evacuate(self, act, gain, shift=None):
        for k in range(KT):
            act.wait_ge(self.turned, k + 1)
            act.activation(self.high[:, k, :], self.banks[k % 4][:, :], ACT.Copy,
                           scale=gain[:, k:k + 1]).then_inc(self.high_ready, 1)

    def vector_evacuate(self, dve, gain):
        for k in range(KT):
            dve.wait_ge(self.high_ready, k + 1)
            dve.scalar_tensor_tensor(out=self.low[:, k, :], in0=self.banks[k % 4][:, :], scalar=gain[:, k:k + 1],
                                     in1=self.high[:, k, :].bitcast(FP32), op0=ALU.mult, op1=ALU.subtract)\
                .then_inc(self.low_ready, 1)


def start(chip, name="start"):
    nc = chip.nc
    with Scope(nc, name) as s:
        x_loaded, zeroed, made = s.sem("x_loaded"), s.sem("zeroed"), s.sem("made")
        block = s.block()

        @block.sync
        def _(sp):
            sp.dma_start(chip.x[:, :, :], chip.dram["x"]).then_inc(x_loaded, 16)
            sp.wait_ge(x_loaded, 16)
            sp.dma_start(chip.cols[:, :], chip.dram["cols"]).then_inc(x_loaded, 16)
            sp.wait_ge(x_loaded, 32)

        @block.scalar
        def _(act):
            act.wait_ge(x_loaded, 32)
            act.activation(chip.cond[:, :], chip.gain("c_2", 0), ACT.Silu).then_inc(made, 1)

        @block.gpsimd
        def _(pool):
            pool.memset(chip.ones[:, :], 1.0)
            pool.memset(chip.ident[:, :], 0.0).then_inc(zeroed, 1)
            pool.wait_ge(zeroed, 1)
            pool.affine_select(out=chip.ident[:, :], in_=chip.ident[:, :], compare_op=ALU.not_equal, fill=1.0,
                               base=0, pattern=[[-1, P]], channel_multiplier=1).then_inc(made, 1)


NFT = DFF // P
NCHUNK = NFT // 2


def ffn(chip, name, which, gain):
    nc = chip.nc
    ada_dram = chip.dram["ada_w"]
    gate_up_dram, down_dram = chip.dram["ffn_gate_up"], chip.dram["ffn_down"]
    base = which * NFT
    with Scope(nc, name) as s:
        gate_up_ps = [s.ps(f"gate_up{i}", [P, SEQ]) for i in range(4)]
        down_ps = [s.ps(f"down{i}", [P, SEQ]) for i in range(4)]
        norm = SplitNorm(chip, s, down_ps)
        hid_high = [s.sb(f"hid_high{i}", [P, SEQ], F32R) for i in range(4)]
        hid_low = [s.sb(f"hid_low{i}", [P, SEQ], F32R) for i in range(4)]
        norm.allocate(s)
        raw_gu = [s.sb(f"raw_gate_up{i}", [P, 2, KT, P]) for i in range(2)]
        raw_d = [s.sb(f"raw_down{i}", [P, DM]) for i in range(2)]
        gu_high = [s.sb(f"gate_up_high{i}", [P, 2, KT, P], F32R) for i in range(2)]
        gu_low = [s.sb(f"gate_up_low{i}", [P, 2, KT, P], F32R) for i in range(2)]
        d_high = [s.sb(f"down_high{i}", [P, DM], F32R) for i in range(4)]
        d_low = [s.sb(f"down_low{i}", [P, DM], F32R) for i in range(4)]
        silu_gate = [s.sb(f"silu_gate{i}", [P, SEQ]) for i in range(2)]
        product = [s.sb(f"product{i}", [P, SEQ]) for i in range(2)]
        gu_loaded = [s.sem(f"gate_up_loaded{i}") for i in range(2)]
        d_loaded = [s.sem(f"down_loaded{i}") for i in range(2)]
        gu_high_ready, gu_ready = s.sem("gate_up_high_ready"), s.sem("gate_up_split")
        d_high_ready, d_ready = s.sem("down_high_ready"), s.sem("down_split")
        gate_up_done, silu_done, product_ready = s.sem("gate_up_done"), s.sem("silu_done"), s.sem("product_ready")
        hid_high_ready, hid_ready = s.sem("hid_high_ready"), s.sem("hid_split")
        down_done, x_added = s.sem("down_done"), s.sem("x_added")
        ada_w = [s.sb(f"ada_w{i}", [P, 3 * DM]) for i in range(2)]
        ada_acc = s.sb("ada_acc", [P, 3 * DM])
        ada_loaded = [s.sem(f"ada_loaded{i}") for i in range(2)]
        ada_added, ada_summed, mod_ready = s.sem("ada_added"), s.sem("ada_summed"), s.sem("mod_ready")
        block = s.block()

        @block.sync
        def _(sp):
            def load(n, slot, again):
                if again:
                    sp.wait_ge(gu_ready, n - 1)
                sp.dma_start(raw_gu[slot][:, :, :, :], gate_up_dram[base + n]).then_inc(gu_loaded[slot], 16)
                if again:
                    sp.wait_ge(d_ready, n - 1)
                sp.dma_start(raw_d[slot][:, :], down_dram[base + n]).then_inc(d_loaded[slot], 16)

            def load_ada(k, slot, again):
                if again:
                    sp.wait_ge(ada_added, k - 1)
                sp.dma_start(ada_w[slot][:, :], ada_dram[which * KT + k]).then_inc(ada_loaded[slot], 16)

            load(0, 0, False)
            load(1, 1, False)
            load_ada(0, 0, False)
            load_ada(1, 1, False)
            load(2, 0, True)
            load(3, 1, True)
            with sp.Fori(1, KT // 2) as i:
                load(4 * i, 0, True)
                load(4 * i + 1, 1, True)
                load_ada(2 * i, 0, True)
                load(4 * i + 2, 0, True)
                load(4 * i + 3, 1, True)
                load_ada(2 * i + 1, 1, True)
            with sp.Fori(2 * KT, NFT - 1, 2) as n:
                load(n, 0, True)
                load(n + 1, 1, True)

        @block.tensor
        def _(pe):
            norm.tensor(pe)
            norm.complete(pe)

            def gate_up(n, slot, again=True):
                pe.wait_ge(gu_ready, n + 1)
                if again:
                    pe.wait_ge(product_ready, n - 1)
                for m in range(2):
                    for k in range(KT):
                        last = split_matmul(pe, gate_up_ps[2 * slot + m][:, :],
                                            (gu_high[slot][:, m, k, :], gu_low[slot][:, m, k, :]),
                                            (norm.high[:, k, :], norm.low[:, k, :]), k == 0, k == KT - 1)
                last.then_inc(gate_up_done, 1)

            def down(c, slots, again=True):
                pe.wait_ge(d_ready, 2 * (c + 1))
                pe.wait_ge(hid_ready, 2 * (c + 1))
                for o in range(8):
                    if again or o >= 4:
                        pe.wait_ge(x_added, 8 * c + o - 3)
                    t, half = o // 2, o % 2
                    tokens, cols = slice(t * P, (t + 1) * P), slice(half * 512, (half + 1) * 512)
                    for i, f in enumerate(slots):
                        last = split_matmul(pe, down_ps[o % 4][:, :], (hid_high[f][:, tokens], hid_low[f][:, tokens]),
                                            (d_high[f][:, cols], d_low[f][:, cols]), i == 0, i == 1)
                    last.then_inc(down_done, 1)

            gate_up(0, 0, False)
            gate_up(1, 1, False)
            gate_up(2, 0)
            gate_up(3, 1)
            down(0, (0, 1), False)
            gate_up(4, 0)
            gate_up(5, 1)
            down(1, (2, 3))
            with pe.Fori(1, NCHUNK // 2) as i:
                gate_up(4 * i + 2, 0)
                gate_up(4 * i + 3, 1)
                down(2 * i, (0, 1))
                gate_up(4 * i + 4, 0)
                gate_up(4 * i + 5, 1)
                down(2 * i + 1, (2, 3))
            pe.wait_ge(ada_added, KT)
            pe.wait_ge(product_ready, NFT)
            for j in range(3 * KT):
                last = pe.matmul(gate_up_ps[0][:, j:j + 1], ada_acc[:, j * P:(j + 1) * P], chip.ones[:, 0:1],
                                 start=True, stop=True)
            last.then_inc(ada_summed, 1)
            down(NCHUNK - 1, (0, 1))

        @block.scalar
        def _(act):
            def split_gate_up(n, slot, again=True):
                act.wait_ge(gu_loaded[slot], 8 * (n - slot) + 16)
                if again:
                    act.wait_ge(gate_up_done, n - 1)
                act.activation(gu_high[slot][:, :, :, :], raw_gu[slot][:, :, :, :], ACT.Copy).then_inc(gu_high_ready, 1)

            norm.scalar_stats(act)
            split_gate_up(0, 0, False)
            norm.scalar_evacuate(act, gain)
            split_gate_up(1, 1, False)

            def step(m, f, more=True):
                slot = f % 2
                act.wait_ge(gate_up_done, m + 1)
                act.activation(silu_gate[slot][:, :], gate_up_ps[2 * slot][:, :], ACT.Silu).then_inc(silu_done, 1)
                if more:
                    split_gate_up(m + 2, slot)
                act.wait_ge(d_loaded[slot], 8 * (m - slot) + 16)
                act.activation(d_high[f][:, :], raw_d[slot][:, :], ACT.Copy).then_inc(d_high_ready, 1)
                act.wait_ge(product_ready, m + 1)
                act.activation(hid_high[f][:, :], product[slot][:, :], ACT.Copy).then_inc(hid_high_ready, 1)

            with act.Fori(0, NCHUNK // 2) as i:
                for f in range(4):
                    step(4 * i + f, f)
            step(NFT - 2, 0, False)
            step(NFT - 1, 1, False)

        @block.vector
        def _(dve):
            def split_gate_up(n, slot):
                dve.wait_ge(gu_high_ready, n + 1)
                dve.tensor_tensor(gu_low[slot][:, :, :, :], raw_gu[slot][:, :, :, :], gu_high[slot][:, :, :, :].bitcast(FP32),
                                  ALU.subtract).then_inc(gu_ready, 1)

            norm.vector(dve)
            split_gate_up(0, 0)
            norm.vector_evacuate(dve, gain)
            split_gate_up(1, 1)

            def step(m, f, more=True, add=()):
                slot = f % 2
                dve.wait_ge(silu_done, m + 1)
                dve.tensor_tensor(product[slot][:, :], silu_gate[slot][:, :], gate_up_ps[2 * slot + 1][:, :], ALU.mult)\
                    .then_inc(product_ready, 1)
                add_some(0, 2, *add)
                if more:
                    split_gate_up(m + 2, slot)
                add_some(2, 4, *add)
                dve.wait_ge(d_high_ready, m + 1)
                dve.tensor_tensor(d_low[f][:, :], raw_d[slot][:, :], d_high[f][:, :].bitcast(FP32), ALU.subtract)\
                    .then_inc(d_ready, 1)
                dve.wait_ge(hid_high_ready, m + 1)
                dve.tensor_tensor(hid_low[f][:, :], product[slot][:, :], hid_high[f][:, :].bitcast(FP32), ALU.subtract)\
                    .then_inc(hid_ready, 1)
                add_some(4, 8, *add)

            def add_some(first, last, c=None, again=True):
                if c is None:
                    return
                for o in range(first, last):
                    t, half = o // 2, o % 2
                    xs = chip.x[:, t, half * 512:(half + 1) * 512]
                    dve.wait_ge(down_done, 8 * c + o + 1)
                    if again:
                        dve.wait_ge(x_added, 8 * c + o - 7)
                    dve.scalar_tensor_tensor(out=xs, in0=down_ps[o % 4][:, :], scalar=0.5, in1=xs,
                                             op0=ALU.mult, op1=ALU.add).then_inc(x_added, 1)

            def add_ada(k, slot, n, again=True):
                dve.wait_ge(ada_loaded[slot], 16 * (n + 1))
                if again:
                    dve.wait_ge(ada_added, k)
                    dve.scalar_tensor_tensor(out=ada_acc[:, :], in0=ada_w[slot][:, :],
                                             scalar=chip.cond[:, bass.ds(k, 1)], in1=ada_acc[:, :],
                                             op0=ALU.mult, op1=ALU.add).then_inc(ada_added, 1)
                else:
                    dve.tensor_scalar(ada_acc[:, :], ada_w[slot][:, :], chip.cond[:, 0:1], None, ALU.mult)\
                        .then_inc(ada_added, 1)

            step(0, 0)
            step(1, 1)
            add_ada(0, 0, 0, False)
            step(2, 2)
            step(3, 3, add=(0, False))
            add_ada(1, 1, 0)
            with dve.Fori(1, KT // 2) as i:
                step(4 * i, 0)
                step(4 * i + 1, 1, add=(2 * i - 1,))
                add_ada(2 * i, 0, i)
                step(4 * i + 2, 2)
                step(4 * i + 3, 3, add=(2 * i,))
                add_ada(2 * i + 1, 1, i)
            with dve.Fori(KT // 2, NCHUNK // 2) as i:
                step(4 * i, 0)
                step(4 * i + 1, 1, add=(2 * i - 1,))
                step(4 * i + 2, 2)
                step(4 * i + 3, 3, add=(2 * i,))
            step(NFT - 2, 0, False)
            step(NFT - 1, 1, False, add=(NCHUNK - 2,))
            dve.wait_ge(ada_summed, 1)
            mod = chip.mod[:, which, :, :]
            bias = chip.gain("ada_b_2", which).rearrange("p (a k) -> p a k", a=3)
            dve.tensor_tensor(mod, gate_up_ps[0][:, 0:3 * KT].rearrange("p (a k) -> p a k", a=3), bias, ALU.add)\
                .then_inc(mod_ready, 1)
            dve.wait_ge(mod_ready, 1)
            dve.scalar_tensor_tensor(out=chip.mod_gain[:, which, :], in0=mod[:, 1, :], scalar=1.0,
                                     in1=chip.gain("norm_g_2", which), op0=ALU.add, op1=ALU.mult)\
                .then_inc(mod_ready, 1)
            add_some(0, 8, NCHUNK - 1)
            dve.wait_ge(mod_ready, 2)


class Banks:

    def __init__(self, s, n=8):
        self.n = n
        self.ps = [s.ps(f"bank{i}", [P, 512]) for i in range(n)]
        self.computed = s.sem("computed")
        self.evacuated = [s.sem("evacuated_by_scalar"), s.sem("evacuated_by_vector")]

    def open(self, pe, o):
        if o >= self.n:
            pe.wait_ge(self.evacuated[o % 2], (o - self.n) // 2 + 1)
        return self.ps[o % self.n]

    def take(self, eng, o):
        eng.wait_ge(self.computed, o + 1)
        return self.ps[o % self.n]

    def wait_for(self, eng, o):
        eng.wait_ge(self.evacuated[o % 2], o // 2 + 1)


def piece(dst, cols=(0, 512), scale=None, rows=(0, P), func=None, bias=None):
    return dst, rows, cols, scale, func, bias


def evacuate(banks, eng, parity, outputs, first=0, last=None):
    for o in sorted(outputs):
        if o % 2 != parity or o < first or (last is not None and o >= last):
            continue
        bank = banks.take(eng, o)
        for dst, rows, cols, scale, func, bias in outputs[o]:
            src = bank[rows[0]:rows[1], cols[0]:cols[1]]
            if bias is not None:
                ins = eng.activation(dst, src, func, bias=bias)
            elif parity == 0:
                ins = eng.activation(dst, src, func or ACT.Copy, scale=1.0 if scale is None else scale)
            elif scale is None:
                ins = eng.tensor_copy(dst, src)
            else:
                ins = eng.tensor_scalar(dst, src, scale, None, ALU.mult)
        ins.then_inc(banks.evacuated[parity], 1)


class Ring:

    def __init__(self, s, slots, loads, computed):
        self.slots = [s.sb(f"ring{i}", [P, 4096]) for i in range(slots)]
        self.loaded = [s.sem(f"ring_loaded{i}") for i in range(slots)]
        self.loads, self.computed = loads, computed

    def fill(self, sp, first=0, last=None):
        n = len(self.slots)
        for i in range(first, len(self.loads) if last is None else last):
            src, width, _ = self.loads[i]
            if i >= n:
                sp.wait_ge(self.computed, self.loads[i - n][2])
            sp.dma_start(self.slots[i % n][:, 0:width], src).then_inc(self.loaded[i % n], 16)

    def get(self, pe, i):
        n = len(self.slots)
        pe.wait_ge(self.loaded[i % n], 16 * (i // n + 1))
        return self.slots[i % n]

    def weights(self, pe, i):
        return self.get(pe, i)[:, :].rearrange("p (k n) -> p k n", k=KT)


class Own:

    def __init__(self, eng, done):
        self.eng, self.done, self.n = eng, done, 0

    def __call__(self, ins):
        self.n += 1
        ins.then_inc(self.done, 1)
        self.eng.wait_ge(self.done, self.n)


def token_major(pe, banks, o, w, hT):
    for t in range(TT):
        bank = banks.open(pe, o + t)
        for k in range(KT):
            last = pe.matmul(bank[:, :], hT[:, k, t * P:(t + 1) * P], w[:, k, :], start=(k == 0), stop=(k == KT - 1))
        last.then_inc(banks.computed, 1)


def feature_major(pe, banks, o, w, hT, tiles=4):
    for m in range(tiles):
        bank = banks.open(pe, o + m)
        for k in range(KT):
            last = pe.matmul(bank[:, :], w[:, k, m * P:(m + 1) * P], hT[:, k, :], start=(k == 0), stop=(k == KT - 1))
        last.then_inc(banks.computed, 1)


HEADS = 4
STRIP = 896


def mixer(chip, name, layer, lam_init):
    nc, dram = chip.nc, chip.dram
    scale = 64 ** -0.5
    units = [(h, i) for h in range(HEADS) for i in range(TT)]
    U = len(units)
    with Scope(nc, name) as s:
        banks = Banks(s)
        norm = Norm(chip, s, banks.ps[0:4])
        ws = [dram["mix_w"][layer, i] for i in range(6)]
        cs = [dram["mix_const"][i] for i in range(3)]
        ring = Ring(s, 3, [(w, 4096, n) for w, n in zip(ws[0:4] + cs + ws[4:6], [4, 8, 12, 16, 17, 18, 24, 36, 40])],
                    banks.computed)
        yT = norm.xn[:, :, :].rearrange("p t d -> p (t d)").rearrange("p (k t) -> p k t", k=KT)
        spare = norm.hT[:, :, :].rearrange("p k t -> p (k t)")
        pooled = spare[:, 0:1024].rearrange("p (a t) -> p a t", a=2)
        chan = spare[:, 1024:2048].rearrange("p (a n) -> p a n", a=2)
        timed = spare[:, 2048:4096].rearrange("p (a t) -> p a t", a=4)
        af = s.sb("af", [P, TT, 512])
        qT = s.sb("qT", [P, HEADS, SEQ])
        kT = s.sb("kT", [P, HEADS, SEQ])
        v = s.sb("v", [P, TT, 512])
        small = s.sb("small", [P, 1024])
        pool_blk = small[:, 0:256].rearrange("p (a n) -> p a n", a=2)
        four_w = small[:, 256:768].rearrange("p (a n) -> p a n", a=2)
        lam_in = small[:, 768:1024].rearrange("p (a n) -> p a n", a=4)
        chan_dft = s.sb("chan_dft", [P, 2, P])
        alibi = s.sb("alibi", [P, HEADS, STRIP])
        sc = [s.sb(f"scores{i}", [P, 2, SEQ]) for i in range(2)]
        ex = [s.sb(f"exps{i}", [P, 2, SEQ]) for i in range(2)]
        mix = [s.sb(f"mixed{i}", [P, SEQ]) for i in range(2)]
        mixT = [s.sb(f"mixedT{i}", [P, TT, P]) for i in range(2)]
        o_tok = s.sb("o_tok", [P, TT, HEADS, P])
        lam = s.sb("lam", [P, 8])
        lam_prod = s.sb("lam_prod", [P, 2, 64])
        head_gain = s.sb("head_gain", [P, HEADS])
        neg_max = s.sb("neg_max", [P, U, 2])
        sums = s.sb("sums", [P, U, 2])
        rsum = s.sb("rsum", [P, U, 2])
        ratio = s.sb("ratio", [P, U])
        hss = s.sb("hss", [P, 4, U])
        small_loaded, alibi_loaded = s.sem("small_loaded"), s.sem("alibi_loaded")
        lam_dots, lam_exps = s.sem("lam_dots"), s.sem("lam_exps")
        own_v = s.sem("own_v")
        scores_done, scores_read, max_ready = s.sem("scores_done"), s.sem("scores_read"), s.sem("max_ready")
        exps_done, mixed, mix_turned = s.sem("exps_done"), s.sem("mixed"), s.sem("mix_turned")
        mixT_ready, values_done, o_ready = s.sem("mixT_ready"), s.sem("values_done"), s.sem("o_ready")
        head_var, head_rstd, o_normed = s.sem("head_var"), s.sem("head_rstd"), s.sem("o_normed")
        x_added = s.sem("x_added")
        block = s.block()

        outputs = {}
        for t in range(TT):
            outputs[t] = [piece(af[:, t, :])]
            outputs[4 + t] = [piece(qT[:, t, :])]
            outputs[8 + t] = [piece(kT[:, t, :])]
            outputs[12 + t] = [piece(v[:, t, :])]
        for a in range(2):
            outputs[16 + a] = [piece(pooled[:, a, :])]
            outputs[18 + a] = [piece(chan[:, a, :])]
            outputs[20 + a] = [piece(timed[:, a, :])]
            outputs[22 + a] = [piece(timed[:, 2 + a, :])]
            outputs[24 + a] = [piece(yT[:, a, :], scale=chip.gain("pool_scale", layer)[:, a:a + 1])]
            outputs[26 + a] = [piece(yT[:, 2 + a, :])]
        HEAD_T = 28
        OUT = 32
        late = {HEAD_T + h: [piece(yT[:, 4 + h, :], scale=head_gain[:, h:h + 1])] for h in range(HEADS)}

        @block.sync
        def _(sp):
            ring.fill(sp, 0, 1)
            sp.dma_start(small[:, :], dram["mix_small"][layer]).then_inc(small_loaded, 16)
            sp.dma_start(chan_dft[:, :, :], dram["chan_dft"]).then_inc(small_loaded, 16)
            ring.fill(sp, 1, 3)
            sp.dma_start(alibi[:, :, :], dram["alibi"]).then_inc(alibi_loaded, 16)
            ring.fill(sp, 3)

        @block.tensor
        def _(pe):
            norm.tensor(pe)
            norm.complete(pe)
            token_major(pe, banks, 0, ring.weights(pe, 0), norm.hT)
            feature_major(pe, banks, 4, ring.weights(pe, 1), norm.hT)
            feature_major(pe, banks, 8, ring.weights(pe, 2), norm.hT)
            token_major(pe, banks, 12, ring.weights(pe, 3), norm.hT)
            banks.wait_for(pe, 2)
            banks.wait_for(pe, 3)
            for a in range(2):
                near = ring.get(pe, 4 + a)[:, :].rearrange("p (g s t) -> p g s t", g=2, s=TT)
                bank = banks.open(pe, 16 + a)
                for g in range(2):
                    for t in range(TT):
                        last = pe.matmul(bank[64 * g:64 * g + 64, :], af[:, t, P * a + 64 * g:P * a + 64 * g + 64],
                                         near[:, g, t, :], start=(t == 0), stop=(t == TT - 1))
                last.then_inc(banks.computed, 1)
            pe.wait_ge(small_loaded, 32)
            for part in range(2):
                bank = banks.open(pe, 18 + part)
                for a in range(2):
                    last = pe.matmul(bank[:, 256 * a:256 * a + 256], chan_dft[:, part, :], four_w[:, a, :],
                                     start=True, stop=True)
                last.then_inc(banks.computed, 1)
            dft = ring.get(pe, 6)[:, :].rearrange("p (c s t) -> p c s t", c=2, s=TT)
            for part in range(2):
                for a in range(2):
                    bank = banks.open(pe, 20 + 2 * part + a)
                    for t in range(TT):
                        last = pe.matmul(bank[:, :], af[:, t, 256 + P * a:256 + P * a + P], dft[:, part, t, :],
                                         start=(t == 0), stop=(t == TT - 1))
                    last.then_inc(banks.computed, 1)
            banks.wait_for(pe, 16)
            banks.wait_for(pe, 17)
            for a in range(2):
                bank = banks.open(pe, 24 + a)
                pe.matmul(bank[:, :], pool_blk[:, a, :], pooled[:, a, :], start=True, stop=True)\
                    .then_inc(banks.computed, 1)
            banks.wait_for(pe, 22)
            banks.wait_for(pe, 23)
            for m in range(2):
                bank = banks.open(pe, 26 + m)
                for part in range(2):
                    for a in range(2):
                        last = pe.matmul(bank[:, :], chan[:, part, 256 * a + P * m:256 * a + P * m + P],
                                         timed[:, 2 * part + a, :], start=(part == 0 and a == 0),
                                         stop=(part == 1 and a == 1))
                last.then_inc(banks.computed, 1)
            banks.wait_for(pe, 26)
            banks.wait_for(pe, 27)
            for step in range(U + 3):
                if step < U:
                    h, i = units[step]
                    if step >= 2:
                        pe.wait_ge(scores_read, step - 1)
                    for j in range(2):
                        last = pe.matmul(banks.ps[2 * (step % 2) + j][:, :],
                                         qT[64 * j:64 * j + 64, h, i * P:(i + 1) * P], kT[64 * j:64 * j + 64, h, :],
                                         start=True, stop=True)
                    last.then_inc(scores_done, 1)
                if 2 <= step <= U + 1:
                    u = step - 2
                    pe.wait_ge(mixed, u + 1)
                    if u >= 2:
                        pe.wait_ge(mixT_ready, u - 1)
                    for b in range(TT):
                        last = pe.transpose(banks.ps[4 + u % 2][:, b * P:(b + 1) * P], mix[u % 2][:, b * P:(b + 1) * P],
                                            chip.ident[:, :])
                    last.then_inc(mix_turned, 1)
                if step >= 3:
                    u = step - 3
                    h, i = units[u]
                    pe.wait_ge(mixT_ready, u + 1)
                    if u >= 2:
                        pe.wait_ge(o_ready, u - 1)
                    for b in range(TT):
                        last = pe.matmul(banks.ps[6 + u % 2][:, 0:P], mixT[u % 2][:, b, :], v[:, b, h * P:(h + 1) * P],
                                         start=(b == 0), stop=(b == TT - 1))
                    last.then_inc(values_done, 1)
            for h in range(HEADS):
                bank = banks.open(pe, HEAD_T + h)
                for t in range(TT):
                    if h == 0:
                        pe.wait_ge(o_normed, 1)
                    last = pe.transpose(bank[:, t * P:(t + 1) * P], o_tok[:, t, h, :], chip.ident[:, :])
                last.then_inc(banks.computed, 1)
            banks.wait_for(pe, HEAD_T + 2)
            banks.wait_for(pe, HEAD_T + 3)
            token_major(pe, banks, OUT, ring.weights(pe, 7), yT)
            token_major(pe, banks, OUT + 4, ring.weights(pe, 8), yT)

        @block.scalar
        def _(act):
            norm.scalar_stats(act)
            norm.scalar_evacuate(act, chip.gain("mix_norm", layer))
            evacuate(banks, act, 0, outputs)
            act.wait_ge(lam_dots, 1)
            act.activation(lam[:, 2:4], lam[:, 0:2], ACT.Exp).then_inc(lam_exps, 1)
            for step in range(U + 3):
                if step < U:
                    u = step
                    act.wait_ge(max_ready, u + 1)
                    if u >= 2:
                        act.wait_ge(mixed, u - 1)
                    for j in range(2):
                        act.activation(ex[u % 2][:, j, :], sc[u % 2][:, j, :], ACT.Exp, bias=neg_max[:, u, j:j + 1],
                                       accum_out=sums[:, u, j:j + 1]).then_inc(exps_done, 1)
                if 2 <= step <= U + 1:
                    u = step - 2
                    act.wait_ge(mix_turned, u + 1)
                    if u >= 2:
                        act.wait_ge(values_done, u - 1)
                    act.activation(mixT[u % 2][:, :, :].rearrange("p b q -> p (b q)"), banks.ps[4 + u % 2][:, :],
                                   ACT.Copy).then_inc(mixT_ready, 1)
                if step >= 3:
                    u = step - 3
                    h, i = units[u]
                    act.wait_ge(values_done, u + 1)
                    act.activation(o_tok[:, i, h, :], banks.ps[6 + u % 2][:, 0:P], ACT.Copy,
                                   scale=rsum[:, u, 0:1]).then_inc(o_ready, 1)
            act.wait_ge(head_var, 1)
            act.activation(hss[:, 3, :], hss[:, 2, :], ACT.Sqrt).then_inc(head_rstd, 1)
            evacuate(banks, act, 0, late)

        @block.vector
        def _(dve):
            own = Own(dve, own_v)
            norm.vector(dve)
            norm.vector_evacuate(dve, chip.gain("mix_norm", layer))
            evacuate(banks, dve, 1, outputs)
            dve.wait_ge(small_loaded, 32)
            own(dve.tensor_tensor(lam_prod[:, :, :], lam_in[:, 0:4:2, :], lam_in[:, 1:4:2, :], ALU.mult))
            dve.reduce_sum(lam[:, 0:2], lam_prod[:, :, :], AXX).then_inc(lam_dots, 1)
            dve.wait_ge(lam_exps, 1)
            own(dve.tensor_tensor(lam[:, 4:5], lam[:, 3:4], lam[:, 2:3], ALU.subtract))
            own(dve.tensor_scalar(lam[:, 5:6], lam[:, 4:5], -lam_init, None, ALU.add))
            own(dve.tensor_scalar(head_gain[:, :], chip.gain("attn_head_norm", layer), 1.0 - lam_init, None, ALU.mult))
            dve.wait_ge(alibi_loaded, 16)
            for step in range(U + 1):
                if step < U:
                    u = step
                    h, i = units[u]
                    dve.wait_ge(scores_done, u + 1)
                    if u >= 2:
                        dve.wait_ge(exps_done, 2 * (u - 1))
                    c = 384 - P * i
                    for j in range(2):
                        last = dve.scalar_tensor_tensor(out=sc[u % 2][:, j, :], in0=banks.ps[2 * (u % 2) + j][:, :],
                                                        scalar=scale, in1=alibi[:, h, c:c + SEQ],
                                                        op0=ALU.mult, op1=ALU.add)
                        if j == 0:
                            own(last)
                    last.then_inc(scores_read, 1)
                    dve.wait_ge(scores_read, u + 1)
                    dve.tensor_reduce(neg_max[:, u, :], sc[u % 2][:, :, :], axis=AXX, op=ALU.max, negate=True)\
                        .then_inc(max_ready, 1)
                if step >= 1:
                    u = step - 1
                    dve.wait_ge(exps_done, 2 * (u + 1))
                    own(dve.reciprocal(rsum[:, u, :], sums[:, u, :]))
                    own(dve.scalar_tensor_tensor(out=ratio[:, u:u + 1], in0=sums[:, u, 0:1], scalar=rsum[:, u, 1:2],
                                                 in1=lam[:, 5:6], op0=ALU.mult, op1=ALU.mult))
                    if u >= 2:
                        dve.wait_ge(mix_turned, u - 1)
                    dve.scalar_tensor_tensor(out=mix[u % 2][:, :], in0=ex[u % 2][:, 1, :], scalar=ratio[:, u:u + 1],
                                             in1=ex[u % 2][:, 0, :], op0=ALU.mult, op1=ALU.add).then_inc(mixed, 1)
            dve.wait_ge(o_ready, U)
            flat = o_tok[:, :, :, :].rearrange("p t h e -> p (t h) e")
            squares = spare[:, 0:2048].rearrange("p (u e) -> p u e", u=U)
            own(dve.tensor_tensor(squares, flat, flat, ALU.mult))
            own(dve.reduce_sum(hss[:, 0, :], squares, AXX))
            own(dve.tensor_scalar(hss[:, 1, :], hss[:, 0, :], 1.0 / P, EPS, ALU.mult, ALU.add))
            dve.reciprocal(hss[:, 2, :], hss[:, 1, :]).then_inc(head_var, 1)
            dve.wait_ge(head_rstd, 1)
            dve.tensor_tensor(flat, flat, hss[:, 3, :].unsqueeze(2).broadcast_to([P, U, P]), ALU.mult)\
                .then_inc(o_normed, 1)
            evacuate(banks, dve, 1, late)
            for o in range(8):
                t, half = o % 4, o // 4
                xs = chip.x[:, t, half * 512:(half + 1) * 512]
                dve.tensor_tensor(xs, banks.take(dve, OUT + o)[:, :], xs, ALU.add).then_inc(x_added, 1)
            dve.wait_ge(x_added, 8)


NH, NG, HD = 16, 4, 64
NCMP = 31
BELOW = 512
MASKED = -1e30


def modulated_residual(dve, chip, banks, first, gate_row, scratch, own, x_added):
    for o in range(8):
        t, half = o % 4, o // 4
        cols = slice(half * 512, (half + 1) * 512)
        own(dve.tensor_tensor(scratch, banks.take(dve, first + o)[:, :], gate_row[:, cols], ALU.mult))
        dve.tensor_tensor(chip.x[:, t, cols], scratch, chip.x[:, t, cols], ALU.add).then_inc(x_added, 1)
        dve.wait_ge(x_added, o + 1)


def nsa(chip):
    nc, dram = chip.nc, chip.dram
    scale = HD ** -0.5
    units = [(h, i) for h in range(NH) for i in range(TT)]
    U = len(units)
    NB = [min(8 * i + 7, NCMP) for i in range(TT)]
    with Scope(nc, "nsa") as s:
        banks = Banks(s)
        ROWS, Q, K, V, C, GATES, QT, KTR = 0, 2, 10, 14, 18, 22, 23, 31
        PEB, HID, GROW, CMP, CMPT, OT, OUT = 35, 36, 37, 40, 42, 43, 51
        region = s.sb("region", [P, NH * BELOW])
        norm = Norm(chip, s, banks.ps[4:8], region[:, 0:4096], region[:, 4096:8192])
        norm.allocate(s)
        strip = region[:, :].rearrange("p (h c) -> p h c", h=NH)
        loads = [(dram["nsa_w"][i], 4096, n) for i, n in enumerate([6, 10, 14, 18, 22])]
        loads += [(dram["nsa_cmp_w1"], 4096, HID + 3), (dram["nsa_w"][5], 4096, OUT + 4), (dram["nsa_w"][6], 4096, OUT + 8)]
        ring = Ring(s, 2, loads, banks.computed)
        q_tok = s.sb("q_tok", [P, TT, NH, HD])
        o_tok = q_tok
        k_tok = s.sb("k_tok", [P, TT, 2 * NG, HD])
        cT = s.sb("cT", [P, 2, NG, SEQ])
        oT = cT[:, :, :, :].rearrange("p a g t -> p (a g) t")
        qT = s.sb("qT", [P, KT, SEQ])
        kT = s.sb("kT", [P, 4, SEQ])
        v = s.sb("v", [P, TT, 2, NG, HD])
        gates = s.sb("gates", [P, TT, 3 * NH])
        w_gates = s.sb("w_gates", [P, KT, 3 * NH])
        small = s.sb("small", [64, 192])
        peT = small[:, 0:64].rearrange("p (a j) -> p a j", a=2)
        w2 = small[:, 64:192].rearrange("p (a n) -> p a n", a=2)
        table = s.sb("table", [64, NH])
        buckets = s.sb("buckets", [64, 640])
        rows = s.sb("rows", [NH, 640])
        peb = s.sb("peb", [64, 2])
        hid = s.sb("hid", [64, 2, NG * NCMP])
        kc_tok = s.sb("kc_tok", [NCMP, NG, HD])
        vc = s.sb("vc", [NCMP, NG * HD])
        kcT = s.sb("kcT", [P, 2, NCMP])
        gate_row = s.sb("gate_row", [P, DM])
        cmp_bias = k_tok[:, :, :, :].rearrange("p t g d -> p (t g d)")[:, 0:NH * TT * NCMP]\
            .rearrange("p (h i n) -> p h i n", h=NH, i=TT)
        sc = [s.sb(f"scores{i}", [P, 2, SEQ]) for i in range(2)]
        ex = [s.sb(f"exps{i}", [P, 2, SEQ]) for i in range(2)]
        pT = [s.sb(f"probsT{i}", [P, 2, SEQ]) for i in range(2)]
        diag = sc[1][:, :, :].rearrange("p a c -> p (a c)").rearrange("p (k n) -> p k n", k=KT)
        squares = sc[0][:, :, :].rearrange("p a c -> p (a c)").rearrange("p (h d) -> p h d", d=HD)
        qs = s.sb("q_stat", [P, 4, TT * NH])
        ks = s.sb("k_stat", [P, 4, TT * 2 * NG])
        cs = s.sb("cmp_stat", [NCMP, 4, NG])
        neg_max = s.sb("neg_max", [P, U, 2])
        sums = s.sb("sums", [P, U, 2])
        rsum = s.sb("rsum", [P, U, 2])
        fac = s.sb("fac", [P, U, 2])
        c_neg_max, c_raw_max, c_sums, c_safe, c_rsum, c_fac = [
            s.sb(f"cmp_{what}", [P, NH, TT]) for what in ("neg_max", "raw_max", "sums", "safe", "rsum", "fac")]
        small_loaded, rows_stored, strip_loaded = s.sem("small_loaded"), s.sem("rows_stored"), s.sem("strip_loaded")
        own_v, stat_var, stat_rstd = s.sem("own_v"), s.sem("stat_var"), s.sem("stat_rstd")
        q_normed, k_normed, kc_normed = s.sem("q_normed"), s.sem("k_normed"), s.sem("kc_normed")
        diag_ready, bias_filled = s.sem("diag_ready"), s.sem("bias_filled")
        c_scores, c_read, c_max, c_exps = s.sem("c_scores"), s.sem("c_read"), s.sem("c_max"), s.sem("c_exps")
        c_turned, c_probsT, c_values, c_out = s.sem("c_turned"), s.sem("c_probsT"), s.sem("c_values"), s.sem("c_out")
        scores_done, scores_read, max_ready = s.sem("scores_done"), s.sem("scores_read"), s.sem("max_ready")
        exps_done, turned, probsT, values_done = s.sem("exps_done"), s.sem("probs_turned"), s.sem("probsT"), s.sem("values_done")
        o_added, x_added = s.sem("o_added"), s.sem("x_added")
        block = s.block()

        outputs = {ROWS: [piece(rows[:, 0:512], rows=(0, NH))],
                   ROWS + 1: [piece(rows[:, 512:640], cols=(0, 128), rows=(0, NH))],
                   GATES: [piece(gates[:, :, :].rearrange("p t c -> p (t c)"), cols=(0, 192), func=ACT.Sigmoid)],
                   PEB: [piece(peb[:, :], cols=(0, 2), rows=(0, 64))],
                   CMP: [piece(kc_tok[:, :, :].rearrange("n g d -> n (g d)"), cols=(0, 256), rows=(0, NCMP))],
                   CMP + 1: [piece(vc[:, :], cols=(0, 256), rows=(0, NCMP))],
                   CMPT: [piece(kcT[:, a, :], cols=(32 * a, 32 * a + NCMP), scale=chip.gain("nsa_k_gain_2", 0))
                          for a in range(2)]}
        for t in range(TT):
            for a in range(2):
                outputs[Q + 4 * a + t] = [piece(q_tok[:, t, 8 * a:8 * a + 8, :].rearrange("p h d -> p (h d)"))]
            outputs[K + t] = [piece(k_tok[:, t, :, :].rearrange("p g d -> p (g d)"))]
            outputs[V + t] = [piece(v[:, t, :, :, :].rearrange("p a g d -> p (a g d)"))]
            outputs[C + t] = [piece(cT[0:64, t // 2, 2 * (t % 2) + a, :], rows=(64 * a, 64 * a + 64)) for a in range(2)]
            outputs[KTR + t] = [piece(kT[:, t, :], scale=chip.gain("nsa_k_gain_2", 1 + t // 2))]
        for m in range(KT):
            outputs[QT + m] = [piece(qT[:, m, :], scale=chip.gain("nsa_q_gain_2", 0))]
            outputs[OT + m] = [piece(oT[:, m, :])]
        for a in range(2):
            outputs[HID + 2 * a] = [piece(hid[:, a, :], cols=(0, NG * NCMP), rows=(0, 64), func=ACT.Silu,
                                          bias=peb[:, a:a + 1])]
            outputs[GROW + 2 * a] = [piece(gate_row[:, 512 * a:512 * a + 512])]

        def query(h, i):
            half, m = (h // 4) % 2, (h // 8) * 4 + h % 4
            return qT[64 * half:64 * half + 64, m, i * P:(i + 1) * P]

        @block.sync
        def _(sp):
            sp.dma_start(table[:, :], dram["nsa_table"]).then_inc(small_loaded, 16)
            sp.dma_start(buckets[:, :], dram["nsa_buckets"]).then_inc(small_loaded, 16)
            ring.fill(sp, 0, 2)
            sp.dma_start(small[:, :], dram["nsa_small"]).then_inc(small_loaded, 16)
            sp.dma_start(w_gates[:, :, :], dram["nsa_w_gates"]).then_inc(small_loaded, 16)
            banks.wait_for(sp, ROWS)
            banks.wait_for(sp, ROWS + 1)
            sp.dma_start(dram["bias_rows"], rows[:, :]).then_inc(rows_stored, 16)
            sp.wait_ge(rows_stored, 16)
            one = bass.AP(dram["bias_rows"].tensor, 0, [[0, P], [1, NH * 640]])
            sp.dma_start(dram["bias_copies"], one).then_inc(rows_stored, 16)
            ring.fill(sp, 2, 6)
            sp.wait_ge(banks.computed, GATES + 1)
            sp.wait_ge(rows_stored, 32)
            askew = bass.AP(dram["bias_copies"].tensor, 127, [[NH * 640 - 1, P], [640, NH], [1, BELOW]])
            sp.dma_start(strip, askew).then_inc(strip_loaded, 16)
            ring.fill(sp, 6)

        @block.gpsimd
        def _(pool):
            pool.wait_ge(banks.computed, KTR + 4)
            pool.memset(cmp_bias, MASKED).then_inc(bias_filled, 1)

        @block.tensor
        def _(pe):
            pe.wait_ge(small_loaded, 64)
            for o, (a, b) in enumerate(((0, 512), (512, 640))):
                pe.matmul(banks.open(pe, ROWS + o)[0:NH, 0:b - a], table[:, :], buckets[:, a:b],
                          start=True, stop=True).then_inc(banks.computed, 1)
            norm.tensor(pe)
            norm.complete(pe)
            token_major(pe, banks, Q, ring.weights(pe, 0), norm.hT)
            token_major(pe, banks, Q + 4, ring.weights(pe, 1), norm.hT)
            token_major(pe, banks, K, ring.weights(pe, 2), norm.hT)
            token_major(pe, banks, V, ring.weights(pe, 3), norm.hT)
            feature_major(pe, banks, C, ring.weights(pe, 4), norm.hT)
            bank = banks.open(pe, GATES)
            for t in range(TT):
                for k in range(KT):
                    last = pe.matmul(bank[:, 48 * t:48 * t + 48], norm.hT[:, k, t * P:(t + 1) * P], w_gates[:, k, :],
                                     start=(k == 0), stop=(k == KT - 1))
            last.then_inc(banks.computed, 1)
            pe.wait_ge(q_normed, TT)
            for m in range(KT):
                bank = banks.open(pe, QT + m)
                for t in range(TT):
                    last = pe.transpose(bank[:, t * P:(t + 1) * P],
                                        q_tok[:, t, 2 * m:2 * m + 2, :].rearrange("p h d -> p (h d)"), chip.ident[:, :])
                last.then_inc(banks.computed, 1)
            pe.wait_ge(k_normed, 1)
            for m in range(4):
                bank = banks.open(pe, KTR + m)
                for t in range(TT):
                    last = pe.transpose(bank[:, t * P:(t + 1) * P],
                                        k_tok[:, t, 2 * m:2 * m + 2, :].rearrange("p g d -> p (g d)"), chip.ident[:, :])
                last.then_inc(banks.computed, 1)
            w1 = ring.get(pe, 5)[:, :].rearrange("p (a j e) -> p a j e", a=2, j=32)
            bank = banks.open(pe, PEB)
            for a in range(2):
                for j in range(32):
                    last = pe.matmul(bank[0:64, a:a + 1], w1[0:64, a, j, :], peT[:, a, j:j + 1],
                                     start=(j == 0), stop=(j == 31))
            last.then_inc(banks.computed, 1)
            banks.wait_for(pe, C + 2)
            banks.wait_for(pe, C + 3)
            for a in range(2):
                bank = banks.open(pe, HID + 2 * a)
                for j in range(32):
                    last = pe.matmul(bank[0:64, 0:NG * NCMP].rearrange("p (g n) -> p g n", g=NG), w1[0:64, a, j, :],
                                     cT[0:64, a, :, j:j + 16 * (NCMP - 1) + 1:16], start=(j == 0), stop=(j == 31))
                last.then_inc(banks.computed, 1)
                pe.wait_ge(diag_ready, 1)
                bank = banks.open(pe, GROW + 2 * a)
                for k in range(4):
                    last = pe.matmul(bank[:, k * P:(k + 1) * P], chip.ones[:, :], diag[:, 4 * a + k, :],
                                     start=True, stop=True)
                last.then_inc(banks.computed, 1)
            banks.wait_for(pe, HID + 2)
            for a in range(2):
                bank = banks.open(pe, CMP + a)
                for g in range(NG):
                    last = pe.matmul(bank[0:NCMP, g * HD:(g + 1) * HD], hid[:, a, g * NCMP:(g + 1) * NCMP], w2[:, a, :],
                                     start=True, stop=True)
                last.then_inc(banks.computed, 1)
            pe.wait_ge(kc_normed, 1)
            bank = banks.open(pe, CMPT)
            for a in range(2):
                last = pe.transpose(bank[:, 32 * a:32 * a + NCMP],
                                    kc_tok[:, 2 * a:2 * a + 2, :].rearrange("n g d -> n (g d)"),
                                    chip.ident[0:NCMP, 0:NCMP])
            last.then_inc(banks.computed, 1)
            banks.wait_for(pe, CMPT)
            banks.wait_for(pe, CMPT - 1)
            for step in range(NH + 2):
                if step < NH:
                    h = step
                    half = (h // 4) % 2
                    if h >= 2:
                        pe.wait_ge(c_read, h - 1)
                    for i in range(TT):
                        last = pe.matmul(banks.ps[h % 2][:, i * NCMP:(i + 1) * NCMP], query(h, i),
                                         kcT[64 * half:64 * half + 64, h // 8, :], start=True, stop=True)
                    last.then_inc(c_scores, 1)
                if 1 <= step <= NH:
                    h = step - 1
                    pe.wait_ge(c_exps, TT * (h + 1))
                    if h >= 2:
                        pe.wait_ge(c_probsT, h - 1)
                    for i in range(TT):
                        last = pe.transpose(banks.ps[2 + h % 2][0:NCMP, i * P:(i + 1) * P],
                                            ex[h % 2][:, 0, i * NCMP:(i + 1) * NCMP], chip.ident[:, :])
                    last.then_inc(c_turned, 1)
                if step >= 2:
                    h = step - 2
                    pe.wait_ge(c_probsT, h + 1)
                    if h >= 2:
                        pe.wait_ge(c_out, h - 1)
                    for i in range(TT):
                        last = pe.matmul(banks.ps[4 + h % 2][:, i * HD:(i + 1) * HD], pT[h % 2][0:NCMP, 0, i * P:(i + 1) * P],
                                         vc[:, (h // 4) * HD:(h // 4 + 1) * HD], start=True, stop=True)
                    last.then_inc(c_values, 1)
            pe.wait_ge(c_out, NH)
            for step in range(U + 2):
                if step < U:
                    u = step
                    h, i = units[u]
                    half = (h // 4) % 2
                    W = (i + 1) * P
                    if u >= 2:
                        pe.wait_ge(scores_read, u - 1)
                    for b in range(2):
                        last = pe.matmul(banks.ps[2 * (u % 2) + b][:, 0:W], query(h, i),
                                         kT[64 * half:64 * half + 64, 2 * b + h // 8, 0:W], start=True, stop=True)
                    last.then_inc(scores_done, 1)
                if 1 <= step <= U:
                    u = step - 1
                    h, i = units[u]
                    pe.wait_ge(exps_done, 2 * (u + 1))
                    if u >= 1:
                        pe.wait_ge(probsT, 2 * u)
                    for b in range(2):
                        for c in range(i + 1):
                            last = pe.transpose(banks.ps[4 + b][:, c * P:(c + 1) * P], ex[u % 2][:, b, c * P:(c + 1) * P],
                                                chip.ident[:, :])
                    last.then_inc(turned, 1)
                if step >= 2:
                    u = step - 2
                    h, i = units[u]
                    pe.wait_ge(probsT, 2 * (u + 1))
                    if u >= 2:
                        pe.wait_ge(o_added, 2 * (u - 1))
                    for b in range(2):
                        for c in range(i + 1):
                            last = pe.matmul(banks.ps[6 + u % 2][:, b * HD:(b + 1) * HD], pT[u % 2][:, b, c * P:(c + 1) * P],
                                             v[:, c, b, h // 4, :], start=(c == 0), stop=(c == i))
                    last.then_inc(values_done, 1)
            pe.wait_ge(o_added, 2 * U)
            for m in range(KT):
                bank = banks.open(pe, OT + m)
                for t in range(TT):
                    last = pe.transpose(bank[:, t * P:(t + 1) * P],
                                        o_tok[:, t, 2 * m:2 * m + 2, :].rearrange("p h d -> p (h d)"), chip.ident[:, :])
                last.then_inc(banks.computed, 1)
            banks.wait_for(pe, OT + KT - 2)
            banks.wait_for(pe, OT + KT - 1)
            token_major(pe, banks, OUT, ring.weights(pe, 6), oT)
            token_major(pe, banks, OUT + 4, ring.weights(pe, 7), oT)

        @block.scalar
        def _(act):
            evacuate(banks, act, 0, outputs, 0, Q)
            norm.scalar_stats(act)
            norm.scalar_evacuate(act, chip.mod_gain[:, 0, :], chip.mod[:, 0, 0, :])
            evacuate(banks, act, 0, outputs, Q, V)
            for n, st in enumerate((qs, ks)):
                act.wait_ge(stat_var, n + 1)
                act.activation(st[:, 3, :], st[:, 2, :], ACT.Sqrt).then_inc(stat_rstd, 1)
            evacuate(banks, act, 0, outputs, V, PEB)
            banks.wait_for(act, PEB)
            evacuate(banks, act, 0, outputs, PEB, CMP + 1)
            act.wait_ge(stat_var, 3)
            act.activation(cs[:, 3, :], cs[:, 2, :], ACT.Sqrt).then_inc(stat_rstd, 1)
            evacuate(banks, act, 0, outputs, CMP + 1, OT)
            for step in range(NH + 1):
                if step < NH:
                    h = step
                    act.wait_ge(c_max, h + 1)
                    if h >= 2:
                        act.wait_ge(c_turned, h - 1)
                    for i in range(TT):
                        act.activation(ex[h % 2][:, 0, i * NCMP:(i + 1) * NCMP], sc[h % 2][:, 0, i * NCMP:(i + 1) * NCMP],
                                       ACT.Exp, bias=c_neg_max[:, h, i:i + 1], accum_out=c_sums[:, h, i:i + 1])\
                            .then_inc(c_exps, 1)
                if step >= 1:
                    h = step - 1
                    act.wait_ge(c_turned, h + 1)
                    if h >= 2:
                        act.wait_ge(c_values, h - 1)
                    act.activation(pT[h % 2][0:NCMP, 0, :], banks.ps[2 + h % 2][0:NCMP, :], ACT.Copy)\
                        .then_inc(c_probsT, 1)
            act.wait_ge(c_out, NH)
            for step in range(U + 1):
                if step < U:
                    u = step
                    h, i = units[u]
                    W = (i + 1) * P
                    act.wait_ge(max_ready, u + 1)
                    if u >= 2:
                        act.wait_ge(turned, u - 1)
                    for b in range(2):
                        act.activation(ex[u % 2][:, b, 0:W], sc[u % 2][:, b, 0:W], ACT.Exp, bias=neg_max[:, u, b:b + 1],
                                       accum_out=sums[:, u, b:b + 1]).then_inc(exps_done, 1)
                if step >= 1:
                    u = step - 1
                    h, i = units[u]
                    W = (i + 1) * P
                    act.wait_ge(turned, u + 1)
                    if u >= 2:
                        act.wait_ge(values_done, u - 1)
                    for b in range(2):
                        act.activation(pT[u % 2][:, b, 0:W], banks.ps[4 + b][:, 0:W], ACT.Copy).then_inc(probsT, 1)
            evacuate(banks, act, 0, outputs, OT)

        @block.vector
        def _(dve):
            own = Own(dve, own_v)
            evacuate(banks, dve, 1, outputs, 0, Q)
            norm.vector(dve)
            norm.vector_evacuate(dve, chip.mod_gain[:, 0, :], chip.mod[:, 0, 0, :])
            evacuate(banks, dve, 1, outputs, Q, V)

            def head_stats(t, n, st, src, at):
                width = src.shape[1]
                sq = squares[0:n, 0:width, :]
                own(dve.tensor_tensor(sq, src, src, ALU.mult))
                own(dve.reduce_sum(st[:, 0, at:at + width], sq, AXX))

            def head_var(st):
                own(dve.tensor_scalar(st[:, 1, :], st[:, 0, :], 1.0 / HD, EPS, ALU.mult, ALU.add))
                dve.reciprocal(st[:, 2, :], st[:, 1, :]).then_inc(stat_var, 1)

            for o in (V - 2, V - 1):
                banks.wait_for(dve, o)
            for t in range(TT):
                head_stats(t, P, qs, q_tok[:, t, :, :], NH * t)
            head_var(qs)
            for t in range(TT):
                head_stats(t, P, ks, k_tok[:, t, :, :], 2 * NG * t)
            dve.wait_ge(stat_rstd, 1)
            for t in range(TT):
                dve.tensor_tensor(q_tok[:, t, :, :], q_tok[:, t, :, :],
                                  qs[:, 3, NH * t:NH * t + NH].unsqueeze(2).broadcast_to([P, NH, HD]), ALU.mult)\
                    .then_inc(q_normed, 1)
            head_var(ks)
            dve.wait_ge(stat_rstd, 2)
            k_all = k_tok[:, :, :, :].rearrange("p t g d -> p (t g) d")
            dve.tensor_tensor(k_all, k_all, ks[:, 3, :].unsqueeze(2).broadcast_to([P, TT * 2 * NG, HD]), ALU.mult)\
                .then_inc(k_normed, 1)
            dve.tensor_tensor(diag, chip.ident[:, :].unsqueeze(1).broadcast_to([P, KT, P]),
                              chip.mod[:, 0, 2, :].unsqueeze(2).broadcast_to([P, KT, P]), ALU.mult).then_inc(diag_ready, 1)
            evacuate(banks, dve, 1, outputs, V, CMP)
            banks.wait_for(dve, CMP)
            head_stats(0, NCMP, cs, kc_tok[:, :, :], 0)
            head_var(cs)
            dve.wait_ge(stat_rstd, 3)
            dve.tensor_tensor(kc_tok[:, :, :], kc_tok[:, :, :], cs[:, 3, :].unsqueeze(2).broadcast_to([NCMP, NG, HD]),
                              ALU.mult).then_inc(kc_normed, 1)
            evacuate(banks, dve, 1, outputs, CMP, OT)
            dve.wait_ge(strip_loaded, 16)
            dve.wait_ge(bias_filled, 1)
            for i in range(TT):
                c = 384 - P * i + 31
                own(dve.tensor_copy(cmp_bias[:, :, i, 0:NB[i]], strip[:, :, c:c + 16 * (NB[i] - 1) + 1:16]))
            for step in range(NH + 2):
                if step < NH:
                    h = step
                    dve.wait_ge(c_scores, h + 1)
                    if h >= 2:
                        dve.wait_ge(c_exps, TT * (h - 1))
                    W = TT * NCMP
                    dve.scalar_tensor_tensor(out=sc[h % 2][:, 0, 0:W], in0=banks.ps[h % 2][:, 0:W], scalar=scale,
                                             in1=cmp_bias[:, h, :, :].rearrange("p i n -> p (i n)"),
                                             op0=ALU.mult, op1=ALU.add).then_inc(c_read, 1)
                    dve.wait_ge(c_read, h + 1)
                    own(dve.tensor_reduce(c_raw_max[:, h, :], sc[h % 2][:, 0, 0:W].rearrange("p (i n) -> p i n", i=TT),
                                          axis=AXX, op=ALU.max, negate=True))
                    dve.tensor_scalar(c_neg_max[:, h, :], c_raw_max[:, h, :], -MASKED * 1e-6, None, ALU.min)\
                        .then_inc(c_max, 1)
                if 1 <= step <= NH:
                    h = step - 1
                    dve.wait_ge(c_exps, TT * (h + 1))
                    own(dve.tensor_scalar(c_safe[:, h, :], c_sums[:, h, :], 1e-30, None, ALU.max))
                    own(dve.reciprocal(c_rsum[:, h, :], c_safe[:, h, :]))
                    own(dve.tensor_tensor(c_fac[:, h, :], c_rsum[:, h, :], gates[:, :, 3 * h], ALU.mult))
                if step >= 2:
                    h = step - 2
                    dve.wait_ge(c_values, h + 1)
                    dve.tensor_tensor(o_tok[:, :, h, :], banks.ps[4 + h % 2][:, 0:TT * HD].rearrange("p (i d) -> p i d", i=TT),
                                      c_fac[:, h, :].unsqueeze(2).broadcast_to([P, TT, HD]), ALU.mult).then_inc(c_out, 1)
            dve.wait_ge(c_out, NH)
            for step in range(U + 2):
                if step < U:
                    u = step
                    h, i = units[u]
                    W, c = (i + 1) * P, 384 - P * i
                    dve.wait_ge(scores_done, u + 1)
                    if u >= 2:
                        dve.wait_ge(exps_done, 2 * (u - 1))
                    for b in range(2):
                        last = dve.scalar_tensor_tensor(out=sc[u % 2][:, b, 0:W], in0=banks.ps[2 * (u % 2) + b][:, 0:W],
                                                        scalar=scale, in1=strip[:, h, c:c + W], op0=ALU.mult, op1=ALU.add)
                        if b == 0:
                            own(last)
                    last.then_inc(scores_read, 1)
                    dve.wait_ge(scores_read, u + 1)
                    dve.tensor_reduce(neg_max[:, u, :], sc[u % 2][:, :, 0:W], axis=AXX, op=ALU.max, negate=True)\
                        .then_inc(max_ready, 1)
                if 1 <= step <= U:
                    u = step - 1
                    h, i = units[u]
                    dve.wait_ge(exps_done, 2 * (u + 1))
                    own(dve.reciprocal(rsum[:, u, :], sums[:, u, :]))
                    own(dve.tensor_tensor(fac[:, u, :], rsum[:, u, :], gates[:, i, 3 * h + 1:3 * h + 3], ALU.mult))
                if step >= 2:
                    u = step - 2
                    h, i = units[u]
                    dve.wait_ge(values_done, u + 1)
                    for b in range(2):
                        dve.scalar_tensor_tensor(out=o_tok[:, i, h, :], in0=banks.ps[6 + u % 2][:, b * HD:(b + 1) * HD],
                                                 scalar=fac[:, u, b:b + 1], in1=o_tok[:, i, h, :],
                                                 op0=ALU.mult, op1=ALU.add).then_inc(o_added, 1)
                        dve.wait_ge(o_added, 2 * u + b + 1)
            evacuate(banks, dve, 1, outputs, OT)
            modulated_residual(dve, chip, banks, OUT, gate_row, sc[0][:, 0, :], own, x_added)


HG = 8
LEVELS = [None] + [1 << l for l in range(7)]


def hgrn(chip):
    nc, dram = chip.nc, chip.dram
    units = [(h, None) for h in range(HG)] + [(h, b) for h in range(HG) for b in LEVELS[1:]]
    U = len(units)
    with Scope(nc, "hgrn") as s:
        banks = Banks(s, 6)
        level_ps = [s.ps(f"level{i}", [P, SEQ]) for i in range(2)]
        FQ, VG, KK, GROW, OC, OT, OUT = 0, 16, 32, 40, 42, 50, 58
        a = s.sb("region_a", [P, 4096])
        b = s.sb("region_b", [P, 4096])
        norm = Norm(chip, s, banks.ps[0:4], a[:, :], b[:, :])
        norm.allocate(s)
        qT = s.sb("qT", [P, HG, SEQ])
        kT = s.sb("kT", [P, HG, SEQ])
        cum = s.sb("cum", [P, HG, SEQ])
        v = s.sb("v", [P, TT, DM])
        g = s.sb("g", [P, TT, DM])
        scratch = a[:, :].rearrange("p (h t) -> p h t", h=HG)
        att = b[:, :].rearrange("p (h c t) -> p h c t", h=HG, c=TT)
        kk = a[:, :].rearrange("p (c d) -> p c d", c=TT)
        o_tok = cum[:, :, :].rearrange("p h t -> p (h t)").rearrange("p (c d) -> p c d", c=TT)
        o_heads = cum[:, :, :].rearrange("p h t -> p (h t)").rearrange("p (u e) -> p u e", e=P)
        squares = kT[:, :, :].rearrange("p h t -> p (h t)").rearrange("p (u e) -> p u e", e=P)
        cum_ch = cum[:, :, :].rearrange("p h t -> p (h t)").rearrange("p (u t) -> p u t", t=P)
        scratch_ch = a[:, :].rearrange("p (u t) -> p u t", t=P)
        counts = [4, 8, 12, 16, 20, 24, 28, 32, OUT + 4, OUT + 8]
        ring = Ring(s, 2, [(dram["hgrn_w"][i], 4096, n) for i, n in enumerate(counts)], banks.computed)
        masks = s.sb("masks", [P, len(LEVELS), P], I32)
        keep = s.sb("keep", [P, SEQ])
        M = [s.sb(f"decayed{i}", [P, SEQ]) for i in range(4)]
        state = [s.sb(f"state{i}", [P, HG, P]) for i in range(2)]
        decay = s.sb("decay", [P, HG, TT])
        lb = s.sb("lb", [P, 8, 2 * HG])
        ost = s.sb("o_stat", [P, 4, TT * HG])
        gate_row = s.sb("gate_row", [P, DM])
        diag = s.sb("diag", [P, KT, P])
        small_loaded, own_v = s.sem("small_loaded"), s.sem("own_v")
        lb_diff, lb_exp = s.sem("lb_diff"), s.sem("lb_exp")
        f_scaled, f_log, q_silu, g_silu, cum_ready = s.sem("f_scaled"), s.sem("f_log"), s.sem("q_silu"), s.sem("g_silu"), s.sem("cum_ready")
        gaps_ready, decays_ready, m_ready = s.sem("gaps_ready"), s.sem("decays_ready"), s.sem("m_ready")
        level_done, level_taken, att_zeroed = s.sem("level_done"), s.sem("level_taken"), s.sem("att_zeroed")
        cum_exp, last_gaps, last_exp, q_decayed, k_decayed = s.sem("cum_exp"), s.sem("last_gaps"), s.sem("last_exp"), s.sem("q_decayed"), s.sem("k_decayed")
        decay_ready, state_done, state_ready = s.sem("decay_ready"), s.sem("state_done"), s.sem("state_ready")
        o_var, o_rstd, o_normed, diag_ready, x_added = s.sem("o_var"), s.sem("o_rstd"), s.sem("o_normed"), s.sem("diag_ready"), s.sem("x_added")
        block = s.block()

        outputs = {}
        for m in range(HG):
            outputs[FQ + 2 * m] = [piece(cum[:, m, :], func=ACT.Sigmoid), piece(kT[:, m, :], func=ACT.Sigmoid, scale=-1.0)]
            outputs[FQ + 2 * m + 1] = [piece(qT[:, m, :])]
            outputs[KK + m] = [piece(kk[:, m // 2, 512 * (m % 2):512 * (m % 2) + 512])]
            outputs[OC + m] = [piece(o_tok[:, m // 2, 512 * (m % 2):512 * (m % 2) + 512])]
            outputs[OT + m] = [piece(qT[:, m, :], scale=chip.gain("hgrn_out_gain_2", 0))]
        for o in range(16):
            dst, half, t = (v, g)[o // 8], (o // 4) % 2, o % 4
            outputs[VG + o] = [piece(dst[:, t, 512 * half:512 * half + 512])]
        for half in range(2):
            outputs[GROW + half] = [piece(gate_row[:, 512 * half:512 * half + 512])]

        def halves(x, size):
            blocks = x.rearrange("p (n s) -> p n s", s=2 * size)
            return blocks[:, :, 0:size], blocks[:, :, size:2 * size]

        @block.sync
        def _(sp):
            ring.fill(sp, 0, 2)
            sp.dma_start(masks[:, :, :], dram["hgrn_masks"]).then_inc(small_loaded, 16)
            sp.dma_start(keep[:, :], dram["hgrn_keep"]).then_inc(small_loaded, 16)
            ring.fill(sp, 2)

        @block.gpsimd
        def _(pool):
            pool.wait_ge(norm.turned, KT)
            pool.memset(b[:, :], 0.0).then_inc(att_zeroed, 1)

        @block.tensor
        def _(pe):
            norm.tensor(pe)
            norm.complete(pe)
            for j in range(4):
                w = ring.weights(pe, j)
                for m in range(4):
                    bank = banks.open(pe, FQ + 4 * j + m)
                    for k in range(KT):
                        last = pe.matmul(bank[:, :], w[:, k, m * P:(m + 1) * P], norm.hT[:, k, :],
                                         start=(k == 0), stop=(k == KT - 1))
                    last.then_inc(banks.computed, 1)
            for step in range(16):
                if step % 4 == 0:
                    w = ring.weights(pe, 4 + step // 4)
                bank = banks.open(pe, VG + step)
                t = step % 4
                for k in range(KT):
                    last = pe.matmul(bank[:, :], norm.hT[:, k, t * P:(t + 1) * P], w[:, k, :],
                                     start=(k == 0), stop=(k == KT - 1))
                last.then_inc(banks.computed, 1)
                for u in range(4 * step, 4 * step + 4):
                    h, size = units[u]
                    if size is None:
                        pe.wait_ge(cum_ready, h + 1)
                        pe.wait_ge(q_silu, h + 1)
                        left, right = kT[:, h, :], qT[:, h, :]
                    else:
                        pe.wait_ge(m_ready, u - HG + 1)
                        left = right = M[u % 4][:, :]
                    if u >= 2:
                        pe.wait_ge(level_taken, u - 1)
                    for c in range(TT):
                        last = pe.matmul(level_ps[u % 2][:, c * P:(c + 1) * P], left[:, c * P:(c + 1) * P],
                                         right[:, c * P:(c + 1) * P], start=True, stop=True)
                    last.then_inc(level_done, 1)
            pe.wait_ge(k_decayed, 1)
            for m in range(HG):
                bank = banks.open(pe, KK + m)
                for i in range(4):
                    h = 4 * (m % 2) + i
                    last = pe.transpose(bank[:, i * P:(i + 1) * P], kT[:, h, (m // 2) * P:(m // 2 + 1) * P], chip.ident[:, :])
                last.then_inc(banks.computed, 1)
            pe.wait_ge(diag_ready, 1)
            for half in range(2):
                bank = banks.open(pe, GROW + half)
                for k in range(4):
                    last = pe.matmul(bank[:, k * P:(k + 1) * P], chip.ones[:, :], diag[:, 4 * half + k, :],
                                     start=True, stop=True)
                last.then_inc(banks.computed, 1)
            banks.wait_for(pe, KK + HG - 2)
            banks.wait_for(pe, KK + HG - 1)
            pe.wait_ge(level_taken, U)
            pe.wait_ge(q_decayed, 1)
            for c in range(TT):
                for half in range(2):
                    if c < TT - 1:
                        if c >= 1:
                            pe.wait_ge(state_ready, HG * (c - 1) + 4 * half + 4)
                        for i in range(4):
                            h = 4 * half + i
                            last = pe.matmul(level_ps[half][:, i * P:(i + 1) * P], kk[:, c, h * P:(h + 1) * P],
                                             v[:, c, h * P:(h + 1) * P], start=True, stop=True)
                        last.then_inc(state_done, 1)
                for half in range(2):
                    bank = banks.open(pe, OC + 2 * c + half)
                    for i in range(4):
                        h = 4 * half + i
                        last = pe.matmul(bank[:, i * P:(i + 1) * P], att[:, h, c, :], v[:, c, h * P:(h + 1) * P],
                                         start=True, stop=(c == 0))
                        if c >= 1:
                            pe.wait_ge(state_ready, HG * (c - 1) + h + 1)
                            last = pe.matmul(bank[:, i * P:(i + 1) * P], qT[:, h, c * P:(c + 1) * P],
                                             state[c % 2][:, h, :], start=False, stop=True)
                    last.then_inc(banks.computed, 1)
            pe.wait_ge(o_normed, 1)
            for m in range(KT):
                bank = banks.open(pe, OT + m)
                for t in range(TT):
                    last = pe.transpose(bank[:, t * P:(t + 1) * P], o_tok[:, t, m * P:(m + 1) * P], chip.ident[:, :])
                last.then_inc(banks.computed, 1)
            banks.wait_for(pe, OT + KT - 2)
            banks.wait_for(pe, OT + KT - 1)
            for half in range(2):
                w = ring.weights(pe, 8 + half)
                for t in range(TT):
                    o = 4 * half + t
                    if o >= 6:
                        pe.wait_ge(x_added, o - 5)
                        bank = banks.ps[(OUT + o) % 6]
                    else:
                        bank = banks.open(pe, OUT + o)
                    for k in range(KT):
                        last = pe.matmul(bank[:, :], qT[:, k, t * P:(t + 1) * P], w[:, k, :],
                                         start=(k == 0), stop=(k == KT - 1))
                    last.then_inc(banks.computed, 1)

        @block.scalar
        def _(act):
            norm.scalar_stats(act)
            act.wait_ge(lb_diff, 1)
            act.activation(lb[:, 2, :], lb[:, 1, :], ACT.Exp).then_inc(lb_exp, 1)
            norm.scalar_evacuate(act, chip.mod_gain[:, 2, :], chip.mod[:, 2, 0, :])
            evacuate(banks, act, 0, outputs, FQ, VG)
            for h in range(HG):
                act.wait_ge(f_scaled, h + 1)
                act.activation(cum[:, h, :], cum[:, h, :], ACT.Ln).then_inc(f_log, 1)
            banks.wait_for(act, VG - 1)
            for h in range(HG):
                act.activation(qT[:, h, :], qT[:, h, :], ACT.Silu).then_inc(q_silu, 1)
            for u in range(U):
                h, size = units[u]
                if size is not None:
                    act.wait_ge(gaps_ready, u - HG + 1)
                    act.activation(M[u % 4][:, :], M[u % 4][:, :], ACT.Exp).then_inc(decays_ready, 1)
                if u % 4 == 3:
                    evacuate(banks, act, 0, outputs, VG + u // 4, VG + u // 4 + 1)
            banks.wait_for(act, VG + 15)
            act.wait_ge(level_done, U)
            act.activation(scratch, cum[:, :, :], ACT.Exp).then_inc(cum_exp, 1)
            act.activation(decay[:, :, :].rearrange("p h c -> p (h c)"), cum_ch[:, :, P - 1], ACT.Exp).then_inc(decay_ready, 1)
            act.wait_ge(last_gaps, 1)
            act.activation(scratch, scratch, ACT.Exp).then_inc(last_exp, 1)
            for t in range(TT):
                act.activation(g[:, t, :], g[:, t, :], ACT.Silu).then_inc(g_silu, 1)
            evacuate(banks, act, 0, outputs, KK, OT)
            act.wait_ge(o_var, 1)
            act.activation(ost[:, 3, :], ost[:, 2, :], ACT.Sqrt).then_inc(o_rstd, 1)
            evacuate(banks, act, 0, outputs, OT)

        @block.vector
        def _(dve):
            own = Own(dve, own_v)
            low = [chip.gain("hgrn_lower_bounds_2", l) for l in range(2)]
            own(dve.tensor_tensor(lb[:, 0, 0:HG], low[0], low[1], ALU.max))
            own(dve.tensor_tensor(lb[:, 1, 0:HG], low[0], lb[:, 0, 0:HG], ALU.subtract))
            dve.tensor_tensor(lb[:, 1, HG:2 * HG], low[1], lb[:, 0, 0:HG], ALU.subtract).then_inc(lb_diff, 1)
            norm.vector(dve)
            norm.vector_evacuate(dve, chip.mod_gain[:, 2, :], chip.mod[:, 2, 0, :])
            dve.wait_ge(lb_exp, 1)
            own(dve.tensor_tensor(lb[:, 3, 0:HG], lb[:, 2, 0:HG], lb[:, 2, HG:2 * HG], ALU.add))
            own(dve.reciprocal(lb[:, 3, HG:2 * HG], lb[:, 3, 0:HG]))
            for l in range(2):
                own(dve.tensor_tensor(lb[:, 4, HG * l:HG * l + HG], lb[:, 2, HG * l:HG * l + HG], lb[:, 3, HG:2 * HG], ALU.mult))
            own(dve.tensor_tensor(lb[:, 5, 0:HG], lb[:, 4, 0:HG], lb[:, 4, HG:2 * HG], ALU.add))
            own(dve.tensor_tensor(lb[:, 6, 0:HG], lb[:, 5, 0:HG], lb[:, 4, 0:HG], ALU.subtract))
            own(dve.tensor_scalar(lb[:, 7, 0:HG], lb[:, 6, 0:HG], -1.0, 1.0, ALU.mult, ALU.add))
            low, rest = lb[:, 6, 0:HG], lb[:, 7, 0:HG]
            dve.tensor_tensor(diag[:, :, :], chip.ident[:, :].unsqueeze(1).broadcast_to([P, KT, P]),
                              chip.mod[:, 2, 2, :].unsqueeze(2).broadcast_to([P, KT, P]), ALU.mult).then_inc(diag_ready, 1)
            for h in range(HG):
                evacuate(banks, dve, 1, outputs, FQ + 2 * h, FQ + 2 * h + 2)
                banks.wait_for(dve, FQ + 2 * h)
                own(dve.tensor_scalar(kT[:, h, :], kT[:, h, :], rest[:, h:h + 1], None, ALU.mult))
                own(dve.tensor_scalar(cum[:, h, :], cum[:, h, :], rest[:, h:h + 1], low[:, h:h + 1], ALU.mult, ALU.add))
                dve.tensor_scalar(cum[:, h, :], cum[:, h, :], 1e-19, None, ALU.max).then_inc(f_scaled, 1)
            dve.wait_ge(small_loaded, 32)
            for h in range(HG):
                dve.wait_ge(f_log, h + 1)
                dve.tensor_tensor_scan(cum[:, h, :], keep[:, :], cum[:, h, :], 0.0, ALU.mult, ALU.add).then_inc(cum_ready, 1)
            dve.wait_ge(cum_ready, HG)
            dve.wait_ge(q_silu, HG)
            dve.wait_ge(att_zeroed, 1)
            for u in range(U + 2):
                if u < U and units[u][1] is not None:
                    h, size = units[u]
                    if u - 4 >= HG:
                        dve.wait_ge(level_done, u - 3)
                    c1, c2 = halves(cum[:, h, :], size)
                    m1, m2 = halves(M[u % 4][:, :], size)
                    mid = c1[:, :, size - 1:size].broadcast_to([P, SEQ // (2 * size), size])
                    own(dve.tensor_tensor(m1, mid, c1, ALU.subtract))
                    dve.tensor_tensor(m2, c2, mid, ALU.subtract).then_inc(gaps_ready, 1)
                if 1 <= u <= U and units[u - 1][1] is not None:
                    w = u - 1
                    h, size = units[w]
                    dve.wait_ge(decays_ready, w - HG + 1)
                    m1, m2 = halves(M[w % 4][:, :], size)
                    k1, _ = halves(kT[:, h, :], size)
                    _, q2 = halves(qT[:, h, :], size)
                    own(dve.tensor_tensor(m1, m1, k1, ALU.mult))
                    dve.tensor_tensor(m2, m2, q2, ALU.mult).then_inc(m_ready, 1)
                if u >= 2:
                    w = u - 2
                    h, size = units[w]
                    dve.wait_ge(level_done, w + 1)
                    if w >= 1:
                        dve.wait_ge(level_taken, w)
                    dve.copy_predicated(att[:, h, :, :], masks[:, LEVELS.index(size), :].unsqueeze(1).broadcast_to([P, TT, P]),
                                        level_ps[w % 2][:, :].rearrange("p (c t) -> p c t", c=TT)).then_inc(level_taken, 1)
                if u % 4 == 3 and u < U:
                    evacuate(banks, dve, 1, outputs, VG + u // 4, VG + u // 4 + 1)
            dve.wait_ge(cum_exp, 1)
            dve.tensor_tensor(qT[:, :, :], qT[:, :, :], scratch, ALU.mult).then_inc(q_decayed, 1)
            dve.wait_ge(q_decayed, 1)
            dve.tensor_tensor(scratch_ch, cum_ch[:, :, P - 1:P].broadcast_to([P, HG * TT, P]), cum_ch, ALU.subtract)\
                .then_inc(last_gaps, 1)
            dve.wait_ge(last_exp, 1)
            dve.tensor_tensor(kT[:, :, :], kT[:, :, :], scratch, ALU.mult).then_inc(k_decayed, 1)
            evacuate(banks, dve, 1, outputs, KK, OC)
            dve.wait_ge(decay_ready, 1)
            for c in range(TT):
                if c < TT - 1:
                    for h in range(HG):
                        if h % 4 == 0:
                            dve.wait_ge(state_done, 2 * c + h // 4 + 1)
                        new = state[(c + 1) % 2][:, h, :]
                        inc = level_ps[h // 4][:, (h % 4) * P:(h % 4 + 1) * P]
                        if c == 0:
                            dve.tensor_copy(new, inc).then_inc(state_ready, 1)
                        else:
                            dve.wait_ge(state_ready, HG * (c - 1) + h + 1)
                            if h == 0:
                                dve.wait_ge(banks.computed, OC + 2 * c)
                            dve.scalar_tensor_tensor(out=new, in0=state[c % 2][:, h, :], scalar=decay[:, h, c:c + 1],
                                                     in1=inc, op0=ALU.mult, op1=ALU.add).then_inc(state_ready, 1)
                evacuate(banks, dve, 1, outputs, OC + 2 * c, OC + 2 * c + 2)
            banks.wait_for(dve, OT - 2)
            banks.wait_for(dve, OT - 1)
            own(dve.tensor_tensor(squares, o_heads, o_heads, ALU.mult))
            own(dve.reduce_sum(ost[:, 0, :], squares, AXX))
            own(dve.tensor_scalar(ost[:, 1, :], ost[:, 0, :], 1.0 / P, EPS, ALU.mult, ALU.add))
            dve.reciprocal(ost[:, 2, :], ost[:, 1, :]).then_inc(o_var, 1)
            dve.wait_ge(o_rstd, 1)
            own(dve.tensor_tensor(o_heads, o_heads, ost[:, 3, :].unsqueeze(2).broadcast_to([P, TT * HG, P]), ALU.mult))
            dve.wait_ge(g_silu, TT)
            dve.tensor_tensor(o_tok, o_tok, g[:, :, :], ALU.mult).then_inc(o_normed, 1)
            evacuate(banks, dve, 1, outputs, OT)
            modulated_residual(dve, chip, banks, OUT, gate_row, M[0][:, :], own, x_added)


NE, NEG = 16, 4
NOV = 7
FF = 512
U32 = mybir.dt.uint32


def moe(chip, name, layer):
    nc, dram = chip.nc, chip.dram
    part = 2 * layer + 1
    mod, mod_gain = chip.mod[:, part, :, :], chip.mod_gain[:, part, :]
    with Scope(nc, name) as s:
        ps = [s.ps(f"bank{i}", [P, 512]) for i in range(8)]
        gather_ps, up_ps, turn_ps = ps[0:2], ps[2:4], ps[4:8]
        with nc.sbuf_tensor(f"{name}_hT", [P, KT * SEQ], FP32) as hT, nc.sbuf_tensor(f"{name}_xn", [P, TT * DM], FP32) as xn:
            norm = Norm(chip, s, ps[0:4], hT[:, :], xn[:, :])
        xn_high = s.sb("xn_high", [P, TT, DM], F32R)
        xn_low = s.sb("xn_low", [P, TT, DM], F32R)
        norm.allocate(s)
        w_router = s.sb("w_router", [P, KT, NEG + NE])
        const = s.sb("const", [P, 512])
        earlier, slot_no = const[:, 0:P], const[:, P:2 * P]
        first_slot, expert_no, block_no = const[:, 256:272], const[:, 272:288], const[:, 288:288 + NOV]
        w13 = [s.sb(f"w13_{i}", [P, 2, KT, FF]) for i in range(2)]
        w2 = [s.sb(f"w2_{i}", [P, TT, DM]) for i in range(2)]
        gate_row = s.sb("gate_row", [P, DM])
        logits = s.sb("logits", [P, TT, NEG + NE])
        group8 = s.sb("group8", [P, TT, 8])
        top = s.sb("top", [P, 2, TT, 8])
        top_at = s.sb("top_at", [P, 2, TT, 8], U32)
        top_f = s.sb("top_f", [P, 2, TT, 2])
        group_exp = s.sb("group_exp", [P, TT, NEG])
        pick = s.sb("pick", [P, TT, NEG])
        score = s.sb("score", [P, TT, NE])
        hot = s.sb("hot", [P, 2, TT, NE])
        member = s.sb("member", [P, TT, NE])
        tiny = s.sb("tiny", [P, 8, TT])
        weight = s.sb("weight", [P, 2, TT])
        place = s.sb("place", [P, TT, NE])
        over = s.sb("over", [P, 8, NE])
        slot_of = s.sb("slot_of", [P, 2, TT])
        route = s.sb("route", [P, 2, TT, NE])
        over_cmp = s.sb("over_cmp", [P, NOV, NE])
        over_expert = s.sb("over_expert", [P, NOV])
        over_expert_i = s.sb("over_expert_i", [P, NOV], I32)
        over_count_i = s.sb("over_count_i", [P, 1], I32)
        equal = s.sb("equal", [P, 2 * TT, P])
        diag = equal[:, :, :]
        sel = [s.sb(f"sel{i}", [P, TT, P], F32R) for i in range(2)]
        selT = [s.sb(f"selT{i}", [P, SEQ], F32R) for i in range(2)]
        in_block = s.sb("in_block", [P, 2, 2, TT])
        token_w = [s.sb(f"token_w{i}", [P, TT]) for i in range(2)]
        slot_w = [s.sb(f"slot_w{i}", [P, 1]) for i in range(2)]
        xeT = [s.sb(f"xeT{i}", [P, KT, P]) for i in range(2)]
        silu_gate = s.sb("silu_gate", [P, FF])
        hid = s.sb("hid", [P, FF])
        hidT = s.sb("hidT", [P, 4, P])
        y = s.sb("y", [P, DM])
        y_high = [s.sb(f"y_high{i}", [P, DM], F32R) for i in range(2)]
        y_low = [s.sb(f"y_low{i}", [P, DM], F32R) for i in range(2)]

        w_loaded = [s.sem(f"w13_loaded{i}") for i in range(2)]
        w2_loaded = [s.sem(f"w2_loaded{i}") for i in range(2)]
        small_loaded, own_v = s.sem("small_loaded"), s.sem("own_v")
        logits_done, exp_in, exp_out = s.sem("logits_done"), s.sem("exp_in"), s.sem("exp_out")
        member_ready, places_done, diag_ready, rows_done = s.sem("member_ready"), s.sem("places_done"), s.sem("diag_ready"), s.sem("rows_done")
        row_ready = s.sem("row_ready")
        sel_ready, gathered, xe_ready = s.sem("sel_ready"), s.sem("gathered"), s.sem("xe_ready")
        up_done, silu_done, hid_ready, hid_turned, hidT_ready = s.sem("up_done"), s.sem("silu_done"), s.sem("hid_ready"), s.sem("hid_turned"), s.sem("hidT_ready")
        down_done, y_ready, sel_turned, selT_ready = s.sem("down_done"), s.sem("y_ready"), s.sem("sel_turned"), s.sem("selT_ready")
        scattered, x_added = s.sem("scattered"), s.sem("x_added")
        sel_steps, slots_moved = s.sem("sel_steps"), s.sem("slots_moved")
        slot_w_done, slot_w_ready = s.sem("slot_w_done"), s.sem("slot_w_ready")
        xn_high_ready, xn_low_ready = s.sem("xn_high_ready"), s.sem("xn_low_ready")
        y_raw_ready, y_high_ready = s.sem("y_raw_ready"), s.sem("y_high_ready")
        block = s.block()

        def gather(pe, i, slot):
            for k in range(4 * i, 4 * i + 4):
                for t in range(TT):
                    for source in (xn_high, xn_low):
                        last = pe.matmul(gather_ps[i][:, (k % 4) * P:(k % 4 + 1) * P], source[:, t, k * P:(k + 1) * P],
                                         sel[slot][:, t, :], start=(t == 0 and source is xn_high),
                                         stop=(t == TT - 1 and source is xn_low))
            last.then_inc(gathered, 1)

        def weigh_slots(pe, slot):
            for t in range(TT):
                last = pe.matmul(gather_ps[0][:, 0:1], sel[slot][:, t, :].bitcast(FP32), token_w[slot][:, t:t + 1],
                                 start=(t == 0), stop=(t == TT - 1))
            last.then_inc(slot_w_done, 1)

        def gate_up(pe, m, slot):
            for k in range(KT):
                last = pe.matmul(up_ps[m][:, :], xeT[slot][:, k, :], w13[slot][:, m, k, :], start=(k == 0), stop=(k == KT - 1))
            last.then_inc(up_done, 1)

        def turn(pe, bank, src, done):
            for t in range(TT):
                last = pe.transpose(bank[:, t * P:(t + 1) * P], src[:, t * P:(t + 1) * P], chip.ident[:, :])
            last.then_inc(done, 1)

        def down(pe, half, slot):
            bank, w = turn_ps[1 + half], w2[slot]
            for f in range(4):
                last = pe.matmul(bank[:, :], hidT[:, f, :], w[:, f, half * 512:(half + 1) * 512], start=(f == 0), stop=(f == 3))
            last.then_inc(down_done, 1)

        def scatter(pe, o, bank, slot):
            t, half = o // 2, o % 2
            tokens, cols = slice(t * P, (t + 1) * P), slice(half * 512, (half + 1) * 512)
            pe.matmul(bank[:, :], selT[slot][:, tokens], y_high[slot][:, cols], start=True, stop=False)
            pe.matmul(bank[:, :], selT[slot][:, tokens], y_low[slot][:, cols], start=False, stop=True).then_inc(scattered, 1)

        def take_gathered(act, i, slot, b):
            act.wait_ge(gathered, 2 * b + i + 1)
            for k in range(4 * i, 4 * i + 4):
                ins = act.activation(xeT[slot][:, k, :], gather_ps[k // 4][:, (k % 4) * P:(k % 4 + 1) * P], ACT.Identity,
                                     scale=mod_gain[:, k:k + 1], bias=mod[:, 0, k:k + 1])
                if k % 4 == 3:
                    ins.then_inc(xe_ready, 1)

        def take_slot_w(act, slot, b):
            act.wait_ge(slot_w_done, b + 1)
            act.activation(slot_w[slot][:, :], gather_ps[0][:, 0:1], ACT.Copy).then_inc(slot_w_ready, 1)

        def weighted_y(dve, half, slot):
            cols = slice(half * 512, (half + 1) * 512)
            dve.scalar_tensor_tensor(out=y[:, cols], in0=turn_ps[1 + half][:, :], scalar=slot_w[slot][:, 0:1],
                                     in1=gate_row[:, cols], op0=ALU.mult, op1=ALU.mult).then_inc(y_raw_ready, 1)

        def split_y_high(act, half, slot):
            cols = slice(half * 512, (half + 1) * 512)
            act.activation(y_high[slot][:, cols], y[:, cols], ACT.Copy).then_inc(y_high_ready, 1)

        def split_y_low(dve, half, slot):
            cols = slice(half * 512, (half + 1) * 512)
            dve.tensor_tensor(y_low[slot][:, cols], y[:, cols], y_high[slot][:, cols].bitcast(FP32), ALU.subtract)\
                .then_inc(y_ready, 1)

        def select(dve, slot, steps, ready, n, r):
            dve.tensor_tensor(equal[:, :, :], slot_no.unsqueeze(1).broadcast_to([P, 2 * TT, P]),
                              slot_of[:, :, :].rearrange("p a t -> p (a t)").unsqueeze(2).broadcast_to([P, 2 * TT, P]),
                              ALU.is_equal).then_inc(steps, 1)
            dve.scalar_tensor_tensor(out=in_block[:, 0, :, :], in0=slot_of[:, :, :], scalar=0.0, in1=weight[:, :, :],
                                     op0=ALU.is_ge, op1=ALU.mult).then_inc(steps, 1)
            dve.wait_ge(steps, n + 2)
            dve.scalar_tensor_tensor(out=in_block[:, 1, :, :], in0=slot_of[:, :, :], scalar=float(P), in1=in_block[:, 0, :, :],
                                     op0=ALU.is_lt, op1=ALU.mult).then_inc(steps, 1)
            dve.tensor_tensor(sel[slot][:, :, :], equal[:, 0:TT, :], equal[:, TT:2 * TT, :], ALU.add).then_inc(ready, 1)
            dve.wait_ge(steps, n + 3)
            dve.tensor_tensor(token_w[slot][:, :], in_block[:, 1, 0, :], in_block[:, 1, 1, :], ALU.add).then_inc(ready, 1)
            dve.wait_ge(ready, r + 2)

        def add_to_x(dve, o, bank):
            t, half = o // 2, o % 2
            xs = chip.x[:, t, half * 512:(half + 1) * 512]
            dve.tensor_tensor(xs, bank[:, :], xs, ALU.add).then_inc(x_added, 1)

        @block.sync
        def _(sp):
            sp.dma_start(w_router[:, :, :], dram["moe_router"][layer]).then_inc(small_loaded, 16)
            sp.dma_start(const[:, :], dram["moe_const"]).then_inc(small_loaded, 16)

            def load(b, slot, again):
                if again:
                    sp.wait_ge(up_done, 2 * (b - 1))
                sp.dma_start(w13[slot][:, :, :, :], dram["moe_w13"][NE * layer + b]).then_inc(w_loaded[slot], 16)
                if again:
                    sp.wait_ge(down_done, 2 * (b - 1))
                sp.dma_start(w2[slot][:, :, :], dram["moe_w2"][NE * layer + b]).then_inc(w2_loaded[slot], 16)

            load(0, 0, False)
            load(1, 1, False)
            with sp.Fori(1, NE // 2) as i:
                load(2 * i, 0, True)
                load(2 * i + 1, 1, True)

        @block.tensor
        def _(pe):
            norm.tensor(pe)
            norm.complete(pe)
            pe.wait_ge(small_loaded, 32)
            for t in range(TT):
                for k in range(KT):
                    last = pe.matmul(ps[4][:, 20 * t:20 * t + 20], norm.hT[:, k, t * P:(t + 1) * P], w_router[:, k, :],
                                     start=(k == 0), stop=(k == KT - 1))
            last.then_inc(logits_done, 1)
            pe.wait_ge(diag_ready, 1)
            for k in range(KT):
                last = pe.matmul(ps[6 + k // 4][:, (k % 4) * P:(k % 4 + 1) * P], chip.ones[:, :], diag[:, k, :],
                                 start=True, stop=True)
            last.then_inc(rows_done, 1)
            pe.wait_ge(member_ready, 1)
            for t in range(TT):
                for u in range(t + 1):
                    pe.matmul(ps[5][:, NE * t:NE * t + NE], earlier if u == t else chip.ones[:, :], member[:, u, :],
                              start=(u == 0), stop=(u == t))
            for u in range(TT):
                last = pe.matmul(ps[5][:, NE * TT:NE * TT + NE], chip.ones[:, :], member[:, u, :], start=(u == 0), stop=(u == 3))
            last.then_inc(places_done, 1)
            pe.wait_ge(row_ready, 2)
            pe.wait_ge(xn_low_ready, TT)

            def iteration(b, slot, n, peeled=None):
                pe.wait_ge(w_loaded[slot], 16 * (n + 1))
                pe.wait_ge(xe_ready, 2 * (b + 1))
                if peeled != 0:
                    pe.wait_ge(hid_ready, b)
                gate_up(pe, 0, slot)
                if peeled != NE - 1:
                    pe.wait_ge(sel_ready, 2 * (b + 2))
                    weigh_slots(pe, 1 - slot)
                if peeled != 0:
                    pe.wait_ge(y_ready, 2 * b)
                    pe.wait_ge(selT_ready, b)
                    scatter_half(b, 0, 1 - slot)
                gate_up(pe, 1, slot)
                if peeled != 0:
                    scatter_half(b, 1, 1 - slot)
                if peeled != NE - 1:
                    pe.wait_ge(slot_w_ready, b + 2)
                    gather(pe, 0, 1 - slot)
                pe.wait_ge(hid_ready, b + 1)
                if peeled != 0:
                    pe.wait_ge(x_added, 8 * b)
                turn(pe, turn_ps[0], hid, hid_turned)
                if peeled != NE - 1:
                    gather(pe, 1, 1 - slot)
                turn(pe, turn_ps[3], sel[slot][:, :, :].rearrange("p t s -> p (t s)").bitcast(FP32), sel_turned)
                pe.wait_ge(hidT_ready, b + 1)
                pe.wait_ge(w2_loaded[slot], 16 * (n + 1))
                for half in range(2):
                    down(pe, half, slot)

            def scatter_half(b, half, slot):
                for o in range(4 * half, 4 * half + 4):
                    if half == 1:
                        pe.wait_ge(x_added, 8 * (b - 1) + o - 3)
                    scatter(pe, o, turn_ps[(o + 1) % 4], slot)

            pe.wait_ge(sel_ready, 2)
            weigh_slots(pe, 0)
            pe.wait_ge(slot_w_ready, 1)
            gather(pe, 0, 0)
            gather(pe, 1, 0)
            iteration(0, 0, 0, peeled=0)
            iteration(1, 1, 0, peeled=1)
            with pe.Fori(1, NE // 2 - 1) as i:
                iteration(2 * i, 0, i)
                iteration(2 * i + 1, 1, i)
            iteration(NE - 2, 0, NE // 2 - 1)
            iteration(NE - 1, 1, NE // 2 - 1, peeled=NE - 1)
            pe.wait_ge(y_ready, 2 * NE)
            pe.wait_ge(selT_ready, NE)
            scatter_half(NE, 0, 1)
            scatter_half(NE, 1, 1)

        @block.scalar
        def _(act):
            norm.scalar_stats(act)
            norm.scalar_evacuate(act, mod_gain, mod[:, 0, :])
            act.wait_ge(logits_done, 1)
            for t in range(TT):
                act.activation(xn_high[:, t, :], norm.xn[:, t, :], ACT.Copy).then_inc(xn_high_ready, 1)
            act.wait_ge(exp_in, 1)
            act.activation(group_exp[:, :, :], group_exp[:, :, :], ACT.Exp).then_inc(exp_out, 1)
            act.wait_ge(exp_in, 2)
            act.activation(tiny[:, 1, :], tiny[:, 0, :], ACT.Exp).then_inc(exp_out, 1)
            act.wait_ge(rows_done, 1)
            for half in range(2):
                act.activation(gate_row[:, half * 512:(half + 1) * 512], ps[6 + half][:, :], ACT.Copy).then_inc(row_ready, 1)

            def iteration(b, slot, peeled=None):
                act.wait_ge(up_done, 2 * b + 1)
                if peeled != 0:
                    act.wait_ge(hid_ready, b)
                act.activation(silu_gate[:, :], up_ps[0][:, :], ACT.Silu).then_inc(silu_done, 1)
                if peeled != NE - 1:
                    take_slot_w(act, 1 - slot, b + 1)
                    take_gathered(act, 0, 1 - slot, b + 1)
                act.wait_ge(hid_turned, b + 1)
                if peeled != 0:
                    act.wait_ge(down_done, 2 * b)
                act.activation(hidT[:, :, :].rearrange("p f s -> p (f s)"), turn_ps[0][:, :], ACT.Copy).then_inc(hidT_ready, 1)
                if peeled != NE - 1:
                    take_gathered(act, 1, 1 - slot, b + 1)
                act.wait_ge(sel_turned, b + 1)
                if peeled not in (0, 1):
                    act.wait_ge(scattered, 8 * (b - 1))
                act.activation(selT[slot][:, :], turn_ps[3][:, :], ACT.Copy).then_inc(selT_ready, 1)
                for half in range(2):
                    act.wait_ge(y_raw_ready, 2 * b + half + 1)
                    split_y_high(act, half, slot)

            take_slot_w(act, 0, 0)
            take_gathered(act, 0, 0, 0)
            take_gathered(act, 1, 0, 0)
            iteration(0, 0, peeled=0)
            iteration(1, 1, peeled=1)
            with act.Fori(1, NE // 2 - 1) as i:
                iteration(2 * i, 0)
                iteration(2 * i + 1, 1)
            iteration(NE - 2, 0)
            iteration(NE - 1, 1, peeled=NE - 1)

        @block.gpsimd
        def _(pool):
            for t in range(TT):
                pool.wait_ge(xn_high_ready, t + 1)
                pool.tensor_tensor(xn_low[:, t, :], norm.xn[:, t, :], xn_high[:, t, :].bitcast(FP32), ALU.subtract)\
                    .then_inc(xn_low_ready, 1)

        @block.vector
        def _(dve):
            own = Own(dve, own_v)
            norm.vector(dve)
            norm.vector_evacuate(dve, mod_gain, mod[:, 0, :])
            own(dve.memset(group8[:, :, :], MASKED))
            dve.wait_ge(logits_done, 1)
            own(dve.tensor_copy(logits[:, :, :].rearrange("p t c -> p (t c)"), ps[4][:, 0:TT * (NEG + NE)]))
            dve.tensor_tensor(diag, chip.ident[:, :].unsqueeze(1).broadcast_to([P, KT, P]),
                              mod[:, 2, :].unsqueeze(2).broadcast_to([P, KT, P]), ALU.mult).then_inc(diag_ready, 1)
            dve.wait_ge(small_loaded, 32)
            own(dve.tensor_copy(group8[:, :, 0:NEG], logits[:, :, 0:NEG]))
            for t in range(TT):
                own(dve.max(top[:, 0, t, :], group8[:, t, :]))
                own(dve.max_index(top_at[:, 0, t, :], top[:, 0, t, :], group8[:, t, :]))
            own(dve.tensor_copy(top_f[:, 0, :, :], top_at[:, 0, :, 0:2]))
            dve.tensor_tensor(group_exp[:, :, :], logits[:, :, 0:NEG], top[:, 0, :, 0:1].broadcast_to([P, TT, NEG]),
                              ALU.subtract).then_inc(exp_in, 1)
            own(dve.tensor_tensor(pick[:, :, :], expert_no[:, 0:NEG].unsqueeze(1).broadcast_to([P, TT, NEG]),
                                  top_f[:, 0, :, 0:1].broadcast_to([P, TT, NEG]), ALU.is_equal))
            own(dve.tensor_scalar(pick[:, :, :], pick[:, :, :], -MASKED, MASKED, ALU.mult, ALU.add))
            for t in range(TT):
                own(dve.tensor_tensor(score[:, t, :].rearrange("p (g e) -> p g e", g=NEG),
                                      logits[:, t, NEG:NEG + NE].rearrange("p (g e) -> p g e", g=NEG),
                                      pick[:, t, :].unsqueeze(2).broadcast_to([P, NEG, 4]), ALU.add))
                own(dve.max(top[:, 1, t, :], score[:, t, :]))
                own(dve.max_index(top_at[:, 1, t, :], top[:, 1, t, :], score[:, t, :]))
            dve.tensor_tensor(tiny[:, 0, :], top[:, 1, :, 1], top[:, 1, :, 0], ALU.subtract).then_inc(exp_in, 1)
            own(dve.tensor_copy(top_f[:, 1, :, :], top_at[:, 1, :, 0:2]))
            for a in range(2):
                own(dve.tensor_tensor(hot[:, a, :, :], expert_no.unsqueeze(1).broadcast_to([P, TT, NE]),
                                      top_f[:, 1, :, a:a + 1].broadcast_to([P, TT, NE]), ALU.is_equal))
            dve.tensor_tensor(member[:, :, :], hot[:, 0, :, :], hot[:, 1, :, :], ALU.add).then_inc(member_ready, 1)
            dve.wait_ge(exp_out, 2)
            own(dve.reduce_sum(tiny[:, 2, :], group_exp[:, :, :], AXX))
            own(dve.tensor_scalar(tiny[:, 3, :], tiny[:, 1, :], 1.0, None, ALU.add))
            own(dve.tensor_tensor(tiny[:, 4, :], tiny[:, 3, :], tiny[:, 2, :], ALU.mult))
            own(dve.reciprocal(weight[:, 0, :], tiny[:, 4, :]))
            own(dve.tensor_tensor(weight[:, 1, :], weight[:, 0, :], tiny[:, 1, :], ALU.mult))
            dve.wait_ge(places_done, 1)
            count = over[:, 0, :]
            own(dve.tensor_copy(place[:, :, :].rearrange("p t e -> p (t e)"), ps[5][:, 0:TT * NE]))
            own(dve.tensor_copy(count, ps[5][:, TT * NE:(TT + 1) * NE]))
            own(dve.tensor_scalar(over[:, 1, :], count, float(P), None, ALU.is_gt))
            for i in range(2, 4):
                own(dve.scalar_tensor_tensor(out=over[:, i, :], in0=count, scalar=float(i * P), in1=over[:, i - 1, :],
                                             op0=ALU.is_gt, op1=ALU.add))
            ends = over[:, 4, :]
            own(dve.tensor_tensor_scan(ends, chip.ones[:, 0:NE], over[:, 3, :], 0.0, ALU.mult, ALU.add))
            own(dve.tensor_tensor(over[:, 5, :], ends, over[:, 3, :], ALU.subtract))
            own(dve.tensor_scalar(over[:, 6, :], over[:, 5, :], float(P), float((NE - 1) * P), ALU.mult, ALU.add))
            own(dve.tensor_tensor(over[:, 7, :], over[:, 6, :], first_slot, ALU.subtract))
            slots = route[:, 0, :, :]
            own(dve.tensor_scalar(slots, place[:, :, :], float(P), None, ALU.is_ge))
            own(dve.tensor_tensor(slots, slots, over[:, 7, :].unsqueeze(1).broadcast_to([P, TT, NE]), ALU.mult))
            own(dve.tensor_tensor(slots, slots, first_slot.unsqueeze(1).broadcast_to([P, TT, NE]), ALU.add))
            own(dve.tensor_tensor(place[:, :, :], place[:, :, :], slots, ALU.add))
            for a in range(2):
                own(dve.tensor_tensor(route[:, a, :, :], hot[:, a, :, :], place[:, :, :], ALU.mult))
                own(dve.reduce_sum(slot_of[:, a, :], route[:, a, :, :], AXX))
            own(dve.tensor_tensor(over_cmp[:, :, :], ends.unsqueeze(1).broadcast_to([P, NOV, NE]),
                                  block_no.unsqueeze(2).broadcast_to([P, NOV, NE]), ALU.is_le))
            own(dve.reduce_sum(over_expert[:, :], over_cmp[:, :, :], AXX))
            own(dve.tensor_scalar(over_expert[:, :], over_expert[:, :], float(NE - 1), float(NE * layer), ALU.min, ALU.add))
            own(dve.tensor_copy(over_expert_i[:, :], over_expert[:, :]))
            own(dve.tensor_copy(over_count_i[:, :], ends[:, NE - 1:NE]))

            def next_block(slot, n):
                select(dve, slot, sel_steps, sel_ready, 3 * n, 2 * n)
                dve.tensor_scalar(slot_of[:, :, :], slot_of[:, :, :], -float(P), None, ALU.add).then_inc(slots_moved, 1)
                dve.wait_ge(slots_moved, n + 1)

            def add_half(b, half, peeled=None):
                for o in range(4 * half, 4 * half + 4):
                    dve.wait_ge(scattered, 8 * (b - 1) + o + 1)
                    if peeled != 1:
                        dve.wait_ge(x_added, 8 * (b - 2) + o + 1)
                    add_to_x(dve, o, turn_ps[(o + 1) % 4])

            def iteration(b, slot, peeled=None):
                if peeled != 0:
                    add_half(b, 0, peeled)
                dve.wait_ge(silu_done, b + 1)
                dve.wait_ge(up_done, 2 * b + 2)
                if peeled != 0:
                    dve.wait_ge(hid_turned, b)
                dve.tensor_tensor(hid[:, :], silu_gate[:, :], up_ps[1][:, :], ALU.mult).then_inc(hid_ready, 1)
                if peeled != 0:
                    add_half(b, 1, peeled)
                if peeled not in (NE - 2, NE - 1):
                    dve.wait_ge(sel_turned, b + 1)
                    next_block(slot, b + 2)
                dve.wait_ge(slot_w_ready, b + 1)
                if peeled != 0:
                    dve.wait_ge(y_ready, 2 * b)
                for half in range(2):
                    dve.wait_ge(down_done, 2 * b + half + 1)
                    weighted_y(dve, half, slot)
                for half in range(2):
                    dve.wait_ge(y_high_ready, 2 * b + half + 1)
                    split_y_low(dve, half, slot)

            next_block(0, 0)
            next_block(1, 1)
            dve.wait_ge(row_ready, 2)
            iteration(0, 0, peeled=0)
            iteration(1, 1, peeled=1)
            with dve.Fori(1, NE // 2 - 1) as i:
                iteration(2 * i, 0)
                iteration(2 * i + 1, 1)
            iteration(NE - 2, 0, peeled=NE - 2)
            iteration(NE - 1, 1, peeled=NE - 1)
            add_half(NE, 0)
            add_half(NE, 1)

        up_done, down_done, hid_turned, gathered, xe_ready, sel_turned, scattered, x_added = [
            s.sem("over_" + what) for what in ("up_done", "down_done", "hid_turned", "gathered", "xe_ready", "sel_turned",
                                               "scattered", "x_added")]
        slot_w_done, slot_w_ready, y_raw_ready, y_high_ready, sel_ready = [
            s.sem("over_" + what) for what in ("slot_w_done", "slot_w_ready", "y_raw_ready", "y_high_ready", "sel_ready")]
        silu_done, hid_ready, hidT_ready, y_ready, selT_ready, sel_steps, w_arrived, block_gone = [
            s.sem("over_" + what) for what in ("silu_done", "hid_ready", "hidT_ready", "y_ready", "selT_ready", "sel_steps",
                                               "w_arrived", "block_gone")]
        block = s.block("overflow")

        def if_overflow(eng):
            count = eng.value_load(over_count_i[0:1, 0:1], min_val=0, max_val=NOV)
            return eng.If(count > 0)

        @block.sync
        def _(sp):
            with if_overflow(sp):
                with sp.Fori(0, NOV) as j:
                    sp.wait_ge(block_gone, j + 1)
                    e = sp.value_load(over_expert_i[0:1, bass.ds(j, 1)], min_val=0, max_val=2 * NE - 1)
                    sp.dma_start(w13[0][:, :, :, :], dram["moe_w13"][bass.ds(e, 1)][0]).then_inc(w_arrived, 16)
                    sp.dma_start(w2[0][:, :, :], dram["moe_w2"][bass.ds(e, 1)][0]).then_inc(w_arrived, 16)

        @block.tensor
        def _(pe):
            with if_overflow(pe):
                with pe.Fori(0, NOV) as j:
                    pe.wait_ge(sel_ready, 2 * j + 2)
                    weigh_slots(pe, 0)
                    pe.wait_ge(slot_w_ready, j + 1)
                    gather(pe, 0, 0)
                    gather(pe, 1, 0)
                    pe.wait_ge(w_arrived, 32 * (j + 1))
                    pe.wait_ge(xe_ready, 2 * (j + 1))
                    gate_up(pe, 0, 0)
                    gate_up(pe, 1, 0)
                    turn(pe, turn_ps[3], sel[0][:, :, :].rearrange("p t s -> p (t s)").bitcast(FP32), sel_turned)
                    pe.wait_ge(hid_ready, j + 1)
                    turn(pe, turn_ps[0], hid, hid_turned)
                    pe.wait_ge(hidT_ready, j + 1)
                    down(pe, 0, 0)
                    down(pe, 1, 0)
                    pe.wait_ge(y_ready, 2 * (j + 1))
                    pe.wait_ge(selT_ready, j + 1)
                    for o in range(8):
                        if o >= 4:
                            pe.wait_ge(x_added, 8 * j + o - 3)
                        scatter(pe, o, turn_ps[(o + 1) % 4], 0)

        @block.scalar
        def _(act):
            with if_overflow(act):
                with act.Fori(0, NOV) as j:
                    take_slot_w(act, 0, j)
                    take_gathered(act, 0, 0, j)
                    take_gathered(act, 1, 0, j)
                    act.wait_ge(up_done, 2 * j + 1)
                    act.activation(silu_gate[:, :], up_ps[0][:, :], ACT.Silu).then_inc(silu_done, 1)
                    act.wait_ge(sel_turned, j + 1)
                    act.activation(selT[0][:, :], turn_ps[3][:, :], ACT.Copy).then_inc(selT_ready, 1)
                    act.wait_ge(hid_turned, j + 1)
                    act.activation(hidT[:, :, :].rearrange("p f s -> p (f s)"), turn_ps[0][:, :], ACT.Copy).then_inc(hidT_ready, 1)
                    for half in range(2):
                        act.wait_ge(y_raw_ready, 2 * j + half + 1)
                        split_y_high(act, half, 0)

        @block.vector
        def _(dve):
            with if_overflow(dve):
                dve.sem_inc(block_gone, 1)
                with dve.Fori(0, NOV) as j:
                    select(dve, 0, sel_steps, sel_ready, 3 * j, 2 * j)
                    dve.wait_ge(silu_done, j + 1)
                    dve.wait_ge(up_done, 2 * j + 2)
                    dve.tensor_tensor(hid[:, :], silu_gate[:, :], up_ps[1][:, :], ALU.mult).then_inc(hid_ready, 1)
                    for half in range(2):
                        dve.wait_ge(down_done, 2 * j + half + 1)
                        weighted_y(dve, half, 0)
                    for half in range(2):
                        dve.wait_ge(y_high_ready, 2 * j + half + 1)
                        split_y_low(dve, half, 0)
                    for o in range(8):
                        dve.wait_ge(scattered, 8 * j + o + 1)
                        add_to_x(dve, o, turn_ps[(o + 1) % 4])
                    dve.wait_ge(x_added, 8 * j + 8)
                    dve.tensor_scalar(slot_of[:, :, :], slot_of[:, :, :], -float(P), None, ALU.add).then_inc(block_gone, 1)
                    dve.wait_ge(block_gone, j + 2)


def final_norm(chip):
    with Scope(chip.nc, "final_norm") as s:
        row = s.sb("row", [P, DM])
        scratch = s.sb("scratch", [P, TT, DM])
        stat = s.sb("stat", [P, 4, TT])
        row_loaded, squared, var_ready, rstd_ready = s.sem("row_loaded"), s.sem("squared"), s.sem("var_ready"), s.sem("rstd_ready")
        block = s.block()

        @block.sync
        def _(sp):
            sp.dma_start(row[:, :], chip.dram["final_row"]).then_inc(row_loaded, 16)

        @block.scalar
        def _(act):
            for t in range(TT):
                act.activation(scratch[:, t, :], chip.x[:, t, :], ACT.Square, accum_out=stat[:, 0, t:t + 1])\
                    .then_inc(squared, 1)
            act.wait_ge(var_ready, 2)
            act.activation(stat[:, 3, :], stat[:, 2, :], ACT.Sqrt).then_inc(rstd_ready, 1)

        @block.vector
        def _(dve):
            dve.wait_ge(squared, TT)
            dve.tensor_scalar(stat[:, 1, :], stat[:, 0, :], 1.0 / DM, EPS, ALU.mult, ALU.add).then_inc(var_ready, 1)
            dve.wait_ge(var_ready, 1)
            dve.reciprocal(stat[:, 2, :], stat[:, 1, :]).then_inc(var_ready, 1)
            dve.wait_ge(row_loaded, 16)
            dve.wait_ge(rstd_ready, 1)
            for t in range(TT):
                dve.scalar_tensor_tensor(out=chip.x[:, t, :], in0=chip.x[:, t, :], scalar=stat[:, 3, t:t + 1],
                                         in1=row[:, :], op0=ALU.mult, op1=ALU.mult)


def store(chip, out):
    with Scope(chip.nc, "store") as s:
        stored = chip.stored
        block = s.block()

        @block.sync
        def _(sp):
            sp.dma_start(out[0].rearrange("(t p) d -> p t d", p=P), chip.x[:, :, :]).then_inc(stored, 16)
            sp.wait_ge(stored, 16)


def program(nc, dram, out):
    with ExitStack() as ctx:
        chip = Chip(nc, ctx, dram)
        start(chip)
        for l in range(2):
            ffn(chip, f"ffn1_{l}", l, chip.gain("ffn1_norm", l))
            mixer(chip, f"mixer_{l}", l, 0.8 - 0.6 * math.exp(-0.3 * l))
            ffn(chip, f"ffn2_{l}", 2 + l, chip.gain("ffn2_norm", l))
        final_norm(chip)
        nsa(chip)
        moe(chip, "moe_0", 0)
        hgrn(chip)
        moe(chip, "moe_1", 1)
        store(chip, out)



def constants():
    import numpy as np
    t = np.arange(SEQ)
    near = np.zeros((4, SEQ, SEQ))
    for g, w in enumerate((2, 4, 8, 16)):
        lo, hi = np.maximum(t - w // 2, 0), np.minimum(t + w - w // 2, SEQ)
        inside = (t[:, None] >= lo[None, :]) & (t[:, None] < hi[None, :])
        near[g] = inside / (hi - lo)[None, :] - np.eye(SEQ)
    near = near.reshape(2, 2, TT, P, SEQ).transpose(0, 3, 1, 2, 4).reshape(2, P, 4096)
    turn = 2 * np.pi * (np.outer(t, t) % SEQ) / SEQ
    dft = np.stack([np.cos(turn), np.sin(turn)]) / math.sqrt(SEQ)
    dft = dft.reshape(2, TT, P, SEQ).transpose(2, 0, 1, 3).reshape(1, P, 4096)
    c = np.arange(64)
    turn = 2 * np.pi * (np.outer(c, c) % 64) / 64
    chan = np.zeros((P, 2, P))
    for i in range(2):
        chan[64 * i:64 * i + 64, 0, 64 * i:64 * i + 64] = np.cos(turn) / 8
        chan[64 * i:64 * i + 64, 1, 64 * i:64 * i + 64] = -np.sin(turn) / 8
    gap = np.abs(np.arange(P)[:, None] + 384 - np.arange(STRIP)[None, :])
    slopes = 2.0 ** (-8.0 * (np.arange(HEADS) + 1) / HEADS)
    alibi = -slopes[None, :, None] * gap[:, None, :]
    at = np.arange(P)
    masks = np.zeros((P, len(LEVELS), P), np.int32)
    masks[:, 0] = np.eye(P)
    for l, b in enumerate(LEVELS[1:]):
        same = at[:, None] // (2 * b) == at[None, :] // (2 * b)
        masks[:, l + 1] = same & (at[:, None] // b % 2 == 0) & (at[None, :] // b % 2 == 1)
    keep = np.broadcast_to((np.arange(SEQ) % P != 0).astype(np.float32), (P, SEQ))
    moe = np.zeros((P, 512))
    moe[:, 0:P] = at[:, None] < at[None, :]
    moe[:, P:2 * P] = at
    moe[:, 256:272], moe[:, 272:288], moe[:, 288:288 + NOV] = P * np.arange(NE), np.arange(NE), np.arange(NOV)
    f = np.float32
    return {"moe_const": moe.astype(f), "hgrn_masks": masks, "hgrn_keep": keep, "nsa_buckets": distance_buckets(), "mix_const": np.concatenate([near, dft]).astype(f), "chan_dft": chan.astype(f), "alibi": alibi.astype(f)}


def distance_buckets():
    import numpy as np
    dist = 511 - np.arange(640)
    nf = np.maximum(dist, 1).astype(np.float32)
    large = 16 + (np.log(nf / np.float32(16)) / np.float32(math.log(64)) * np.float32(16)).astype(np.int32)
    bucket = np.where(dist < 16, dist, np.minimum(large, 31))
    bucket = np.where(dist < 0, 32, bucket)
    return (bucket[None, :] == np.arange(64)[:, None]).astype(np.float32)


def nsa_layouts(inp):
    import numpy as np
    w = inp["nsa_w_in_2"][0]
    heads = [8 * (m // 4) + 4 * half + m % 4 for m in range(KT) for half in range(2)]
    q = w[:, 0:1024].reshape(DM, NH, HD)[:, heads].reshape(DM, 1024)
    kc, vc, ks, vs, kw, vw = (w[:, 1024 + 256 * i:1280 + 256 * i] for i in range(6))
    groups = column_groups(np.concatenate([q, ks, kw, vs, vw, kc, vc], 1))
    gates = w[:, 2560:].reshape(KT, P, 3 * NH).transpose(1, 0, 2)
    small = np.concatenate([inp["nsa_cmp_pe_2"][0].transpose(2, 0, 1).reshape(64, 64),
                            inp["nsa_cmp_w2_2"][0].transpose(1, 0, 2).reshape(64, 128)], 1)
    return np.concatenate([groups, column_groups(inp["nsa_w_out_2"][0])]), gates, small


def column_groups(w):
    return w.reshape(KT, P, -1, 512).transpose(2, 1, 0, 3).reshape(-1, P, 4096)


def hidden_tiles(w_gate, w_up, w_down):
    import numpy as np
    n = len(w_gate)
    gu = np.stack([w_gate, w_up], 1).reshape(n, 2, KT, P, NFT, P).transpose(0, 4, 3, 1, 2, 5)
    return gu.reshape(n * NFT, P, 2, KT, P), w_down.reshape(n * NFT, P, DM)


def layouts(inp):
    import numpy as np
    d = {}
    d["x"] = inp["x"][0].reshape(TT, P, DM).transpose(1, 0, 2)
    cols = []
    for name, width in COLS:
        a = np.broadcast_to(inp[name], inp[name].shape).reshape(-1, width)
        if width >= P:
            a = a.reshape(-1, P)
        elif width == 64:
            a = np.concatenate([a, a], 1)
        cols.append(a.T)
    d["cols"] = np.concatenate(cols, 1)
    gs = [hidden_tiles(inp[f"ffn{i}_w_gate"], inp[f"ffn{i}_w_up"], inp[f"ffn{i}_w_down"]) for i in (1, 2)]
    d["ffn_gate_up"] = np.concatenate([g for g, _ in gs])
    d["ffn_down"] = np.concatenate([w for _, w in gs])
    d["mix_w"] = np.stack([np.concatenate([column_groups(inp["w_in"][l]), column_groups(inp["w_out"][l])]) for l in range(2)])
    small = np.zeros((2, P, 1024), np.float32)
    for g in range(4):
        half = 64 * (g % 2)
        small[:, half:half + 64, P * (g // 2) + half:P * (g // 2) + half + 64] = inp["pool_w"][:, g]
    small[:, :, 256:768] = inp["fourier_w"].reshape(2, 2, P, 256).transpose(0, 2, 1, 3).reshape(2, P, 512)
    for i, lam_name in enumerate(("lam_q1", "lam_k1", "lam_q2", "lam_k2")):
        small[:, :, 768 + 64 * i:832 + 64 * i] = inp[lam_name][:, None, :]
    d["mix_small"] = small
    d["ada_w"] = inp["ada_w_2"].reshape(4 * KT, P, 3 * DM)
    d["final_row"] = np.broadcast_to(inp["final_norm"], (P, DM))
    d["nsa_w"], d["nsa_w_gates"], d["nsa_small"] = nsa_layouts(inp)
    d["nsa_cmp_w1"] = np.zeros((P, 4096), np.float32)
    d["nsa_cmp_w1"][0:64] = inp["nsa_cmp_w1_2"][0].reshape(2, 32, 64, 64).transpose(2, 0, 1, 3).reshape(64, 4096)
    d["nsa_table"] = np.zeros((64, NH), np.float32)
    d["nsa_table"][0:32] = inp["rel_bias_2"]
    d["nsa_table"][32] = MASKED
    w = inp["hgrn_w_in_2"][0]
    fq = np.concatenate([w[:, c:c + P] for m in range(HG) for c in (1024 + P * m, P * m)], 1)
    d["hgrn_w"] = np.concatenate([column_groups(np.concatenate([fq, w[:, 2048:]], 1)),
                                  column_groups(inp["hgrn_w_out_2"][0])])
    router = np.concatenate([inp["moe_router_group_2"], inp["moe_router_expert_2"]], 2)
    d["moe_router"] = router.reshape(2, KT, P, NEG + NE).transpose(0, 2, 1, 3)
    w13 = np.stack([inp["moe_w1_2"], inp["moe_w3_2"]], 2).reshape(2 * NE, 2, KT, P, FF)
    d["moe_w13"] = w13.transpose(0, 3, 1, 2, 4)
    d["moe_w2"] = inp["moe_w2_2"].reshape(2 * NE, TT, P, DM).transpose(0, 2, 1, 3)
    d.update(constants())
    return d


def kernel(**inputs):
    import numpy as np
    import concourse.bacc as bacc
    from concourse.bass_utils import run_bass_kernel_spmd

    nc = bacc.Bacc("TRN2", target_bir_lowering=False, num_devices=1)
    arrays, dram = {}, {}
    for name, a in layouts({k: np.asarray(v) for k, v in inputs.items()}).items():
        a = np.ascontiguousarray(a)
        arrays[f"in_{name}"] = a
        dram[name] = nc.dram_tensor(f"in_{name}", a.shape, mybir.dt.from_np(a.dtype), kind="ExternalInput").ap()
    dram["bias_rows"] = nc.dram_tensor("bias_rows", (NH, 640), FP32, kind="Internal").ap()
    dram["bias_copies"] = nc.dram_tensor("bias_copies", (P, NH * 640), FP32, kind="Internal").ap()
    out = nc.dram_tensor("out_x", (1, SEQ, DM), FP32, kind="ExternalOutput").ap()
    program(nc, dram, out)
    r = run_bass_kernel_spmd(nc, [arrays], core_ids=[0])
    return r.results[0]["out_x"]
```
